# Optimizing a Trainium2 kernel written in Bass

```python
import math
import jax, jax.numpy as jnp
from jax import lax
import numpy as np
import jax
import jax.numpy as jnp

D_MODEL = 1024
BATCH = 1
SEQ = 256
DEPTH = 1

HEAD_DIM = 64
N_HEADS_DIL = 8
N_HEADS_MOBA = 8
N_HEADS_SELF = N_HEADS_DIL + N_HEADS_MOBA
DIL_WIDTH = N_HEADS_DIL * HEAD_DIM
MOBA_WIDTH = N_HEADS_MOBA * HEAD_DIM
MIX_WIDTH = DIL_WIDTH + MOBA_WIDTH
DILATION_PAIRS = ((128, 1), (512, 4), (2048, 16))
MOBA_BLOCK = 256
MOBA_TOPK = 3
MOBA_QCHUNK = 16
N_BUCKETS = 32
MAX_DISTANCE = 2048
N_MEM = 256
N_HEADS_MEM = 4
HEAD_DIM_MEM = D_MODEL // N_HEADS_MEM
D_FF = 2816
CONV_WIDTH = 3
EPS = 1e-6
NEG_INF = -1e30


def rmsnorm(x, g):
    xf = x.astype(jnp.float32)
    y = xf * lax.rsqrt(jnp.mean(xf * xf, axis=-1, keepdims=True) + EPS)
    return (y * g.astype(jnp.float32)).astype(x.dtype)

def rel_bucket(dist):
    max_exact = N_BUCKETS // 2
    n = jnp.maximum(dist, 0)
    nf = jnp.maximum(n, 1).astype(jnp.float32)
    large = max_exact + (jnp.log(nf / max_exact) / math.log(MAX_DISTANCE / max_exact)
                         * (N_BUCKETS - max_exact)).astype(jnp.int32)
    large = jnp.minimum(large, N_BUCKETS - 1)
    return jnp.where(n < max_exact, n, large)

def dilated_attention(q, k, v, bias_table):
    B, H, S, hd = q.shape
    scale = hd ** -0.5
    outs, lses = [], []
    for window, dil in DILATION_PAIRS:
        w_sub = window // dil
        L = S // dil
        nblk = -(-L // w_sub)
        Lp = nblk * w_sub

        def to_sub(t):
            t = t.reshape(B, H, L, dil, hd).transpose(0, 1, 3, 2, 4)
            t = jnp.pad(t, ((0, 0), (0, 0), (0, 0), (0, Lp - L), (0, 0)))
            return t.reshape(B, H, dil, nblk, w_sub, hd)

        def with_prev(t):
            prev = jnp.pad(t, ((0, 0), (0, 0), (0, 0), (1, 0), (0, 0), (0, 0)))[:, :, :, :-1]
            return jnp.concatenate([prev, t], axis=4)

        qs = to_sub(q)
        kb = with_prev(to_sub(k))
        vb = with_prev(to_sub(v))
        s = jnp.einsum('bhrnqd,bhrnkd->bhrnqk', qs, kb).astype(jnp.float32) * scale
        i = jnp.arange(w_sub)[:, None]
        j = jnp.arange(2 * w_sub)[None, :]
        diff = w_sub + i - j
        bias = bias_table[:, rel_bucket(diff * dil)].astype(jnp.float32)
        blk = jnp.arange(nblk)[:, None, None]
        valid = (diff >= 0) & (diff <= w_sub) & ((blk - 1) * w_sub + j >= 0)
        s = jnp.where(valid, s + bias[:, None, None], NEG_INF)
        m = jnp.max(s, axis=-1, keepdims=True)
        p = jnp.exp(s - m)
        den = jnp.sum(p, axis=-1, keepdims=True)
        o = jnp.einsum('bhrnqk,bhrnkd->bhrnqd', (p / den).astype(v.dtype), vb)
        lse = (m + jnp.log(den))[..., 0]
        o = o.reshape(B, H, dil, Lp, hd)[:, :, :, :L].transpose(0, 1, 3, 2, 4).reshape(B, H, S, hd)
        lse = lse.reshape(B, H, dil, Lp)[:, :, :, :L].transpose(0, 1, 3, 2).reshape(B, H, S)
        outs.append(o)
        lses.append(lse)
    wts = jax.nn.softmax(jnp.stack(lses), axis=0)
    out = jnp.einsum('pbhs,pbhsd->bhsd', wts, jnp.stack(outs).astype(jnp.float32))
    return out.astype(q.dtype)

def moba_attention(q, k, v, bias_table):
    B, H, S, hd = q.shape
    scale = hd ** -0.5
    nb = -(-S // MOBA_BLOCK)
    Sp = nb * MOBA_BLOCK
    pad = lambda t: jnp.pad(t, ((0, 0), (0, 0), (0, Sp - S), (0, 0)))
    qp, kp, vp = pad(q), pad(k), pad(v)
    kb = kp.reshape(B, H, nb, MOBA_BLOCK, hd)
    vb = vp.reshape(B, H, nb, MOBA_BLOCK, hd)
    k_mean = jnp.mean(kb.astype(jnp.float32), axis=3).astype(q.dtype)
    topk = min(MOBA_TOPK, nb)
    n_chunks = Sp // MOBA_QCHUNK
    qc = qp.reshape(B, H, n_chunks, MOBA_QCHUNK, hd).transpose(2, 0, 1, 3, 4)
    bi = jnp.arange(B)[:, None, None, None]
    hi = jnp.arange(H)[None, :, None, None]
    hi5 = jnp.arange(H)[None, :, None, None, None]
    bias_f = bias_table.astype(jnp.float32)

    def one_chunk(args):
        q_c, c = args
        t = c * MOBA_QCHUNK + jnp.arange(MOBA_QCHUNK)
        own = (c * MOBA_QCHUNK) // MOBA_BLOCK
        gate = jnp.einsum('bhqd,bhnd->bhqn', q_c, k_mean).astype(jnp.float32)
        gate = jnp.where(jnp.arange(nb) < own, gate, NEG_INF)
        _, idx = lax.top_k(gate, topk)
        sel_valid = jnp.arange(topk) < own
        k_sel = kb[bi, hi, idx]
        v_sel = vb[bi, hi, idx]
        s_sel = jnp.einsum('bhqd,bhqnkd->bhqnk', q_c, k_sel).astype(jnp.float32) * scale
        key_pos = idx[..., None] * MOBA_BLOCK + jnp.arange(MOBA_BLOCK)
        dist = t[:, None, None] - key_pos
        s_sel = jnp.where(sel_valid[:, None], s_sel + bias_f[hi5, rel_bucket(dist)], NEG_INF)
        k_own = lax.dynamic_slice_in_dim(kp, own * MOBA_BLOCK, MOBA_BLOCK, axis=2)
        v_own = lax.dynamic_slice_in_dim(vp, own * MOBA_BLOCK, MOBA_BLOCK, axis=2)
        s_own = jnp.einsum('bhqd,bhkd->bhqk', q_c, k_own).astype(jnp.float32) * scale
        dist_own = t[:, None] - (own * MOBA_BLOCK + jnp.arange(MOBA_BLOCK))[None, :]
        s_own = jnp.where(dist_own >= 0, s_own + bias_f[:, rel_bucket(dist_own)][None], NEG_INF)
        nsel = topk * MOBA_BLOCK
        s_all = jnp.concatenate([s_sel.reshape(B, H, MOBA_QCHUNK, nsel), s_own], axis=-1)
        p = jax.nn.softmax(s_all, axis=-1).astype(v.dtype)
        p_sel = p[..., :nsel].reshape(B, H, MOBA_QCHUNK, topk, MOBA_BLOCK)
        o = (jnp.einsum('bhqnk,bhqnkd->bhqd', p_sel, v_sel)
             + jnp.einsum('bhqk,bhkd->bhqd', p[..., nsel:], v_own))
        return o

    out = lax.map(one_chunk, (qc, jnp.arange(n_chunks)))
    return out.transpose(1, 2, 0, 3, 4).reshape(B, H, Sp, hd)[:, :, :S]

def memory_cross_attention(c, m, w_q, w_kv, w_o):
    B, S, D = c.shape
    qm = (c @ w_q).reshape(B, S, N_HEADS_MEM, HEAD_DIM_MEM)
    km, vm = jnp.split(m @ w_kv, 2, axis=-1)
    km = km.reshape(B, N_MEM, N_HEADS_MEM, HEAD_DIM_MEM)
    vm = vm.reshape(B, N_MEM, N_HEADS_MEM, HEAD_DIM_MEM)
    s = jnp.einsum('bqhd,bkhd->bhqk', qm, km).astype(jnp.float32) * (HEAD_DIM_MEM ** -0.5)
    p = jax.nn.softmax(s, axis=-1).astype(c.dtype)
    o = jnp.einsum('bhqk,bkhd->bqhd', p, vm).reshape(B, S, D)
    return o @ w_o

def conv_ffn(f, w_gate, w_up, conv_w, conv_b, w_down):
    S = f.shape[1]
    a = f @ w_gate
    ap = jnp.pad(a, ((0, 0), (CONV_WIDTH - 1, 0), (0, 0)))
    conv = conv_b
    for tap in range(CONV_WIDTH):
        conv = conv + ap[:, tap:tap + S] * conv_w[tap]
    return (jax.nn.silu(conv) * (f @ w_up)) @ w_down

def first_inputs(seed: int = 0) -> dict:
    key = jax.random.key(seed)
    ks = jax.random.split(key, 20)
    f32 = jnp.float32
    nrm = lambda k, shape, scale: jax.random.normal(k, shape, f32) * scale
    gain = lambda k, shape: 1.0 + 0.02 * jax.random.normal(k, shape, f32)
    return {
        "x": nrm(ks[0], (BATCH, SEQ, D_MODEL), 1.0),
        "mem": nrm(ks[1], (BATCH, N_MEM, D_MODEL), 1.0),
        "w_in": nrm(ks[2], (DEPTH, D_MODEL, 3 * MIX_WIDTH), D_MODEL ** -0.5),
        "g_mix": gain(ks[3], (DEPTH, D_MODEL)),
        "g_out_dil": gain(ks[4], (DEPTH, DIL_WIDTH)),
        "g_out_moba": gain(ks[5], (DEPTH, MOBA_WIDTH)),
        "w_out": nrm(ks[6], (DEPTH, MIX_WIDTH, D_MODEL), MIX_WIDTH ** -0.5),
        "rel_bias": nrm(ks[7], (N_HEADS_SELF, N_BUCKETS), 0.5),
        "g_cross": gain(ks[8], (DEPTH, D_MODEL)),
        "g_mem": gain(ks[9], (DEPTH, D_MODEL)),
        "w_q_mem": nrm(ks[10], (DEPTH, D_MODEL, D_MODEL), D_MODEL ** -0.5),
        "w_kv_mem": nrm(ks[11], (DEPTH, D_MODEL, 2 * D_MODEL), D_MODEL ** -0.5),
        "w_o_mem": nrm(ks[12], (DEPTH, D_MODEL, D_MODEL), D_MODEL ** -0.5),
        "g_ffn": gain(ks[13], (DEPTH, D_MODEL)),
        "w_gate": nrm(ks[14], (DEPTH, D_MODEL, D_FF), D_MODEL ** -0.5),
        "w_up": nrm(ks[15], (DEPTH, D_MODEL, D_FF), D_MODEL ** -0.5),
        "conv_w": nrm(ks[16], (DEPTH, CONV_WIDTH, D_FF), CONV_WIDTH ** -0.5),
        "conv_b": nrm(ks[17], (DEPTH, D_FF), 0.02),
        "w_down": nrm(ks[18], (DEPTH, D_FF, D_MODEL), D_FF ** -0.5),
        "g_final": gain(ks[19], (D_MODEL,)),
    }

def first_block(x, mem, w_in, g_mix, g_out_dil, g_out_moba, w_out, rel_bias, g_cross, g_mem,
              w_q_mem, w_kv_mem, w_o_mem, g_ffn, w_gate, w_up, conv_w, conv_b, w_down, g_final):
    B, S, _ = x.shape
    heads = lambda t, n: t.reshape(B, S, n, HEAD_DIM).transpose(0, 2, 1, 3)
    merge = lambda t, w: t.transpose(0, 2, 1, 3).reshape(B, S, w)
    h = x
    for l in range(DEPTH):
        u = rmsnorm(h, g_mix[l])
        qa, ka, va, qb, kb, vb = jnp.split(u @ w_in[l], 6, axis=-1)
        ya = dilated_attention(heads(qa, N_HEADS_DIL), heads(ka, N_HEADS_DIL),
                               heads(va, N_HEADS_DIL), rel_bias[:N_HEADS_DIL])
        yb = moba_attention(heads(qb, N_HEADS_MOBA), heads(kb, N_HEADS_MOBA),
                            heads(vb, N_HEADS_MOBA), rel_bias[N_HEADS_DIL:])
        y = jnp.concatenate([rmsnorm(merge(ya, DIL_WIDTH), g_out_dil[l]),
                             rmsnorm(merge(yb, MOBA_WIDTH), g_out_moba[l])], axis=-1)
        h = h + y @ w_out[l]
        h = h + memory_cross_attention(rmsnorm(h, g_cross[l]), rmsnorm(mem, g_mem[l]),
                                       w_q_mem[l], w_kv_mem[l], w_o_mem[l])
        h = h + conv_ffn(rmsnorm(h, g_ffn[l]), w_gate[l], w_up[l], conv_w[l], conv_b[l], w_down[l])
    return rmsnorm(h, g_final)


DEPTH_2 = 2

CTX_LEN = 256
GRID_W = 64
NA_WIDTH = D_MODEL // 2
NA_HEADS = NA_WIDTH // HEAD_DIM
NA_WIN_ROWS = 8
NA_WIN_COLS = 16
NA_QCB = 16
NA_KCB = 32
RW_WIDTH = D_MODEL // 4
RW_HEADS = RW_WIDTH // HEAD_DIM
RW_DECAY_RANK = 64
RW_A_RANK = 64
RW_GATE_RANK = 128
RW_LORA = RW_DECAY_RANK + RW_A_RANK + RW_GATE_RANK
RW_IN = 3 * RW_WIDTH + 2 * RW_LORA
RW_GN_EPS = 64e-5
CV_WIDTH = D_MODEL // 4
CV_CONV_LEN = 31
MIX_WIDTH_2 = NA_WIDTH + RW_WIDTH + CV_WIDTH
IN_WIDTH = 3 * NA_WIDTH + RW_IN + 2 * CV_WIDTH
N_EXPERTS = 8
TOP_K = 2
D_FF_EXPERT = 3584
MOE_BLOCK = 128
N_DENSE_LAYERS = (DEPTH_2 + 1) // 2
N_MOE_LAYERS = DEPTH_2 // 2
RMS_EPS = 1e-6
LN_EPS = 1e-5


def _rmsnorm(x, g):
    xf = x.astype(jnp.float32)
    y = xf * lax.rsqrt(jnp.mean(xf * xf, axis=-1, keepdims=True) + RMS_EPS)
    return (y * g.astype(jnp.float32)).astype(x.dtype)

def _layernorm(x, g, b):
    xf = x.astype(jnp.float32)
    mu = jnp.mean(xf, axis=-1, keepdims=True)
    var = jnp.mean(jnp.square(xf - mu), axis=-1, keepdims=True)
    y = (xf - mu) * lax.rsqrt(var + LN_EPS)
    return (y * g.astype(jnp.float32) + b.astype(jnp.float32)).astype(x.dtype)

def _modulate(h, shift, scale):
    return h * (1 + scale) + shift

def _swiglu(h, w_gate, w_up, w_down):
    return (jax.nn.silu(h @ w_gate) * (h @ w_up)) @ w_down

def _moe_swiglu(h, router, w_gate, w_up, w_down):
    shp = h.shape
    d = shp[-1]
    xt = h.reshape(-1, d)
    n_tok = xt.shape[0]
    n_asg = n_tok * TOP_K
    logits = (xt @ router).astype(jnp.float32)
    top_logit, top_e = lax.top_k(logits, TOP_K)
    gates = jax.nn.softmax(top_logit, axis=-1)
    flat_e = top_e.reshape(-1)
    flat_tok = jnp.arange(n_asg, dtype=jnp.int32) // TOP_K
    order = jnp.argsort(flat_e)
    s_e = flat_e[order]
    s_tok = flat_tok[order]
    s_gate = gates.reshape(-1)[order]
    counts = jnp.bincount(flat_e, length=N_EXPERTS)
    padded = (counts + MOE_BLOCK - 1) // MOE_BLOCK * MOE_BLOCK
    pad_end = jnp.cumsum(padded)
    pad_start = pad_end - padded
    start = jnp.cumsum(counts) - counts
    dest = pad_start[s_e] + jnp.arange(n_asg, dtype=jnp.int32) - start[s_e]
    n_blocks = (n_asg + MOE_BLOCK - 1) // MOE_BLOCK + N_EXPERTS
    slot_tok = jnp.full((n_blocks * MOE_BLOCK,), n_tok, jnp.int32).at[dest].set(s_tok)
    block_e = jnp.minimum(jnp.searchsorted(pad_end, jnp.arange(n_blocks) * MOE_BLOCK, side='right'), N_EXPERTS - 1)
    x_pad = jnp.concatenate([xt, jnp.zeros((1, d), xt.dtype)], axis=0)
    xb = x_pad[slot_tok].reshape(n_blocks, MOE_BLOCK, d)

    def expert_block(args):
        x_blk, e = args
        return _swiglu(x_blk, w_gate[e], w_up[e], w_down[e])

    yb = lax.map(expert_block, (xb, block_e)).reshape(-1, d)
    y = jnp.zeros_like(xt).at[s_tok].add(yb[dest] * s_gate[:, None].astype(xt.dtype))
    return y.reshape(shp)

def _na_column_layout():
    n_cb = GRID_W // NA_QCB
    q_cols = np.arange(GRID_W).reshape(n_cb, NA_QCB)
    blk_start = np.clip(np.arange(n_cb) * NA_QCB - NA_WIN_COLS // 2, 0, GRID_W - NA_KCB)
    key_cols = blk_start[:, None] + np.arange(NA_KCB)[None, :]
    win_start = np.clip(q_cols - NA_WIN_COLS // 2, 0, GRID_W - NA_WIN_COLS)
    kcol = key_cols[:, None, :]
    ws = win_start[:, :, None]
    mask = (kcol >= ws) & (kcol < ws + NA_WIN_COLS)
    rel_idx = np.clip(kcol - q_cols[:, :, None] + NA_WIN_COLS - 1, 0, 2 * NA_WIN_COLS - 2)
    return key_cols, mask, rel_idx

def _neighbourhood_attention(q, k, v, kc, vc, rpb):
    B, N, H, dh = q.shape
    rows = N // GRID_W
    kr = min(NA_WIN_ROWS, rows)
    n_cb = GRID_W // NA_QCB
    key_cols, col_mask, rel_idx = _na_column_layout()
    qg = (q * dh ** -0.5).reshape(B, rows, GRID_W, H, dh).transpose(1, 0, 3, 2, 4)
    kg = k.reshape(B, rows, GRID_W, H, dh).transpose(0, 3, 1, 2, 4)
    vg = v.reshape(B, rows, GRID_W, H, dh).transpose(0, 3, 1, 2, 4)
    kct = kc.transpose(0, 2, 1, 3)
    vct = vc.transpose(0, 2, 1, 3)
    rpb_cols = rpb[:, :, rel_idx]
    n_win = kr * NA_KCB

    def one_row(args):
        i, qi = args
        rs = jnp.clip(i - kr // 2, 0, rows - kr)
        ks = lax.dynamic_slice_in_dim(kg, rs, kr, axis=2)[:, :, :, key_cols]
        vs = lax.dynamic_slice_in_dim(vg, rs, kr, axis=2)[:, :, :, key_cols]
        qb = qi.reshape(B, H, n_cb, NA_QCB, dh)
        s_win = jnp.einsum('bhcqd,bhrckd->bhcqrk', qb, ks).astype(jnp.float32)
        bias = lax.dynamic_slice_in_dim(rpb_cols, rs - i + NA_WIN_ROWS - 1, kr, axis=1)
        bias = bias.transpose(0, 2, 3, 1, 4).astype(jnp.float32)
        s_win = jnp.where(col_mask[:, :, None, :], s_win + bias, -jnp.inf)
        s_ctx = jnp.einsum('bhcqd,bhld->bhcql', qb, kct).astype(jnp.float32)
        s = jnp.concatenate([s_win.reshape(B, H, n_cb, NA_QCB, n_win), s_ctx], axis=-1)
        p = jax.nn.softmax(s, axis=-1).astype(v.dtype)
        p_win = p[..., :n_win].reshape(B, H, n_cb, NA_QCB, kr, NA_KCB)
        o = (jnp.einsum('bhcqrk,bhrckd->bhcqd', p_win, vs)
             + jnp.einsum('bhcql,bhld->bhcqd', p[..., n_win:], vct))
        return o.reshape(B, H, GRID_W, dh)

    out = lax.map(one_row, (jnp.arange(rows), qg))
    return out.transpose(1, 0, 3, 2, 4).reshape(B, N, H * dh)

def _context_attention(q, k, v):
    B, L, H, dh = q.shape
    s = jnp.einsum('blhd,bmhd->bhlm', q, k).astype(jnp.float32) * (dh ** -0.5)
    p = jax.nn.softmax(s, axis=-1).astype(v.dtype)
    return jnp.einsum('bhlm,bmhd->blhd', p, v).reshape(B, L, H * dh)

def _token_shift(u, mu_prev, mu_next):
    zero = jnp.zeros_like(u[:, :1])
    prev = jnp.concatenate([zero, u[:, :-1]], axis=1)
    nxt = jnp.concatenate([u[:, 1:], zero], axis=1)
    return u + mu_prev * (prev - u) + mu_next * (nxt - u)

def _head_norm(y, g, b):
    mu = jnp.mean(y, axis=-1, keepdims=True)
    var = jnp.mean(jnp.square(y - mu), axis=-1, keepdims=True)
    yn = (y - mu) * lax.rsqrt(var + RW_GN_EPS)
    return yn.reshape(y.shape[0], y.shape[1], -1) * g + b

def _rwkv7_scan(r, w, k, v, z, b):
    G, H, dh = r.shape[1:]

    def step(S, inp):
        r_t, w_t, k_t, v_t, z_t, b_t = inp
        s_z = jnp.einsum('ghvk,ghk->ghv', S, z_t)
        S = S * w_t[:, :, None, :] + s_z[..., None] * b_t[:, :, None, :] + v_t[..., None] * k_t[:, :, None, :]
        return S, jnp.einsum('ghvk,ghk->ghv', S, r_t)

    _, y = lax.scan(step, jnp.zeros((G, H, dh, dh), jnp.float32), (r, w, k, v, z, b))
    return y

def _bi_rwkv7(ul, uc, mu_prev, mu_next, w0, w2, a0, a2, g2, k_k, k_a, r_k, gn_g, gn_b, need_ctx_out):
    B, N, _ = ul.shape
    L = uc.shape[1]
    T = L + N
    u = jnp.concatenate([_token_shift(uc, mu_prev, mu_next), _token_shift(ul, mu_prev, mu_next)],
                        axis=1).astype(jnp.float32)
    heads = lambda t: t.reshape(B, T, RW_HEADS, HEAD_DIM)
    r = u[..., :RW_WIDTH]
    k = u[..., RW_WIDTH:2 * RW_WIDTH]
    v = u[..., 2 * RW_WIDTH:3 * RW_WIDTH]
    kk = heads(k * k_k)
    kk = kk * lax.rsqrt(jnp.sum(kk * kk, axis=-1, keepdims=True) + 1e-12)
    rh, vh = heads(r), heads(v)
    per_dir = []
    for d in range(2):
        lo = 3 * RW_WIDTH + d * RW_LORA
        wd = u[..., lo:lo + RW_DECAY_RANK]
        ad = u[..., lo + RW_DECAY_RANK:lo + RW_DECAY_RANK + RW_A_RANK]
        gd = u[..., lo + RW_DECAY_RANK + RW_A_RANK:lo + RW_LORA]
        log_w = -jax.nn.softplus(-(w0[d] + jnp.tanh(wd) @ w2[d])) - 0.5
        decay = jnp.exp(-jnp.exp(log_w))
        a = jax.nn.sigmoid(a0[d] + ad @ a2[d])
        g = jax.nn.sigmoid(gd) @ g2[d]
        kd = heads(k * (1.0 + (a - 1.0) * k_a))
        per_dir.append((heads(decay), kd, kk * heads(a), g))
    perm = np.concatenate([np.arange(L)[::-1], L + np.arange(N)[::-1]])

    def stack(t_f, t_b):
        return jnp.concatenate([t_f, t_b[:, perm]], axis=0).swapaxes(0, 1)

    (w_f, k_f, b_f, _), (w_b, k_b, b_b, _) = per_dir
    y = _rwkv7_scan(stack(rh, rh), stack(w_f, w_b), stack(k_f, k_b), stack(vh, vh),
                    stack(-kk, -kk), stack(b_f, b_b)).swapaxes(0, 1)
    t0 = 0 if need_ctx_out else L
    y_dirs = (y[:B, t0:], y[B:][:, perm][:, t0:])
    outs = []
    for (_, kd, _, g), yd in zip(per_dir, y_dirs):
        bonus = (jnp.sum(rh * kd * r_k, axis=-1, keepdims=True) * vh)[:, t0:].reshape(B, T - t0, RW_WIDTH)
        outs.append((_head_norm(yd, gn_g, gn_b) + bonus) * g[:, t0:])
    out = (outs[0] + outs[1]).astype(ul.dtype)
    out_l = out[:, L - t0:]
    out_c = out[:, :L] if need_ctx_out else None
    return out_l, out_c

def _conformer_conv(u, dw_w, dw_b, ln_g, ln_b):
    h = u[..., :CV_WIDTH] * jax.nn.sigmoid(u[..., CV_WIDTH:])
    h = lax.conv_general_dilated(h, dw_w[:, None, :], (1,), [(CV_CONV_LEN // 2, CV_CONV_LEN // 2)],
                                 dimension_numbers=('NWC', 'WIO', 'NWC'),
                                 feature_group_count=CV_WIDTH) + dw_b
    return jax.nn.silu(_layernorm(h, ln_g, ln_b))

def _mixers(hl, hc, w_in, w_out, na_rpb, rw_mu_prev, rw_mu_next, rw_w0, rw_w2, rw_a0, rw_a2, rw_g2,
            rw_k_k, rw_k_a, rw_r_k, rw_gn_g, rw_gn_b, cv_dw_w, cv_dw_b, cv_ln_g, cv_ln_b, need_ctx_out):
    o_rw = 3 * NA_WIDTH
    o_cv = o_rw + RW_IN
    heads = lambda t: t.reshape(t.shape[0], t.shape[1], NA_HEADS, HEAD_DIM)
    pl = hl @ w_in
    c_off = 0 if need_ctx_out else NA_WIDTH
    pc = hc @ (w_in if need_ctx_out else w_in[:, NA_WIDTH:o_cv])
    kc = heads(pc[..., NA_WIDTH - c_off:2 * NA_WIDTH - c_off])
    vc = heads(pc[..., 2 * NA_WIDTH - c_off:o_rw - c_off])
    na_l = _neighbourhood_attention(heads(pl[..., :NA_WIDTH]), heads(pl[..., NA_WIDTH:2 * NA_WIDTH]),
                                    heads(pl[..., 2 * NA_WIDTH:o_rw]), kc, vc, na_rpb)
    rw_l, rw_c = _bi_rwkv7(pl[..., o_rw:o_cv], pc[..., o_rw - c_off:o_cv - c_off], rw_mu_prev, rw_mu_next,
                           rw_w0, rw_w2, rw_a0, rw_a2, rw_g2, rw_k_k, rw_k_a, rw_r_k, rw_gn_g, rw_gn_b,
                           need_ctx_out)
    cv_l = _conformer_conv(pl[..., o_cv:], cv_dw_w, cv_dw_b, cv_ln_g, cv_ln_b)
    out_l = jnp.concatenate([na_l, rw_l, cv_l], axis=-1) @ w_out
    if not need_ctx_out:
        return out_l, None
    na_c = _context_attention(heads(pc[..., :NA_WIDTH]), kc, vc)
    cv_c = _conformer_conv(pc[..., o_cv:], cv_dw_w, cv_dw_b, cv_ln_g, cv_ln_b)
    out_c = jnp.concatenate([na_c, rw_c, cv_c], axis=-1) @ w_out
    return out_l, out_c

def second_inputs(seed: int = 0) -> dict:
    key = jax.random.key(seed)
    ks = iter(jax.random.split(key, 40))
    f32 = jnp.float32

    def nrm(shape, std):
        return jax.random.normal(next(ks), shape, f32) * std

    def uni(shape, lo, hi):
        return jax.random.uniform(next(ks), shape, f32, lo, hi)

    D = D_MODEL
    return {
        'x': nrm((BATCH, SEQ, D), 1.0),
        'c': nrm((BATCH, D), 1.0),
        'ctx': nrm((BATCH, CTX_LEN, D), 1.0),
        'c_ctx': nrm((D,), 1.0),
        'norm1_g': 1.0 + nrm((DEPTH_2, D), 0.02),
        'norm2_g': 1.0 + nrm((DEPTH_2, D), 0.02),
        'mod_w': nrm((DEPTH_2, D, 6 * D), 0.5 * D ** -0.5),
        'mod_b': nrm((DEPTH_2, 6 * D), 0.02),
        'w_in': nrm((DEPTH_2, D, IN_WIDTH), D ** -0.5),
        'w_out': nrm((DEPTH_2, MIX_WIDTH_2, D), MIX_WIDTH_2 ** -0.5),
        'na_rpb': nrm((DEPTH_2, NA_HEADS, 2 * NA_WIN_ROWS - 1, 2 * NA_WIN_COLS - 1), 0.1),
        'rw_mu_prev': uni((DEPTH_2, RW_IN), 0.0, 0.5),
        'rw_mu_next': uni((DEPTH_2, RW_IN), 0.0, 0.5),
        'rw_w0': uni((DEPTH_2, 2, RW_WIDTH), -6.0, 1.0),
        'rw_w2': nrm((DEPTH_2, 2, RW_DECAY_RANK, RW_WIDTH), 0.5 * RW_DECAY_RANK ** -0.5),
        'rw_a0': nrm((DEPTH_2, 2, RW_WIDTH), 0.3),
        'rw_a2': nrm((DEPTH_2, 2, RW_A_RANK, RW_WIDTH), 0.5 * RW_A_RANK ** -0.5),
        'rw_g2': nrm((DEPTH_2, 2, RW_GATE_RANK, RW_WIDTH), RW_GATE_RANK ** -0.5),
        'rw_k_k': 0.85 + nrm((DEPTH_2, RW_WIDTH), 0.02),
        'rw_k_a': 1.0 + nrm((DEPTH_2, RW_WIDTH), 0.02),
        'rw_r_k': nrm((DEPTH_2, RW_HEADS, HEAD_DIM), 0.1),
        'rw_gn_g': 1.0 + nrm((DEPTH_2, RW_WIDTH), 0.02),
        'rw_gn_b': nrm((DEPTH_2, RW_WIDTH), 0.02),
        'cv_dw_w': nrm((DEPTH_2, CV_CONV_LEN, CV_WIDTH), CV_CONV_LEN ** -0.5),
        'cv_dw_b': nrm((DEPTH_2, CV_WIDTH), 0.02),
        'cv_ln_g': 1.0 + nrm((DEPTH_2, CV_WIDTH), 0.02),
        'cv_ln_b': nrm((DEPTH_2, CV_WIDTH), 0.02),
        'ffn_w_gate': nrm((N_DENSE_LAYERS, D, D_FF), D ** -0.5),
        'ffn_w_up': nrm((N_DENSE_LAYERS, D, D_FF), D ** -0.5),
        'ffn_w_down': nrm((N_DENSE_LAYERS, D_FF, D), D_FF ** -0.5),
        'moe_router': nrm((N_MOE_LAYERS, D, N_EXPERTS), D ** -0.5),
        'moe_w_gate': nrm((N_MOE_LAYERS, N_EXPERTS, D, D_FF_EXPERT), D ** -0.5),
        'moe_w_up': nrm((N_MOE_LAYERS, N_EXPERTS, D, D_FF_EXPERT), D ** -0.5),
        'moe_w_down': nrm((N_MOE_LAYERS, N_EXPERTS, D_FF_EXPERT, D), D_FF_EXPERT ** -0.5),
        'final_g': 1.0 + nrm((D,), 0.02),
    }

def second_block(x, c, ctx, c_ctx, norm1_g, norm2_g, mod_w, mod_b, w_in, w_out, na_rpb, rw_mu_prev, rw_mu_next,
              rw_w0, rw_w2, rw_a0, rw_a2, rw_g2, rw_k_k, rw_k_a, rw_r_k, rw_gn_g, rw_gn_b, cv_dw_w, cv_dw_b,
              cv_ln_g, cv_ln_b, ffn_w_gate, ffn_w_up, ffn_w_down, moe_router, moe_w_gate, moe_w_up, moe_w_down,
              final_g):
    c_sil = jax.nn.silu(c)
    cc_sil = jax.nn.silu(c_ctx)
    xl, xc = x, ctx
    for layer in range(DEPTH_2):
        need_ctx = layer < DEPTH_2 - 1
        sh1, sc1, g1, sh2, sc2, g2 = jnp.split((c_sil @ mod_w[layer] + mod_b[layer])[:, None, :], 6, axis=-1)
        csh1, csc1, cg1, csh2, csc2, cg2 = jnp.split(cc_sil @ mod_w[layer] + mod_b[layer], 6, axis=-1)
        hl = _modulate(_rmsnorm(xl, norm1_g[layer]), sh1, sc1)
        hc = _modulate(_rmsnorm(xc, norm1_g[layer]), csh1, csc1)
        mix_l, mix_c = _mixers(hl, hc, w_in[layer], w_out[layer], na_rpb[layer], rw_mu_prev[layer],
                               rw_mu_next[layer], rw_w0[layer], rw_w2[layer], rw_a0[layer], rw_a2[layer],
                               rw_g2[layer], rw_k_k[layer], rw_k_a[layer], rw_r_k[layer], rw_gn_g[layer],
                               rw_gn_b[layer], cv_dw_w[layer], cv_dw_b[layer], cv_ln_g[layer], cv_ln_b[layer],
                               need_ctx)
        xl = xl + g1 * mix_l
        hl = _modulate(_rmsnorm(xl, norm2_g[layer]), sh2, sc2)
        j = layer // 2
        if layer % 2 == 0:
            xl = xl + g2 * _swiglu(hl, ffn_w_gate[j], ffn_w_up[j], ffn_w_down[j])
        else:
            xl = xl + g2 * _moe_swiglu(hl, moe_router[j], moe_w_gate[j], moe_w_up[j], moe_w_down[j])
        if need_ctx:
            xc = xc + cg1 * mix_c
            hc = _modulate(_rmsnorm(xc, norm2_g[layer]), csh2, csc2)
            if layer % 2 == 0:
                xc = xc + cg2 * _swiglu(hc, ffn_w_gate[j], ffn_w_up[j], ffn_w_down[j])
            else:
                xc = xc + cg2 * _moe_swiglu(hc, moe_router[j], moe_w_gate[j], moe_w_up[j], moe_w_down[j])
    return _rmsnorm(xl, final_g)


def setup_inputs(seed=0):
    out = dict(first_inputs(seed))
    for name, value in second_inputs(seed + 1).items():
        if name != "x":
            out[name + "_2"] = value
    return out


def reference(
    x, mem, w_in, g_mix, g_out_dil, g_out_moba, w_out, rel_bias, g_cross, g_mem, w_q_mem,
    w_kv_mem, w_o_mem, g_ffn, w_gate, w_up, conv_w, conv_b, w_down, g_final, c_2, ctx_2,
    c_ctx_2, norm1_g_2, norm2_g_2, mod_w_2, mod_b_2, w_in_2, w_out_2, na_rpb_2, rw_mu_prev_2,
    rw_mu_next_2, rw_w0_2, rw_w2_2, rw_a0_2, rw_a2_2, rw_g2_2, rw_k_k_2, rw_k_a_2, rw_r_k_2,
    rw_gn_g_2, rw_gn_b_2, cv_dw_w_2, cv_dw_b_2, cv_ln_g_2, cv_ln_b_2, ffn_w_gate_2, ffn_w_up_2,
    ffn_w_down_2, moe_router_2, moe_w_gate_2, moe_w_up_2, moe_w_down_2, final_g_2,
):
    x = first_block(
        x, mem, w_in, g_mix, g_out_dil, g_out_moba, w_out, rel_bias, g_cross, g_mem, w_q_mem,
        w_kv_mem, w_o_mem, g_ffn, w_gate, w_up, conv_w, conv_b, w_down, g_final,
    )
    return second_block(
        x, c_2, ctx_2, c_ctx_2, norm1_g_2, norm2_g_2, mod_w_2, mod_b_2, w_in_2, w_out_2,
        na_rpb_2, rw_mu_prev_2, rw_mu_next_2, rw_w0_2, rw_w2_2, rw_a0_2, rw_a2_2, rw_g2_2,
        rw_k_k_2, rw_k_a_2, rw_r_k_2, rw_gn_g_2, rw_gn_b_2, cv_dw_w_2, cv_dw_b_2, cv_ln_g_2,
        cv_ln_b_2, ffn_w_gate_2, ffn_w_up_2, ffn_w_down_2, moe_router_2, moe_w_gate_2,
        moe_w_up_2, moe_w_down_2, final_g_2,
    )


_drawn_inputs = setup_inputs


def setup_inputs(seed=0):
    import zlib

    import numpy as np

    out = dict(_drawn_inputs(seed))
    spreads = {}
    factors = {'g_out_dil': 3.897,
     'g_out_moba': 4.06,
     'g_cross': 8.0,
     'g_mem': 8.0,
     'g_ffn': 3.938,
     'conv_b': 4.537,
     'norm1_g_2': 5.891,
     'norm2_g_2': 11.057,
     'na_rpb_2': 31.826,
     'rw_w2_2': 4.67,
     'rw_k_k_2': 43.776,
     'rw_k_a_2': 3.961,
     'rw_gn_g_2': 64.0,
     'rw_gn_b_2': 64.0,
     'cv_dw_b_2': 59.266,
     'cv_ln_g_2': 51.504,
     'cv_ln_b_2': 64.0,
     'final_g_2': 8.4}
    for name, (base, spread) in spreads.items():
        noise = np.random.default_rng([zlib.crc32(name.encode()), seed]).standard_normal(out[name].shape)
        drawn = base * np.exp(spread * noise) if base else spread * noise
        out[name] = jnp.asarray(drawn.astype(out[name].dtype))
    for name, factor in factors.items():
        out[name] = (out[name] * factor).astype(out[name].dtype)
    return out
```

```python
import math
from contextlib import ExitStack

import numpy as np

import concourse.bass as bass
from concourse import mybir

F32 = mybir.dt.float32
U32 = mybir.dt.uint32
ALU = mybir.AluOpType
ACT = mybir.ActivationFunctionType
AX_X = mybir.AxisListType.X

P = 128
SEQ = 256
T2 = 2 * SEQ
D = 1024
DT = D // P
HD = 64
N_BUCKETS = 32
MAX_DISTANCE = 2048
D_FF = 2816
D_FFE = 3584
N_EXPERTS = 8
RW_WIDTH = 256
CV_LEN = 31
GRID_W = 64
NEG = -1e30
EPS = 1e-6
LN_EPS = 1e-5
RW_GN_EPS = 64e-5
CHUNK = 64
DECAY_SCALE = math.exp(-0.5)
WEIGHT_SLOTS = 7
GROUP = 512
TILE_K = 4
CTX = slice(0, SEQ)
LAT = slice(SEQ, T2)
BOTH = slice(0, T2)


def rel_bucket_of(n):
    half = N_BUCKETS // 2
    n = np.maximum(n, 0)
    nf = np.maximum(n, 1).astype(np.float32)
    large = half + (np.log(nf / np.float32(half)) / np.float32(math.log(MAX_DISTANCE / half))
                    * np.float32(N_BUCKETS - half)).astype(np.int32)
    return np.where(n < half, n, np.minimum(large, N_BUCKETS - 1))


def multiplicity(d):
    return (d >= 0) * ((d <= 128).astype(int) + (d % 4 == 0) + (d % 16 == 0))


def shape_tables():
    p = np.arange(P)
    tab = {}
    tab["ident"] = np.eye(P)
    tab["ones"] = np.ones((P, P))
    tab["headones"] = (p[:, None] // HD == p[None, :] // HD).astype(float)
    j = np.arange(T2)
    dist = SEQ - 1 - j
    for name, seen in (("bucket_dil", multiplicity(dist) > 0), ("bucket_moba", dist >= 0)):
        m = np.zeros((P, T2))
        m[rel_bucket_of(dist), j] = seen
        m[N_BUCKETS, :] = ~seen
        tab[name] = m
    t = np.arange(SEQ).reshape(2, P).T[:, :, None]
    tab["count"] = multiplicity(t - np.arange(SEQ)[None, None, :]).reshape(P, 2 * SEQ)
    qc, kc = p % GRID_W, np.arange(SEQ) % GRID_W
    tab["flip"] = np.eye(P)[::-1]
    tab["flip_rows"] = np.kron(np.eye(2), np.eye(GRID_W)[::-1])
    qc = GRID_W - 1 - qc
    start = np.clip(qc - 8, 0, GRID_W - 16)[:, None]
    tab["window"] = np.where((kc >= start) & (kc < start + 16), 0.0, NEG)
    row, col = p[:, None], p[None, :]
    same = row // CHUNK == col // CHUNK
    for d in range(2):
        before = (row < col) if d == 0 else (row > col)
        tab[f"causal{d}"] = np.stack([before & same, (before | (row == col)) & same], 1).reshape(P, 2 * P)
        for lv in range(6):
            s = 1 << lv
            tab[f"level{d}_{lv}"] = before & (row // (2 * s) == col // (2 * s)) & (row // s != col // s)
    tab["restart"] = np.broadcast_to(j % CHUNK != 0, (P, T2))
    tab["iota8"] = np.broadcast_to(np.arange(8), (P, 8))
    return {k: np.asarray(v, np.float32) for k, v in tab.items()}


_TABLES = shape_tables()
RESIDENT = ("ident", "ones", "headones", "iota8")
_TABLES = {**{k: _TABLES[k] for k in RESIDENT}, **_TABLES}
RESIDENT_COLS = sum(_TABLES[k].shape[1] for k in RESIDENT)
TABLE_AT = {}
_at = 0
for _name, _v in _TABLES.items():
    TABLE_AT[_name] = (_at, _v.shape[1])
    _at += _v.shape[1]
TABLE_COLS = _at


class Counted:

    def __init__(self, sem):
        self.sem, self.base = sem, 0

    def at(self, n):
        return self.base + n

    def advance(self, n):
        self.base += n


class Arena:

    def __init__(self, tensor, size):
        self.tensor, self.size, self.used = tensor, size, {}

    def take(self, name, *dims):
        n = 1
        for d in dims:
            n *= d
        at = 0
        for a, k in sorted(self.used.values()):
            if at + n <= a:
                break
            at = max(at, a + k)
        assert at + n <= self.size, (name, n, at, self.size, self.used)
        assert name not in self.used, name
        self.used[name] = (at, n)
        view = self.tensor[:, at:at + n]
        if len(dims) == 2:
            view = view.rearrange("p (a b) -> p a b", a=dims[0])
        if len(dims) == 3:
            view = view.rearrange("p (a b c) -> p a b c", a=dims[0], b=dims[1])
        if len(dims) == 4:
            view = view.rearrange("p (a b c d) -> p a b c d", a=dims[0], b=dims[1], c=dims[2])
        return view

    def free(self, *names):
        for n in names:
            del self.used[n]


class Program:
    def __init__(self, nc, ins, out, ctx):
        self.nc, self.ins, self.out, self.ctx = nc, ins, out, ctx
        self.counts = {}
        self.ring = self.sb("weight_ring", [P, WEIGHT_SLOTS, TILE_K, GROUP])
        self.xT = self.sb("residual", [P, DT, T2])
        self.hT = self.sb("normed", [P, DT, T2])
        self.table = self.sb("tables", [P, RESIDENT_COLS])
        self.small = self.sb("small", [P, 1024])
        size = nc.sbuf_bytes_remaining // 4 - 64
        self.arena = Arena(self.sb("work", [P, size]), size)
        self.bank = [ctx.enter_context(nc.psum_tensor(f"bank{i}", [P, 512], F32))[:, :] for i in range(8)]
        self.slot_full = [self.counted(f"slot{i}_full") for i in range(WEIGHT_SLOTS)]
        self.tile_used = self.counted("tile_used")
        self.weights = []
        self.issued = 0
        self.taken = 0
        self.small_at = 0
        self.vec = {}

    def sb(self, name, shape, dt=F32):
        return self.ctx.enter_context(self.nc.sbuf_tensor(name, shape, dt))

    def counted(self, name):
        if name not in self.counts:
            self.counts[name] = Counted(self.ctx.enter_context(self.nc.semaphore(name)))
        return self.counts[name]

    def tab(self, name):
        a, n = TABLE_AT[name]
        return self.table[:, a:a + n]

    def table_src(self, first, last=None):
        a = TABLE_AT[first][0]
        b, n = TABLE_AT[last or first]
        return self.ins["tables"][:, a:b + n]

    def smallcols(self, n):
        a = self.small_at
        self.small_at += n
        assert self.small_at <= 1024
        return self.small[:, a:a + n]

    def plan(self, w, row0, rows, col0, cols):
        for c in range(col0, col0 + cols, GROUP):
            width = min(GROUP, col0 + cols - c)
            for r in range(row0, row0 + rows, TILE_K * P):
                nk = min(TILE_K, (row0 + rows - r) // P)
                self.weights.append((w[r:r + nk * P, c:c + width].rearrange("(k p) n -> p k n", p=P), nk, width))

    def load_weights(self, sync, used):
        used_total = self.taken + used
        while self.issued < min(len(self.weights), used_total + WEIGHT_SLOTS):
            i = self.issued
            src, nk, width = self.weights[i]
            if i >= WEIGHT_SLOTS:
                sync.wait_ge(self.tile_used.sem, i - WEIGHT_SLOTS + 1)
            s = self.slot_full[i % WEIGHT_SLOTS]
            sync.dma_start(self.ring[:, i % WEIGHT_SLOTS, 0:nk, 0:width], src).then_inc(s.sem, 16)
            self.issued += 1

    def wait_tile(self, pe, i):
        pe.wait_ge(self.slot_full[i % WEIGHT_SLOTS].sem, 16 * (i // WEIGHT_SLOTS + 1))

    def linear(self, groups):
        nc = self.nc
        used = self.tile_used
        evs = {n: self.counted(f"banks_emptied_by_{n}") for n in ("vector", "scalar")}
        first = self.taken
        start, t = [], first
        for g in groups:
            start.append(t)
            t += -(-g["rows"] // (TILE_K * P))
        end = t
        ends = start[1:] + [end]

        def banks(gi):
            return self.bank[4 * (gi % 2):4 * (gi % 2) + 4]

        def emptied(gi, name):
            return sum(1 for g in groups[:gi + 1] if name in g["evac"])

        with nc.Block() as block:
            @block.sync
            def _(sync):
                self.load_weights(sync, end - first)

            @block.tensor
            def _(pe):
                for gi, g in enumerate(groups):
                    if gi >= 2:
                        for name in groups[gi - 2]["evac"]:
                            pe.wait_ge(evs[name].sem, evs[name].at(emptied(gi - 2, name)))
                    total = g["rows"] // P
                    k0 = 0
                    for i in range(start[gi], ends[gi]):
                        _, nk, width = self.weights[i]
                        self.wait_tile(pe, i)
                        w = self.ring[:, i % WEIGHT_SLOTS]
                        if g["kind"] == "F":
                            for j in range(width // P):
                                for k in range(nk):
                                    a = g["act"](k0 + k)
                                    last = nc.tensor.matmul(banks(gi)[j][:, 0:a.shape[-1]], w[:, k, j * P:(j + 1) * P], a,
                                                            start=k0 + k == 0, stop=k0 + k == total - 1)
                        else:
                            n_tok = g["act"](0).shape[-1] // P
                            for j in range(n_tok):
                                for k in range(nk):
                                    a = g["act"](k0 + k)[:, j * P:(j + 1) * P]
                                    last = nc.tensor.matmul(banks(gi)[j][:, 0:width], a, w[:, k, 0:width],
                                                            start=k0 + k == 0, stop=k0 + k == total - 1)
                        last.then_inc(used.sem, 1)
                        k0 += nk

            @block.vector
            def _(dve):
                for gi, g in enumerate(groups):
                    if "vector" in g["evac"]:
                        dve.wait_ge(used.sem, used.at(ends[gi] - first))
                        if g.get("vector_after_scalar"):
                            dve.wait_ge(evs["scalar"].sem, evs["scalar"].at(emptied(gi, "scalar")))
                        g["evac"]["vector"](dve, banks(gi)).then_inc(evs["vector"].sem, 1)

            @block.scalar
            def _(act):
                for gi, g in enumerate(groups):
                    if "scalar" in g["evac"]:
                        act.wait_ge(used.sem, used.at(ends[gi] - first))
                        if g.get("scalar_after_vector"):
                            act.wait_ge(evs["vector"].sem, evs["vector"].at(emptied(gi - 1, "vector")))
                        g["evac"]["scalar"](act, banks(gi)).then_inc(evs["scalar"].sem, 1)

        n = len(groups)
        for name, s in evs.items():
            s.advance(emptied(n - 1, name))
        used.advance(end - first)
        self.taken = end

    def transpose_in(self, jobs):
        nc = self.nc
        landed, turned, moved = self.counted("rows_landed"), self.counted("rows_turned"), self.counted("turned_moved")
        n = len(jobs)
        rows = self.arena.take("rows", n, 2, D)
        ident = self.tab("ident")
        with nc.Block() as block:
            @block.sync
            def _(sync):
                for i, (src, _) in enumerate(jobs):
                    sync.dma_start(rows[:, i], src.rearrange("(t p) d -> p t d", p=P)).then_inc(landed.sem, 16)
                self.load_weights(sync, 0)

            @block.tensor
            def _(pe):
                pe.wait_ge(landed.sem, landed.at(16 * n))
                for i in range(n):
                    for k in range(DT):
                        step = i * DT + k
                        if step >= 8:
                            pe.wait_ge(moved.sem, moved.at(step - 7))
                        for t in range(2):
                            last = nc.tensor.transpose(self.bank[step % 8][:, t * P:(t + 1) * P], rows[:, i, t, k * P:(k + 1) * P], ident)
                        last.then_inc(turned.sem, 1)

            @block.vector
            def _(dve):
                for i, (_, dst) in enumerate(jobs):
                    for k in range(DT):
                        step = i * DT + k
                        dve.wait_ge(turned.sem, turned.at(step + 1))
                        nc.vector.tensor_copy(dst[:, k, :], self.bank[step % 8][:, 0:SEQ]).then_inc(moved.sem, 1)
        landed.advance(16 * n)
        turned.advance(n * DT)
        moved.advance(n * DT)
        self.arena.free("rows")

    def rmsnorm(self, src, n_tiles, tokens, parts, eps=EPS):
        nc = self.nc
        squared, summed = self.counted("squared"), self.counted("squares_summed")
        chain, scaled, shifted = self.counted("mean_ready"), self.counted("scaled"), self.counted("shifted")
        rooted = self.counted("rooted")
        sq = self.arena.take("sq", 2, tokens)
        rstd = self.arena.take("rstd", tokens)
        n = len(parts) * n_tiles
        with nc.Block() as block:
            @block.scalar
            def _(act):
                for k in range(n_tiles):
                    if k >= 2:
                        act.wait_ge(summed.sem, summed.at(k - 1))
                    nc.scalar.activation(sq[:, k % 2], src(k), ACT.Square).then_inc(squared.sem, 1)
                act.wait_ge(chain.sem, chain.at(2))
                nc.scalar.activation(rstd, rstd, ACT.Sqrt).then_inc(rooted.sem, 1)
                i = 0
                for _, dst, _, shift in parts:
                    for k in range(n_tiles):
                        i += 1
                        if shift is not None:
                            act.wait_ge(scaled.sem, scaled.at(i))
                            nc.scalar.activation(dst(k), dst(k), ACT.Identity, bias=shift(k)).then_inc(shifted.sem, 1)

            @block.tensor
            def _(pe):
                for k in range(n_tiles):
                    pe.wait_ge(squared.sem, squared.at(k + 1))
                    nc.tensor.matmul(self.bank[0][:, 0:tokens], self.tab("ones"), sq[:, k % 2], start=k == 0,
                                     stop=k == n_tiles - 1).then_inc(summed.sem, 1)

            @block.vector
            def _(dve):
                dve.wait_ge(summed.sem, summed.at(n_tiles))
                nc.vector.tensor_scalar(rstd, self.bank[0][:, 0:tokens], 1.0 / (n_tiles * P), eps, ALU.mult, ALU.add).then_inc(chain.sem, 1)
                dve.wait_ge(chain.sem, chain.at(1))
                dve.wait_ge(chain.sem, chain.at(1))
                nc.vector.reciprocal(rstd, rstd).then_inc(chain.sem, 1)
                dve.wait_ge(rooted.sem, rooted.at(1))
                for sl, dst, scale, _ in parts:
                    for k in range(n_tiles):
                        nc.vector.scalar_tensor_tensor(dst(k), src(k)[:, sl], scale(k), rstd[:, sl], ALU.mult, ALU.mult).then_inc(scaled.sem, 1)
        squared.advance(n_tiles)
        summed.advance(n_tiles)
        chain.advance(2)
        rooted.advance(1)
        scaled.advance(n)
        shifted.advance(sum(n_tiles for p in parts if p[3] is not None))
        self.arena.free("sq", "rstd")

    def attention(self, units, flip=None):
        nc = self.nc
        scored, probs_ready = self.counted("scores_ready"), self.counted("probs_ready")
        dstep, expd, turned, tmoved = self.counted("softmax_step"), self.counted("exp_done"), self.counted("probs_turned"), self.counted("probsT_ready")
        mixed, outm, biased = self.counted("values_mixed"), self.counted("mixed_moved"), self.counted("max_ready")
        keys = max(u["k"][0].shape[-1] for u in units)
        pr = self.arena.take("pr", 2, keys)
        pt = self.arena.take("pt", 2, keys)
        st = self.arena.take("st", 2, 4)
        ident = self.tab("ident")
        S = self.bank[0:3]
        PT = self.bank[3:6]
        O = self.bank[6:8]
        n = len(units)
        with nc.Block() as block:
            @block.tensor
            def _(pe):
                def scores(i):
                    u = units[i]
                    nk = u["k"][0].shape[-1]
                    if i >= 3:
                        pe.wait_ge(expd.sem, expd.at(i - 2))
                    for b in range(len(u["q"])):
                        last = nc.tensor.matmul(S[i % 3][:, 0:nk], u["q"][b], u["k"][b], start=b == 0,
                                                stop=u["bias"] is None and b == len(u["q"]) - 1)
                    if u["bias"] is not None:
                        last = nc.tensor.matmul(S[i % 3][:, nk - u["bias"].shape[-1]:nk], flip, u["bias"], start=False, stop=True)
                    last.then_inc(scored.sem, 1)

                scores(0)
                if n > 1:
                    scores(1)
                for i, u in enumerate(units):
                    if i + 2 < n:
                        scores(i + 2)
                    nkt = u["k"][0].shape[-1] // P
                    pe.wait_ge(probs_ready.sem, probs_ready.at(i + 1))
                    if i >= 3:
                        pe.wait_ge(tmoved.sem, tmoved.at(i - 2))
                    for t in range(nkt):
                        last = nc.tensor.transpose(PT[i % 3][:, t * P:(t + 1) * P], pr[:, i % 2, t * P:(t + 1) * P], ident)
                    last.then_inc(turned.sem, 1)
                    pe.wait_ge(tmoved.sem, tmoved.at(i + 1))
                    if i >= 2:
                        pe.wait_ge(outm.sem, outm.at(i - 1))
                    hw = u["v"][0].shape[-1]
                    a = u["out_part"]
                    for b in range(-(-hw // P)):
                        w = min(P, hw)
                        for t in range(nkt):
                            last = nc.tensor.matmul(O[i % 2][a:a + w, b * P:(b + 1) * P], u["v"][t][:, b * P:b * P + w],
                                                    pt[:, i % 2, t * P:(t + 1) * P], start=t == 0, stop=t == nkt - 1)
                    last.then_inc(mixed.sem, 1)

            @block.vector
            def _(dve):
                c = 0

                def head(i):
                    u = units[i]
                    nk = u["k"][0].shape[-1]
                    dve.wait_ge(scored.sem, scored.at(i + 1))
                    if i >= 2:
                        dve.wait_ge(probs_ready.sem, probs_ready.at(i - 1))
                    nc.vector.tensor_reduce(st[:, i % 2, 0:1], S[i % 3][:, 0:nk], AX_X, ALU.max, negate=True).then_inc(biased.sem, 1)

                def tail(i):
                    nonlocal c
                    u = units[i]
                    e = pr[:, i % 2, 0:u["k"][0].shape[-1]]
                    den = st[:, i % 2, 1:2]
                    dve.wait_ge(expd.sem, expd.at(i + 1))
                    if u["count"] is not None:
                        nc.vector.scalar_tensor_tensor(e, e, 1.0, u["count"], ALU.mult, ALU.mult, accum_out=den).then_inc(dstep.sem, 1)
                        c += 1
                        dve.wait_ge(dstep.sem, dstep.at(c))
                    nc.vector.reciprocal(st[:, i % 2, 3:4], den).then_inc(dstep.sem, 1)
                    c += 1
                    dve.wait_ge(dstep.sem, dstep.at(c))
                    nc.vector.tensor_scalar(e, e, st[:, i % 2, 3:4], None, ALU.mult).then_inc(probs_ready.sem, 1)

                def move_out(i):
                    u = units[i]
                    dve.wait_ge(mixed.sem, mixed.at(i + 1))
                    a, w = u["out_part"], min(P, u["v"][0].shape[-1])
                    for b, o in enumerate(u["out"]):
                        last = nc.vector.tensor_copy(o, O[i % 2][a:a + w, b * P:(b + 1) * P])
                    last.then_inc(outm.sem, 1)

                head(0)
                for i in range(n):
                    if i + 1 < n:
                        head(i + 1)
                    tail(i)
                    if i >= 1:
                        move_out(i - 1)
                move_out(n - 1)
                dstep.count = c

            @block.scalar
            def _(act):
                def exponent(i):
                    u = units[i]
                    nk = u["k"][0].shape[-1]
                    act.wait_ge(biased.sem, biased.at(i + 1))
                    if i >= 2:
                        act.wait_ge(turned.sem, turned.at(i - 1))
                    nc.scalar.activation(pr[:, i % 2, 0:nk], S[i % 3][:, 0:nk], ACT.Exp, bias=st[:, i % 2, 0:1],
                                         accum_out=st[:, i % 2, 1:2]).then_inc(expd.sem, 1)

                exponent(0)
                for i, u in enumerate(units):
                    if i + 1 < n:
                        exponent(i + 1)
                    nk = u["k"][0].shape[-1]
                    act.wait_ge(turned.sem, turned.at(i + 1))
                    if i >= 2:
                        act.wait_ge(mixed.sem, mixed.at(i - 1))
                    nc.scalar.activation(pt[:, i % 2, 0:nk], PT[i % 3][:, 0:nk], ACT.Copy).then_inc(tmoved.sem, 1)
        for s in (scored, probs_ready, expd, turned, tmoved, mixed, outm, biased):
            s.advance(n)
        dstep.advance(dstep.count)
        self.arena.free("pr", "pt", "st")

    def load(self, pairs):
        nc = self.nc
        landed = self.counted("loads_landed")
        with nc.Block() as block:
            @block.sync
            def _(sync):
                for dst, src in pairs:
                    sync.dma_start(dst, src).then_inc(landed.sem, 16)
                sync.wait_ge(landed.sem, landed.at(16 * len(pairs)))
        landed.advance(16 * len(pairs))

    def load_vectors(self, specs):
        nc = self.nc
        groups, at = 0, 0
        places = []
        for name, src in specs:
            n = src.shape[0]
            if at % P + n > P:
                at += P - at % P
            places.append((name, src, at, n))
            self.vec[name] = at
            at += n
        groups = -(-at // P)
        self.vectors = self.arena.take("vectors", groups * P)
        rows = self.arena.take("vector_rows", groups, P)
        cleared, landed, turned = self.counted("rows_cleared"), self.counted("loads_landed"), self.counted("rows_turned")
        with nc.Block() as block:
            @block.vector
            def _(dve):
                nc.vector.memset(rows, 0.0).then_inc(cleared.sem, 1)
                dve.wait_ge(turned.sem, turned.at(groups))
                for g in range(groups):
                    nc.vector.tensor_copy(self.vectors[:, g * P:(g + 1) * P], self.bank[g][:, 0:P])

            @block.scalar
            def _(act):
                act.dma_start(self.table[:, :], self.ins["tables"][:, 0:RESIDENT_COLS]).then_inc(landed.sem, 16)
                act.wait_ge(cleared.sem, cleared.at(1))
                for _, src, a, n in places:
                    act.dma_start(rows[a % P:a % P + n, a // P, :], src).then_inc(landed.sem, 16)

            @block.sync
            def _(sync):
                self.load_weights(sync, 0)

            @block.tensor
            def _(pe):
                pe.wait_ge(landed.sem, landed.at(16 * (len(places) + 1)))
                for g in range(groups):
                    nc.tensor.transpose(self.bank[g][:, 0:P], rows[:, g, :], self.tab("ident")).then_inc(turned.sem, 1)
        cleared.advance(1)
        landed.advance(16 * (len(places) + 1))
        turned.advance(groups)
        self.arena.free("vector_rows")

    def col(self, name, i=0):
        a = self.vec[name] + i
        return self.vectors[:, a:a + 1]

    def cols(self, name, n, i=0):
        a = self.vec[name] + i
        return self.vectors[:, a:a + n]

    def bias_lines(self):
        nc, ins = self.nc, self.ins
        self.bias_dram = nc.dram_tensor("bias_lines", (16, T2), F32, kind="Internal")
        self.rpb_dram = nc.dram_tensor("rpb_lines", (2 * 8 * 15, 127), F32, kind="Internal")
        tabs = self.arena.take("buckets", 2, T2)
        rb = self.arena.take("rel_bias", 16)
        lines = self.arena.take("lines", 2, T2)
        zero = self.arena.take("zero", 254)
        ready, landed, made, moved, stored = (self.counted(n) for n in
                                              ("rel_bias_cleared", "loads_landed", "lines_made", "lines_moved", "lines_stored"))
        n_load = 2
        with nc.Block() as block:
            @block.vector
            def _(dve):
                nc.vector.memset(rb[0:64, :], NEG).then_inc(ready.sem, 1)
                nc.vector.memset(zero, 0.0).then_inc(ready.sem, 1)
                dve.wait_ge(made.sem, made.at(2))
                nc.vector.tensor_copy(lines[0:8, 0], self.bank[0][0:8, :]).then_inc(moved.sem, 1)
                nc.vector.tensor_copy(lines[0:8, 1], self.bank[1][0:8, :]).then_inc(moved.sem, 1)

            @block.sync
            def _(sync):
                sync.dma_start(tabs.rearrange("p a b -> p (a b)"), self.table_src("bucket_dil", "bucket_moba")).then_inc(landed.sem, 16)
                sync.wait_ge(ready.sem, ready.at(2))
                sync.dma_start(rb[0:N_BUCKETS, :], ins["rel_bias"].rearrange("h b -> b h"), allow_slow_non_contiguous=True).then_inc(landed.sem, 16)
                n = 2 * 8 * 15
                sync.dma_start(bass.AP(self.rpb_dram, 0, [[254, n // 2], [1, 254]]), zero[0:n // 2, :]).then_inc(stored.sem, 16)
                sync.wait_ge(stored.sem, stored.at(16))
                sync.dma_start(self.rpb_dram.ap()[:, 48:79], ins["na_rpb_2"].rearrange("l h r c -> (l h r) c")).then_inc(stored.sem, 16)
                sync.wait_ge(moved.sem, moved.at(2))
                for i in range(2):
                    sync.dma_start(self.bias_dram.ap()[8 * i:8 * i + 8, :], lines[0:8, i]).then_inc(stored.sem, 16)
                sync.wait_ge(stored.sem, stored.at(64))

            @block.tensor
            def _(pe):
                pe.wait_ge(landed.sem, landed.at(32))
                for i in range(2):
                    nc.tensor.matmul(self.bank[i][0:8, :], rb[0:N_BUCKETS + 1, 8 * i:8 * i + 8], tabs[0:N_BUCKETS + 1, i],
                                     start=True, stop=True).then_inc(made.sem, 1)
        ready.advance(2)
        landed.advance(32)
        made.advance(2)
        moved.advance(2)
        stored.advance(64)
        self.arena.free("buckets", "rel_bias", "lines", "zero")

    def copy_f(self, dst, j0, sl=BOTH, scale=None):
        def fn(eng, banks):
            for j in range(4):
                if scale is None:
                    last = self.nc.vector.tensor_copy(dst(j0 + j), banks[j][:, sl])
                else:
                    last = self.nc.vector.tensor_scalar(dst(j0 + j), banks[j][:, sl], scale, None, ALU.mult)
            return last
        return fn

    def residual(self, group, sl, gates=None):
        def fn(eng, banks):
            for j in range(4):
                t = 4 * group + j
                if gates is None:
                    last = self.nc.vector.tensor_tensor(self.xT[:, t, sl], banks[j][:, 0:sl.stop - sl.start], self.xT[:, t, sl], ALU.add)
                else:
                    for tok, column in gates:
                        src = banks[j][:, tok.start - sl.start:tok.stop - sl.start]
                        last = self.nc.vector.scalar_tensor_tensor(self.xT[:, t, tok], src, column(t), self.xT[:, t, tok], ALU.mult, ALU.add)
            return last
        return fn

    def block_one(self):
        nc, ins, ar = self.nc, self.ins, self.arena
        xT, hT = self.xT, self.hT
        x = lambda k: xT[:, k, LAT]
        h = lambda k: hT[:, k, LAT]
        memT = ar.take("memT", DT, SEQ)
        self.transpose_in([(ins["x"][0], xT[:, :, LAT]), (ins["mem"][0], memT), (ins["ctx_2"][0], xT[:, :, CTX])])

        bias = ar.take("bias", 16, 2, SEQ)
        count = ar.take("count", 2, SEQ)
        loads = [(count.rearrange("p a b -> p (a b)"), self.table_src("count"))]
        for hd in range(16):
            loads.append((bias[:, hd], bass.AP(self.bias_dram, hd * T2, [[1, P], [P, 2], [1, SEQ]])))
        flip = ar.take("flip", P)
        loads.append((flip, self.table_src("flip")))
        self.load(loads)

        self.rmsnorm(x, DT, SEQ, [(slice(0, SEQ), h, lambda k: self.col("g_mix", k), None)])
        qk = ar.take("qk", 16, SEQ)
        v = ar.take("v", 2, D)

        def v_evac(c):
            def fn(eng, banks):
                for t in range(2):
                    last = nc.vector.tensor_copy(v[:, t, c:c + 512], banks[t][:, :])
                return last
            return fn

        F = lambda rows, act, evac, **kw: dict(kind="F", rows=rows, act=act, evac=evac, **kw)
        T = lambda rows, act, evac, **kw: dict(kind="T", rows=rows, act=act, evac=evac, **kw)
        at = lambda a: (lambda j: a[:, j])
        half = slice(0, SEQ)
        self.linear([F(D, h, {"vector": self.copy_f(at(qk), 0, half, HD ** -0.5)}), F(D, h, {"vector": self.copy_f(at(qk), 4, half)}),
                     T(D, h, {"vector": v_evac(0)}),
                     F(D, h, {"vector": self.copy_f(at(qk), 8, half, HD ** -0.5)}), F(D, h, {"vector": self.copy_f(at(qk), 12, half)}),
                     T(D, h, {"vector": v_evac(512)})])
        y = ar.take("y", DT, SEQ)
        units = []
        for hd in range(16):
            g, a = 8 * (hd // 8), (hd % 2) * HD
            ft = (hd % 8) // 2
            for i in range(2):
                tq = slice(i * P, (i + 1) * P)
                units.append(dict(q=[qk[a:a + HD, g + ft, tq]], k=[qk[a:a + HD, g + 4 + ft, :]],
                                  v=[v[:, t, hd * HD:(hd + 1) * HD] for t in range(2)],
                                  out=[y[a:a + HD, hd // 2, tq]], out_part=a, bias=bias[:, hd, 1 - i],
                                  count=count[:, i] if hd < 8 else None))
        self.attention(units, flip)
        ar.free("bias", "count", "qk", "v", "flip")
        half_w = DT // 2
        for n, name in enumerate(("g_out_dil", "g_out_moba")):
            self.rmsnorm(lambda k: y[:, n * half_w + k], half_w, SEQ,
                         [(slice(0, SEQ), lambda k: h(n * half_w + k), lambda k: self.col(name, k), None)])
        ar.free("y")
        self.linear([F(D, h, {"vector": self.residual(g, LAT)}) for g in range(2)])

        self.rmsnorm(x, DT, SEQ, [(slice(0, SEQ), h, lambda k: self.col("g_cross", k), None)])
        self.rmsnorm(at(memT), DT, SEQ, [(slice(0, SEQ), at(memT), lambda k: self.col("g_mem", k), None)])
        q, km, v = ar.take("q", DT, SEQ), ar.take("km", DT, SEQ), ar.take("v", 2, D)
        self.linear([F(D, h, {"vector": self.copy_f(at(q), 0, half, 256 ** -0.5)}), F(D, h, {"vector": self.copy_f(at(q), 4, half, 256 ** -0.5)}),
                     F(D, at(memT), {"vector": self.copy_f(at(km), 0, half)}), F(D, at(memT), {"vector": self.copy_f(at(km), 4, half)}),
                     T(D, at(memT), {"vector": v_evac(0)}), T(D, at(memT), {"vector": v_evac(512)})])
        units = []
        for hd in range(4):
            for i in range(2):
                tq = slice(i * P, (i + 1) * P)
                units.append(dict(q=[q[:, 2 * hd + b, tq] for b in range(2)], k=[km[:, 2 * hd + b] for b in range(2)],
                                  v=[v[:, t, hd * 256:(hd + 1) * 256] for t in range(2)],
                                  out=[hT[:, 2 * hd + b, SEQ + i * P:SEQ + (i + 1) * P] for b in range(2)],
                                  out_part=0, bias=None, count=None))
        self.attention(units)
        ar.free("q", "km", "v", "memT")
        self.linear([F(D, h, {"vector": self.residual(g, LAT)}) for g in range(2)])

        self.rmsnorm(x, DT, SEQ, [(slice(0, SEQ), h, lambda k: self.col("g_ffn", k), None)])
        hidden = ar.take("hidden", D_FF // P, SEQ)
        conv = self.counted("conv_step")
        n_conv = 0

        def conv_evac(j0, n):
            def fn(dve, banks):
                nonlocal n_conv
                for tap in (2, 1, 0):
                    lag = 2 - tap
                    for j in range(n):
                        w = self.col(f"conv_w{tap}", j0 + j)
                        if lag == 0:
                            last = nc.vector.tensor_scalar(hidden[:, j0 + j], banks[j][:, 0:SEQ], w, None, ALU.mult)
                        else:
                            last = nc.vector.scalar_tensor_tensor(hidden[:, j0 + j, lag:SEQ], banks[j][:, 0:SEQ - lag], w,
                                                                  hidden[:, j0 + j, lag:SEQ], ALU.mult, ALU.add)
                    if lag < 2:
                        last.then_inc(conv.sem, 1)
                        n_conv += 1
                        dve.wait_ge(conv.sem, conv.at(n_conv))
                return last
            return fn

        def silu_evac(j0, n):
            def fn(act, banks):
                for j in range(j0, j0 + n):
                    last = nc.scalar.activation(hidden[:, j], hidden[:, j], ACT.Silu, bias=self.col("conv_b", j))
                return last
            return fn

        def up_evac(j0, n):
            def fn(dve, banks):
                for j in range(n):
                    last = nc.vector.tensor_tensor(hidden[:, j0 + j], banks[j][:, 0:SEQ], hidden[:, j0 + j], ALU.mult)
                return last
            return fn

        groups = []
        for j0 in range(0, D_FF // P, 4):
            n = min(4, D_FF // P - j0)
            groups.append(F(D, h, {"vector": conv_evac(j0, n)}))
            groups.append(F(D, h, {"scalar": silu_evac(j0, n), "vector": up_evac(j0, n)}, scalar_after_vector=True, vector_after_scalar=True))
        self.linear(groups)
        conv.advance(n_conv)
        self.linear([F(D_FF, at(hidden), {"vector": self.residual(g, LAT)}) for g in range(2)])
        ar.free("hidden")
        self.rmsnorm(x, DT, SEQ, [(slice(0, SEQ), x, lambda k: self.col("g_final", k), None)])

    def modulation(self, layer):
        nc = self.nc
        mod = self.smallcols(96).rearrange("p (j c) -> p j c", c=2)
        gain = self.smallcols(32).rearrange("p (n k c) -> p n k c", n=2, c=2)
        cs = self.cs

        def evac(g):
            def fn(dve, banks):
                for j in range(4):
                    last = nc.vector.tensor_scalar(mod[:, 4 * g + j, :], banks[j][:, 0:2], self.col(f"mod_b{layer}", 4 * g + j), None, ALU.add)
                return last
            return fn

        self.linear([dict(kind="F", rows=D, act=lambda k: cs[:, k, :], evac={"vector": evac(g)}) for g in range(6 * DT // 4)])
        with nc.Block() as block:
            @block.vector
            def _(dve):
                for n in range(2):
                    for k in range(DT):
                        g = self.col(f"norm{n + 1}_g{layer}", k)
                        nc.vector.tensor_scalar(gain[:, n, k, :], mod[:, (3 * n + 1) * DT + k, :], 1.0, g, ALU.add, ALU.mult)
        return mod, gain

    def modulated_norm(self, mod, gain, n, ctx):
        parts, base, tokens = [], 0, T2
        if not ctx:
            base, tokens = SEQ, SEQ
        for c, sl in ((1, CTX), (0, LAT)):
            if c == 1 and not ctx:
                continue
            parts.append((slice(sl.start - base, sl.stop - base), lambda k, sl=sl: self.hT[:, k, sl],
                          lambda k, c=c: gain[:, n, k, c:c + 1], lambda k, c=c: mod[:, 3 * n * DT + k, c:c + 1]))
        self.rmsnorm(lambda k: self.xT[:, k, base:T2], DT, tokens, parts)

    def rwkv(self, rwpad, layer):
        nc, ar, ins = self.nc, self.arena, self.ins
        restart = ar.take("restart", T2)
        w2a2 = ar.take("w2a2", 2, RW_WIDTH)
        g2 = ar.take("g2", 2, RW_WIDTH)
        sh = ar.take("sh", 10, T2)
        self.load([(restart, self.table_src("restart")),
                   (w2a2[0:HD], ins["rw_w2_2"][layer].rearrange("d r n -> r d n")),
                   (w2a2[HD:P], ins["rw_a2_2"][layer].rearrange("d r n -> r d n")),
                   (g2, ins["rw_g2_2"][layer].rearrange("d r n -> r d n"))])
        kept, step = self.counted("shift_kept"), self.counted("shift_step")
        with nc.Block() as block:
            @block.scalar
            def _(act):
                for j in range(10):
                    nc.scalar.activation(sh[:, j, :].rearrange("p (s t) -> p s t", s=2), rwpad[:, j, :, 1:SEQ + 1], ACT.Copy,
                                         scale=self.keep[:, 10 * layer + j:10 * layer + j + 1]).then_inc(kept.sem, 1)

            @block.vector
            def _(dve):
                for j in range(10):
                    s = sh[:, j, :].rearrange("p (s t) -> p s t", s=2)
                    dve.wait_ge(kept.sem, kept.at(j + 1))
                    nc.vector.scalar_tensor_tensor(s, rwpad[:, j, :, 0:SEQ], self.col(f"mu_prev{layer}", j), s, ALU.mult, ALU.add).then_inc(step.sem, 1)
                    dve.wait_ge(step.sem, step.at(j + 1))
                    nc.vector.scalar_tensor_tensor(s, rwpad[:, j, :, 2:SEQ + 2], self.col(f"mu_next{layer}", j), s, ALU.mult, ALU.add)
        kept.advance(10)
        step.advance(10)
        ar.free("rwpad")
        r, k, v = sh[:, 0:2], sh[:, 2:4], sh[:, 4:6]

        kk = ar.take("kk", 2, T2)
        sq = ar.take("sq", 2, T2)
        vtok = ar.take("vtok", 4, RW_WIDTH)
        step, summed, turned = self.counted("kk_step"), self.counted("kk_summed"), self.counted("v_turned")
        rooted = self.counted("rooted")
        with nc.Block() as block:
            @block.vector
            def _(dve):
                for f in range(2):
                    nc.vector.tensor_scalar(kk[:, f], k[:, f], self.col(f"k_k{layer}", f), None, ALU.mult).then_inc(step.sem, 1)
                dve.wait_ge(step.sem, step.at(2))
                nc.vector.tensor_tensor(sq, kk, kk, ALU.mult).then_inc(step.sem, 1)
                dve.wait_ge(summed.sem, summed.at(2))
                for f in range(2):
                    nc.vector.tensor_scalar(sq[:, f], self.bank[f], 1e-12, None, ALU.add).then_inc(step.sem, 1)
                dve.wait_ge(step.sem, step.at(5))
                nc.vector.reciprocal(sq, sq).then_inc(step.sem, 1)
                dve.wait_ge(rooted.sem, rooted.at(1))
                nc.vector.tensor_tensor(kk, kk, sq, ALU.mult)

            @block.tensor
            def _(pe):
                for t in range(4):
                    for f in range(2):
                        last = nc.tensor.transpose(self.bank[4 + t][:, f * P:(f + 1) * P], v[:, f, t * P:(t + 1) * P], self.tab("ident"))
                    last.then_inc(turned.sem, 1)
                pe.wait_ge(step.sem, step.at(3))
                for f in range(2):
                    nc.tensor.matmul(self.bank[f], self.tab("headones"), sq[:, f], start=True, stop=True).then_inc(summed.sem, 1)

            @block.scalar
            def _(act):
                for t in range(4):
                    act.wait_ge(turned.sem, turned.at(t + 1))
                    nc.scalar.activation(vtok[:, t], self.bank[4 + t][:, 0:RW_WIDTH], ACT.Copy)
                act.wait_ge(step.sem, step.at(6))
                nc.scalar.activation(sq, sq, ACT.Sqrt).then_inc(rooted.sem, 1)
        step.advance(6)
        rooted.advance(1)
        summed.advance(2)
        turned.advance(4)
        ar.free("sq")

        zr, bm, km, gate, pc = [], [], [], [], []
        for d in range(2):
            self.rwkv_direction(layer, d, sh, kk, restart, w2a2, g2, zr, bm, km, gate, pc)
        ar.free("sh", "kk", "restart", "w2a2", "g2")
        ytok = self.rwkv_scan(zr, bm, km, pc, vtok)
        ar.free("zr0", "zr1", "bm0", "bm1", "km0", "km1", "pc0", "pc1", "vtok")
        for d in range(2):
            self.rwkv_out(layer, ytok[:, d], gate[d])
        ar.free("ytok", "gate0", "gate1")

    def rwkv_direction(self, layer, d, sh, kk, restart, w2a2, g2, zr, bm, km, gate, pc):
        nc, ar = self.nc, self.arena
        r, k, v = sh[:, 0:2], sh[:, 2:4], sh[:, 4:6]
        lo = 6 + 2 * d
        z = ar.take(f"zr{d}", 2, 2, T2)
        b_, k_, g_ = ar.take(f"bm{d}", 2, T2), ar.take(f"km{d}", 2, T2), ar.take(f"gate{d}", 2, T2)
        pc_ = ar.take(f"pc{d}", 2, T2 // CHUNK)
        zr.append(z), bm.append(b_), km.append(k_), gate.append(g_), pc.append(pc_)
        ld, L, a, kd = (ar.take(n, 2, T2) for n in ("ld", "L", "a", "kd"))
        e = ar.take("e", 2, T2)
        lora, ranked, opened = self.counted("lora_ready"), self.counted("lora_summed"), self.counted("lora_opened")
        st, ex, bs = self.counted("factor_step"), self.counted("factor_exp"), self.counted("bonus_summed")
        n_chunk = T2 // CHUNK
        per_chunk = lambda x: x.rearrange("p (c t) -> p c t", t=CHUNK)
        with nc.Block() as block:
            @block.scalar
            def _(act):
                nc.scalar.activation(sh[0:HD, lo], sh[0:HD, lo], ACT.Tanh).then_inc(lora.sem, 1)
                nc.scalar.activation(sh[:, lo + 1], sh[:, lo + 1], ACT.Sigmoid).then_inc(lora.sem, 1)
                act.wait_ge(ranked.sem, ranked.at(1))
                for f in range(2):
                    nc.scalar.activation(ld[:, f], self.bank[f], ACT.Sigmoid, bias=self.col(f"w0{layer}", 2 * d + f))
                    last = nc.scalar.activation(a[:, f], self.bank[2 + f], ACT.Sigmoid, bias=self.col(f"a0{layer}", 2 * d + f))
                last.then_inc(opened.sem, 1)
                for f in range(2):
                    nc.scalar.activation(g_[:, f], self.bank[4 + f], ACT.Copy)
                act.wait_ge(st.sem, st.at(6))
                nc.scalar.activation(e, L, ACT.Exp).then_inc(ex.sem, 1)
                nc.scalar.activation(ld, ld, ACT.Exp).then_inc(ex.sem, 1)
                act.wait_ge(st.sem, st.at(7))
                nc.scalar.activation(e, L, ACT.Exp, scale=-1.0).then_inc(ex.sem, 1)

            @block.tensor
            def _(pe):
                pe.wait_ge(lora.sem, lora.at(2))
                for f in range(2):
                    c = slice(f * P, (f + 1) * P)
                    nc.tensor.matmul(self.bank[f], w2a2[0:HD, d, c], sh[0:HD, lo], start=True, stop=True)
                    nc.tensor.matmul(self.bank[2 + f], w2a2[HD:P, d, c], sh[HD:P, lo], start=True, stop=True)
                    last = nc.tensor.matmul(self.bank[4 + f], g2[:, d, c], sh[:, lo + 1], start=True, stop=True)
                last.then_inc(ranked.sem, 1)
                pe.wait_ge(st.sem, st.at(11))
                for f in range(2):
                    last = nc.tensor.matmul(self.bank[6 + f], self.tab("headones"), a[:, f], start=True, stop=True)
                last.then_inc(bs.sem, 1)

            @block.vector
            def _(dve):
                n = 0

                def after(last):
                    nonlocal n
                    last.then_inc(st.sem, 1)
                    n += 1
                    dve.wait_ge(st.sem, st.at(n))

                dve.wait_ge(opened.sem, opened.at(1))
                after(nc.vector.tensor_scalar(ld, ld, -DECAY_SCALE, None, ALU.mult))
                for f in range(2):
                    last = nc.vector.tensor_tensor_scan(L[:, f], restart, ld[:, f], 0.0, ALU.mult, ALU.add)
                after(last)
                for f in range(2):
                    total = per_chunk(L[:, f])[:, :, CHUNK - 1:CHUNK]
                    last = nc.vector.tensor_copy(pc_[:, f, :], total[:, :, 0])
                after(last)
                if d == 1:
                    for f in range(2):
                        last = nc.vector.tensor_tensor(per_chunk(L[:, f]), pc_[:, f, :].unsqueeze(2).to_broadcast([P, n_chunk, CHUNK]),
                                                       per_chunk(L[:, f]), ALU.subtract)
                after(last if d == 1 else nc.vector.tensor_copy(e[:, 0, 0:1], L[:, 0, 0:1]))
                if d == 1:
                    after(nc.vector.tensor_tensor(L, L, ld, ALU.add))
                else:
                    after(nc.vector.tensor_copy(e[:, 0, 0:1], L[:, 0, 0:1]))
                after(nc.vector.tensor_tensor(ld, L, ld, ALU.subtract))
                for f in range(2):
                    last = nc.vector.tensor_scalar(kd[:, f], a[:, f], -1.0, self.col(f"k_a{layer}", f), ALU.add, ALU.mult)
                dve.wait_ge(ex.sem, ex.at(2))
                nc.vector.tensor_tensor(z[:, :, 1], r, e, ALU.mult)
                after(nc.vector.scalar_tensor_tensor(z[:, :, 0], kk, -1.0, ld, ALU.mult, ALU.mult))
                after(nc.vector.scalar_tensor_tensor(kd, kd, 1.0, k, ALU.add, ALU.mult))
                after(nc.vector.tensor_tensor(b_, kk, a, ALU.mult))
                dve.wait_ge(ex.sem, ex.at(3))
                nc.vector.tensor_tensor(b_, b_, e, ALU.mult)
                after(nc.vector.tensor_tensor(k_, kd, e, ALU.mult))
                for f in range(2):
                    last = nc.vector.scalar_tensor_tensor(a[:, f], r[:, f], self.col(f"r_k{layer}", f), kd[:, f], ALU.mult, ALU.mult)
                after(last)
                dve.wait_ge(bs.sem, bs.at(1))
                for f in range(2):
                    last = nc.vector.tensor_tensor(ld[:, f], self.bank[6 + f], v[:, f], ALU.mult)
                after(last)
                out = self.hT[:, 4:6, :]
                if d == 0:
                    nc.vector.tensor_tensor(out, ld, g_, ALU.mult)
                else:
                    after(nc.vector.tensor_tensor(ld, ld, g_, ALU.mult))
                    nc.vector.tensor_tensor(out, out, ld, ALU.add)
                st.n = n
        lora.advance(2)
        for s in (ranked, opened, bs):
            s.advance(1)
        ex.advance(3)
        st.advance(st.n)
        with nc.Block() as block:
            @block.scalar
            def _(act):
                nc.scalar.activation(pc_, pc_, ACT.Exp)
        ar.free("ld", "L", "a", "kd", "e")

    def rwkv_scan(self, zr, bm, km, pc, vtok):
        nc, ar = self.nc, self.arena
        ytok = ar.take("ytok", 2, 4, RW_WIDTH)
        causal = ar.take("causal", 2, 2 * P)
        levels = ar.take("levels", 2, 6, P)
        state = ar.take("state", 4, P)
        A = ar.take("A", 8, 4, P)
        X, XT, N, H = (ar.take(n, 8, P) for n in ("X", "XT", "N", "H"))
        btok = ar.take("btok", 4, RW_WIDTH)
        Dm, U = ar.take("Dm", 2, RW_WIDTH), ar.take("U", 2, RW_WIDTH)
        decay = ar.take("decay", 4, P)
        pairs = []
        for d in range(2):
            pairs.append((causal[:, d], self.table_src(f"causal{d}")))
            pairs.append((levels[:, d].rearrange("p a b -> p (a b)"), self.table_src(f"level{d}_0", f"level{d}_5")))
        self.load(pairs)
        ident, headones = self.tab("ident"), self.tab("headones")
        with nc.Block() as block:
            @block.vector
            def _(dve):
                nc.vector.memset(state, 0.0)

        order = ((0, 1, 2, 3), (1, 0, 3, 2))
        for s in range(4):
            tile = (order[0][s], order[1][s])
            tk = [slice(t * P, (t + 1) * P) for t in tile]
            made, masked = self.counted("pairs_made"), self.counted("pairs_masked")
            turned, moved = self.counted("bk_turned"), self.counted("bk_moved")
            with nc.Block() as block:
                @block.tensor
                def _(pe):
                    for i in range(8):
                        d, hd = i // 4, i % 4
                        f, a = hd // 2, (hd % 2) * HD
                        if i >= 4:
                            pe.wait_ge(masked.sem, masked.at(i - 3))
                        zr_h = zr[d][a:a + HD, f, :, tk[d]]
                        nc.tensor.matmul(self.bank[i % 4][:, 0:2 * P], bm[d][a:a + HD, f, tk[d]], zr_h, start=True, stop=True)
                        nc.tensor.matmul(self.bank[i % 4][:, 2 * P:4 * P], km[d][a:a + HD, f, tk[d]], zr_h, start=True, stop=True).then_inc(made.sem, 1)
                    for d in range(2):
                        for i, src in enumerate((bm[d], km[d])):
                            for f in range(2):
                                last = nc.tensor.transpose(self.bank[4 + 2 * d + i][:, f * P:(f + 1) * P], src[:, f, tk[d]], ident)
                            last.then_inc(turned.sem, 1)

                @block.vector
                def _(dve):
                    for i in range(8):
                        dve.wait_ge(made.sem, made.at(i + 1))
                        m = causal[:, i // 4].unsqueeze(1).to_broadcast([P, 2, 2 * P])
                        nc.vector.tensor_tensor(A[:, i].rearrange("p (a b) t -> p a (b t)", a=2),
                                                self.bank[i % 4].rearrange("p (a b) -> p a b", a=2), m, ALU.mult).then_inc(masked.sem, 1)

                @block.scalar
                def _(act):
                    for j in range(4):
                        act.wait_ge(turned.sem, turned.at(j + 1))
                        nc.scalar.activation(btok[:, j], self.bank[4 + j][:, 0:RW_WIDTH], ACT.Copy)
            made.advance(8)
            masked.advance(8)
            turned.advance(4)

            self.rwkv_solve(A, X, XT, N, H, levels)

            half = ((0, 1), (1, 0))
            dsum, dmoved, usum, umoved = (self.counted(n) for n in ("d_summed", "d_moved", "u_summed", "u_moved"))
            ysum, ymoved, ssum, smoved = (self.counted(n) for n in ("y_summed", "y_moved", "state_summed", "state_step"))
            dready = self.counted("decay_ready")
            with nc.Block() as block:
                @block.gpsimd
                def _(pool):
                    for c in range(2):
                        if c == 1:
                            pool.wait_ge(smoved.sem, smoved.at(2))
                        for d in range(2):
                            ch = 2 * tile[d] + half[d][c]
                            for f in range(2):
                                last = nc.gpsimd.tensor_scalar(decay[:, 2 * d + f], headones, pc[d][:, f, ch:ch + 1], None, ALU.mult)
                        last.then_inc(dready.sem, 1)

                @block.tensor
                def _(pe):
                    for c in range(2):
                        if c == 1:
                            pe.wait_ge(smoved.sem, smoved.at(2))
                        hf = [slice(half[d][c] * HD, half[d][c] * HD + HD) for d in range(2)]
                        for d in range(2):
                            for f in range(2):
                                nc.tensor.matmul(self.bank[d][:, f * P:(f + 1) * P], zr[d][:, f, 0, tk[d]], state[:, 2 * d + f], start=True, stop=False)
                                for hd in (2 * f, 2 * f + 1):
                                    hc = slice(hd * HD, (hd + 1) * HD)
                                    last = nc.tensor.matmul(self.bank[d][:, hc], A[hf[d], 4 * d + hd, 2], vtok[hf[d], tile[d], hc],
                                                            start=False, stop=hd % 2 == 1)
                            last.then_inc(dsum.sem, 1)
                        for d in range(2):
                            pe.wait_ge(dmoved.sem, dmoved.at(2 * c + d + 1))
                            for hd in range(4):
                                hc = slice(hd * HD, (hd + 1) * HD)
                                last = nc.tensor.matmul(self.bank[2 + d][:, hc], XT[hf[d], 4 * d + hd], Dm[hf[d], d, hc], start=True, stop=True)
                            last.then_inc(usum.sem, 1)
                        for d in range(2):
                            pe.wait_ge(umoved.sem, umoved.at(2 * c + d + 1))
                            for f in range(2):
                                fc = slice(f * P, (f + 1) * P)
                                nc.tensor.matmul(self.bank[6 + d][:, fc], btok[hf[d], 2 * d, fc], U[hf[d], d, fc], start=True, stop=False)
                                last = nc.tensor.matmul(self.bank[6 + d][:, fc], btok[hf[d], 2 * d + 1, fc], vtok[hf[d], tile[d], fc], start=False, stop=True)
                            last.then_inc(ssum.sem, 1)
                        for d in range(2):
                            if c == 1:
                                pe.wait_ge(ymoved.sem, ymoved.at(d + 1))
                            for f in range(2):
                                nc.tensor.matmul(self.bank[4 + d][:, f * P:(f + 1) * P], zr[d][:, f, 1, tk[d]], state[:, 2 * d + f], start=True, stop=False)
                                for hd in (2 * f, 2 * f + 1):
                                    hc = slice(hd * HD, (hd + 1) * HD)
                                    nc.tensor.matmul(self.bank[4 + d][:, hc], A[hf[d], 4 * d + hd, 1], U[hf[d], d, hc], start=False, stop=False)
                                    last = nc.tensor.matmul(self.bank[4 + d][:, hc], A[hf[d], 4 * d + hd, 3], vtok[hf[d], tile[d], hc],
                                                            start=False, stop=hd % 2 == 1)
                            last.then_inc(ysum.sem, 1)

                @block.vector
                def _(dve):
                    for c in range(2):
                        hf = [slice(half[d][c] * HD, half[d][c] * HD + HD) for d in range(2)]
                        for d in range(2):
                            dve.wait_ge(dsum.sem, dsum.at(2 * c + d + 1))
                            nc.vector.tensor_copy(Dm[hf[d], d], self.bank[d][hf[d], 0:RW_WIDTH]).then_inc(dmoved.sem, 1)
                        for d in range(2):
                            dve.wait_ge(usum.sem, usum.at(2 * c + d + 1))
                            nc.vector.tensor_copy(U[hf[d], d], self.bank[2 + d][hf[d], 0:RW_WIDTH]).then_inc(umoved.sem, 1)
                        dve.wait_ge(ssum.sem, ssum.at(2 * c + 2))
                        dve.wait_ge(ysum.sem, ysum.at(2 * c + 2))
                        dve.wait_ge(dready.sem, dready.at(c + 1))
                        for d in range(2):
                            sd = state[:, 2 * d:2 * d + 2].rearrange("p a b -> p (a b)")
                            last = nc.vector.tensor_tensor(sd, self.bank[6 + d][:, 0:RW_WIDTH], sd, ALU.add)
                        last.then_inc(smoved.sem, 1)
                        dve.wait_ge(smoved.sem, smoved.at(2 * c + 1))
                        nc.vector.tensor_tensor(state, state, decay, ALU.mult).then_inc(smoved.sem, 1)

                @block.scalar
                def _(act):
                    for c in range(2):
                        for d in range(2):
                            act.wait_ge(ysum.sem, ysum.at(2 * c + d + 1))
                            hf = slice(half[d][c] * HD, half[d][c] * HD + HD)
                            nc.scalar.activation(ytok[hf, d, tile[d]], self.bank[4 + d][hf, 0:RW_WIDTH], ACT.Copy).then_inc(ymoved.sem, 1)
            for q in (dsum, dmoved, usum, umoved, ysum, ymoved, ssum, smoved):
                q.advance(4)
            dready.advance(2)
        ar.free("causal", "levels", "state", "A", "X", "XT", "N", "H", "btok", "Dm", "U", "decay")
        return ytok

    def rwkv_solve(self, A, X, XT, N, H, levels):
        nc = self.nc
        ident = self.tab("ident")
        picked, turned, hs, hm, xs, xm = (self.counted(n) for n in ("level_picked", "x_turned", "h_summed", "h_moved", "x_summed", "x_added"))
        idb = ident.unsqueeze(1).to_broadcast([P, 4, P])
        bank4 = lambda b: self.bank[b].rearrange("p (h t) -> p h t", h=4)
        with nc.Block() as block:
            @block.vector
            def _(dve):
                for lv in range(6):
                    for d in range(2):
                        g = slice(4 * d, 4 * d + 4)
                        m = levels[:, d, lv].unsqueeze(1).to_broadcast([P, 4, P])
                        if lv >= 2:
                            dve.wait_ge(hs.sem, hs.at(2 * (lv - 2) + d + 1))
                        nc.vector.tensor_tensor(N[:, g], A[:, g, 0], m, ALU.mult).then_inc(picked.sem, 1)
                        if lv == 0:
                            dve.wait_ge(picked.sem, picked.at(d + 1))
                            nc.vector.tensor_tensor(XT[:, g], N[:, g], idb, ALU.add).then_inc(xm.sem, 1)
                            dve.wait_ge(turned.sem, turned.at(d + 1))
                            nc.vector.tensor_tensor(X[:, g], bank4(d), idb, ALU.add).then_inc(xm.sem, 1)
                        else:
                            i = 2 * (lv - 1) + d
                            dve.wait_ge(xs.sem, xs.at(i + 1))
                            nc.vector.tensor_tensor(XT[:, g], bank4(2 + d), XT[:, g], ALU.add).then_inc(xm.sem, 1)
                            nc.vector.tensor_tensor(X[:, g], bank4(4 + d), X[:, g], ALU.add).then_inc(xm.sem, 1)

            @block.scalar
            def _(act):
                for i in range(10):
                    d = i % 2
                    act.wait_ge(hs.sem, hs.at(i + 1))
                    nc.scalar.activation(H[:, 4 * d:4 * d + 4], bank4(6 + d), ACT.Copy).then_inc(hm.sem, 1)

            @block.tensor
            def _(pe):
                for d in range(2):
                    pe.wait_ge(picked.sem, picked.at(d + 1))
                    for hd in range(4):
                        last = nc.tensor.transpose(self.bank[d][:, hd * P:(hd + 1) * P], N[:, 4 * d + hd], ident)
                    last.then_inc(turned.sem, 1)
                for lv in range(1, 6):
                    for d in range(2):
                        i = 2 * (lv - 1) + d
                        pe.wait_ge(picked.sem, picked.at(2 * lv + d + 1))
                        pe.wait_ge(xm.sem, xm.at(2 * (i + 1)))
                        for hd in range(4):
                            last = nc.tensor.matmul(self.bank[6 + d][:, hd * P:(hd + 1) * P], N[:, 4 * d + hd], X[:, 4 * d + hd], start=True, stop=True)
                        last.then_inc(hs.sem, 1)
                        pe.wait_ge(hm.sem, hm.at(i + 1))
                        for hd in range(4):
                            c, q = slice(hd * P, (hd + 1) * P), 4 * d + hd
                            nc.tensor.matmul(self.bank[2 + d][:, c], H[:, q], XT[:, q], start=True, stop=True)
                            last = nc.tensor.matmul(self.bank[4 + d][:, c], XT[:, q], H[:, q], start=True, stop=True)
                        last.then_inc(xs.sem, 1)
        picked.advance(12)
        turned.advance(2)
        hs.advance(10)
        hm.advance(10)
        xs.advance(10)
        xm.advance(24)

    def rwkv_out(self, layer, y, gate):
        nc, ar = self.nc, self.arena
        yT, sq, o = ar.take("yT", 2, T2), ar.take("sq", 2, T2), ar.take("o", 2, T2)
        turned, st, summed = self.counted("y_turned"), self.counted("headnorm_step"), self.counted("headnorm_summed")
        rooted = self.counted("rooted")
        with nc.Block() as block:
            @block.tensor
            def _(pe):
                for f in range(2):
                    for t in range(4):
                        last = nc.tensor.transpose(self.bank[f][:, t * P:(t + 1) * P], y[:, t, f * P:(f + 1) * P], self.tab("ident"))
                last.then_inc(turned.sem, 1)
                for n, (src, want) in enumerate(((yT, 1), (sq, 3))):
                    pe.wait_ge(st.sem, st.at(want))
                    for f in range(2):
                        last = nc.tensor.matmul(self.bank[2 + 2 * n + f], self.tab("headones"), src[:, f], start=True, stop=True)
                    last.then_inc(summed.sem, 1)

            @block.vector
            def _(dve):
                n = 0

                def after(last):
                    nonlocal n
                    last.then_inc(st.sem, 1)
                    n += 1
                    dve.wait_ge(st.sem, st.at(n))

                dve.wait_ge(turned.sem, turned.at(1))
                for f in range(2):
                    last = nc.vector.tensor_copy(yT[:, f], self.bank[f])
                after(last)
                dve.wait_ge(summed.sem, summed.at(1))
                for f in range(2):
                    last = nc.vector.scalar_tensor_tensor(o[:, f], self.bank[2 + f], -1.0 / HD, yT[:, f], ALU.mult, ALU.add)
                after(last)
                after(nc.vector.tensor_tensor(sq, o, o, ALU.mult))
                dve.wait_ge(summed.sem, summed.at(2))
                for f in range(2):
                    last = nc.vector.tensor_scalar(yT[:, f], self.bank[4 + f], 1.0 / HD, RW_GN_EPS, ALU.mult, ALU.add)
                after(last)
                after(nc.vector.reciprocal(yT, yT))
                dve.wait_ge(rooted.sem, rooted.at(1))
                for f in range(2):
                    last = nc.vector.scalar_tensor_tensor(o[:, f], o[:, f], self.col(f"gn_g{layer}", f), yT[:, f], ALU.mult, ALU.mult)
                after(last)
                for f in range(2):
                    last = nc.vector.scalar_tensor_tensor(o[:, f], o[:, f], self.col(f"gn_b{layer}", f), gate[:, f], ALU.add, ALU.mult)
                after(last)
                nc.vector.tensor_tensor(self.hT[:, 4:6, :], self.hT[:, 4:6, :], o, ALU.add)
                st.n = n

            @block.scalar
            def _(act):
                act.wait_ge(st.sem, st.at(5))
                nc.scalar.activation(yT, yT, ACT.Sqrt).then_inc(rooted.sem, 1)
        rooted.advance(1)
        turned.advance(1)
        summed.advance(2)
        st.advance(st.n)
        ar.free("yT", "sq", "o")

    def conformer(self, cv, layer, seqs):
        nc, ar = self.nc, self.arena
        pad = CV_LEN // 2
        ns, t0 = len(seqs), seqs[0].start
        tokens = slice(t0, T2)
        nt = T2 - t0
        h, o, tmp = ar.take("cvpad", 2, ns, SEQ + 2 * pad), ar.take("o", 2, nt), ar.take("tmp", 2, nt)
        opened, st, summed, done = self.counted("cv_opened"), self.counted("cv_step"), self.counted("cv_summed"), self.counted("cv_out")
        rooted = self.counted("rooted")
        per_seq = lambda x: x.rearrange("p (s t) -> p s t", s=ns)
        with nc.Block() as block:
            @block.scalar
            def _(act):
                nc.scalar.activation(cv[:, 2:4, tokens], cv[:, 2:4, tokens], ACT.Sigmoid).then_inc(opened.sem, 1)
                act.wait_ge(st.sem, st.at(6 + CV_LEN))
                nc.scalar.activation(tmp[:, 0], tmp[:, 0], ACT.Sqrt).then_inc(rooted.sem, 1)
                act.wait_ge(done.sem, done.at(1))
                for f in range(2):
                    nc.scalar.activation(self.hT[:, 6 + f, tokens], o[:, f], ACT.Silu, bias=self.col(f"ln_b{layer}", f))

            @block.tensor
            def _(pe):
                for n in range(2):
                    pe.wait_ge(st.sem, st.at(2 + CV_LEN if n == 0 else 4 + CV_LEN))
                    src = o if n == 0 else tmp
                    for f in range(2):
                        last = nc.tensor.matmul(self.bank[n][:, 0:nt], self.tab("ones"), src[:, f], start=f == 0, stop=f == 1)
                    last.then_inc(summed.sem, 1)

            @block.vector
            def _(dve):
                n = 0

                def after(last):
                    nonlocal n
                    last.then_inc(st.sem, 1)
                    n += 1
                    dve.wait_ge(st.sem, st.at(n))

                after(nc.vector.memset(h, 0.0))
                dve.wait_ge(opened.sem, opened.at(1))
                for f in range(2):
                    last = nc.vector.tensor_tensor(h[:, f, :, pad:pad + SEQ], per_seq(cv[:, f, tokens]), per_seq(cv[:, 2 + f, tokens]), ALU.mult)
                after(last)
                for tap in range(CV_LEN):
                    for f in range(2):
                        w, src = self.col(f"dw_w{layer}_{tap}", f), h[:, f, :, tap:tap + SEQ]
                        if tap == 0:
                            last = nc.vector.tensor_scalar(per_seq(o[:, f]), src, w, self.col(f"dw_b{layer}", f), ALU.mult, ALU.add)
                        else:
                            last = nc.vector.scalar_tensor_tensor(per_seq(o[:, f]), src, w, per_seq(o[:, f]), ALU.mult, ALU.add)
                    after(last)
                dve.wait_ge(summed.sem, summed.at(1))
                for f in range(2):
                    last = nc.vector.scalar_tensor_tensor(o[:, f], self.bank[0][:, 0:nt], -1.0 / RW_WIDTH, o[:, f], ALU.mult, ALU.add)
                after(last)
                after(nc.vector.tensor_tensor(tmp, o, o, ALU.mult))
                dve.wait_ge(summed.sem, summed.at(2))
                after(nc.vector.tensor_scalar(tmp[:, 0], self.bank[1][:, 0:nt], 1.0 / RW_WIDTH, LN_EPS, ALU.mult, ALU.add))
                after(nc.vector.reciprocal(tmp[:, 0], tmp[:, 0]))
                dve.wait_ge(rooted.sem, rooted.at(1))
                for f in range(2):
                    last = nc.vector.scalar_tensor_tensor(o[:, f], o[:, f], self.col(f"ln_g{layer}", f), tmp[:, 0], ALU.mult, ALU.mult)
                last.then_inc(done.sem, 1)
                st.n = n
        rooted.advance(1)
        opened.advance(1)
        summed.advance(2)
        done.advance(1)
        st.advance(st.n)
        ar.free("cvpad", "o", "tmp")

    def block_two(self):
        nc, ins, ar = self.nc, self.ins, self.arena
        xT, hT = self.xT, self.hT
        at = lambda a: (lambda j: a[:, j])
        self.cs = self.smallcols(2 * DT).rearrange("p (k c) -> p k c", c=2)
        self.keep = self.smallcols(20)
        step = self.counted("keep_step")
        with nc.Block() as block:
            @block.scalar
            def _(act):
                nc.scalar.activation(self.cs[:, :, 0], self.cols("c", DT), ACT.Silu)
                nc.scalar.activation(self.cs[:, :, 1], self.cols("c_ctx", DT), ACT.Silu)

            @block.vector
            def _(dve):
                for l in range(2):
                    last = nc.vector.tensor_tensor(self.keep[:, 10 * l:10 * l + 10], self.cols(f"mu_prev{l}", 10), self.cols(f"mu_next{l}", 10), ALU.add)
                last.then_inc(step.sem, 1)
                dve.wait_ge(step.sem, step.at(1))
                nc.vector.tensor_scalar(self.keep, self.keep, -1.0, 1.0, ALU.mult, ALU.add)
        step.advance(1)

        for layer in range(2):
            ctx = layer == 0
            seqs = [CTX, LAT] if ctx else [LAT]
            own = BOTH if ctx else LAT
            mod, gain = self.modulation(layer)
            self.modulated_norm(mod, gain, 0, True)

            qk = ar.take("qk", 8, T2)
            v = ar.take("v", 4, 512)
            cv = ar.take("cv", 4, T2)
            rwpad = ar.take("rwpad", 10, 2, SEQ + 2)
            with nc.Block() as block:
                @block.vector
                def _(dve):
                    for edge in (0, SEQ + 1):
                        nc.vector.memset(rwpad[:, :, :, edge:edge + 1], 0.0)

            def copy_own(dst, j0, scale, n=4):
                def fn(dve, banks):
                    for j in range(n):
                        last = nc.vector.tensor_scalar(dst[:, j0 + j, own], banks[j][:, 0:own.stop - own.start], scale, None, ALU.mult)
                    return last
                return fn

            def v_evac(dve, banks):
                for t in range(4):
                    last = nc.vector.tensor_copy(v[:, t], banks[t])
                return last

            def rw_evac(j0, n):
                def fn(dve, banks):
                    for j in range(n):
                        last = nc.vector.tensor_copy(rwpad[:, j0 + j, :, 1:SEQ + 1], banks[j].rearrange("p (s t) -> p s t", s=2))
                    return last
                return fn

            F = lambda rows, act, evac, **kw: dict(kind="F", rows=rows, act=act, evac=evac, **kw)
            h_all = lambda k: hT[:, k, :]
            h_own = lambda k: hT[:, k, own]
            self.linear([F(D, h_own, {"vector": copy_own(qk, 0, HD ** -0.5)}), F(D, h_all, {"vector": self.copy_f(at(qk), 4)}),
                         dict(kind="T", rows=D, act=h_all, evac={"vector": v_evac}),
                         F(D, h_all, {"vector": rw_evac(0, 4)}), F(D, h_all, {"vector": rw_evac(4, 4)}),
                         F(D, h_all, {"vector": rw_evac(8, 2)}), F(D, h_own, {"vector": copy_own(cv, 0, 1.0)})])

            bias = ar.take("bias", 8, 2, SEQ)
            window = ar.take("window", SEQ)
            flip = ar.take("flip", P)
            loads = [(window, self.table_src("window")), (flip, self.table_src("flip_rows"))]
            for hd in range(8):
                for row in range(4):
                    off = ((layer * 8 + hd) * 15 + 7 - row) * 127
                    loads.append((bias[(row % 2) * GRID_W:(row % 2 + 1) * GRID_W, hd, row // 2].rearrange("p (r c) -> p r c", r=4),
                                  bass.AP(self.rpb_dram, off, [[1, GRID_W], [127, 4], [1, GRID_W]])))
            self.load(loads)
            with nc.Block() as block:
                @block.vector
                def _(dve):
                    for hd in range(8):
                        nc.vector.tensor_tensor(bias[:, hd], bias[:, hd], window.unsqueeze(1).to_broadcast([P, 2, SEQ]), ALU.add)
            units = []
            for hd in range(8):
                a, ft = (hd % 2) * HD, hd // 2
                for i in range(2):
                    tq = slice(SEQ + i * P, SEQ + (i + 1) * P)
                    units.append(dict(q=[qk[a:a + HD, ft, tq]], k=[qk[a:a + HD, 4 + ft, :]],
                                      v=[v[:, t, hd * HD:(hd + 1) * HD] for t in range(4)],
                                      out=[hT[a:a + HD, ft, tq]], out_part=a, bias=bias[:, hd, i], count=None))
            if ctx:
                for hd in range(8):
                    a, ft = (hd % 2) * HD, hd // 2
                    for i in range(2):
                        tq = slice(i * P, (i + 1) * P)
                        units.append(dict(q=[qk[a:a + HD, ft, tq]], k=[qk[a:a + HD, 4 + ft, CTX]],
                                          v=[v[:, t, hd * HD:(hd + 1) * HD] for t in range(2)],
                                          out=[hT[a:a + HD, ft, tq]], out_part=a, bias=None, count=None))
            self.attention(units, flip)
            ar.free("qk", "v", "bias", "window", "flip")
            self.conformer(cv, layer, seqs)
            ar.free("cv")
            self.rwkv(rwpad, layer)

            def gates(n):
                out = [(LAT, lambda t: mod[:, (3 * n + 2) * DT + t, 0:1])]
                if ctx:
                    out.insert(0, (CTX, lambda t: mod[:, (3 * n + 2) * DT + t, 1:2]))
                return out

            self.linear([F(D, h_own, {"vector": self.residual(g, own, gates(0))}) for g in range(2)])
            self.modulated_norm(mod, gain, 1, ctx)
            if layer == 0:
                hidden = ar.take("hidden", D_FF // P, T2)
                groups = []
                for j0 in range(0, D_FF // P, 4):
                    n = min(4, D_FF // P - j0)

                    def silu_evac(act, banks, j0=j0, n=n):
                        for j in range(n):
                            last = nc.scalar.activation(hidden[:, j0 + j], banks[j], ACT.Silu)
                        return last

                    def up_evac(dve, banks, j0=j0, n=n):
                        for j in range(n):
                            last = nc.vector.tensor_tensor(hidden[:, j0 + j], banks[j], hidden[:, j0 + j], ALU.mult)
                        return last

                    groups.append(F(D, h_all, {"scalar": silu_evac}))
                    groups.append(F(D, h_all, {"vector": up_evac}, vector_after_scalar=True))
                self.linear(groups)
                self.linear([F(D_FF, at(hidden), {"vector": self.residual(g, BOTH, gates(1))}) for g in range(2)])
                ar.free("hidden")
            else:
                self.experts(gates(1)[0][1])

        self.rmsnorm(lambda k: xT[:, k, LAT], DT, SEQ, [(slice(0, SEQ), lambda k: xT[:, k, LAT], lambda k: self.col("final_g", k), None)])

    def experts(self, gate_column):
        nc, ar, ins = self.nc, self.arena, self.ins
        hT, xT = self.hT, self.xT
        E = N_EXPERTS
        router = ar.take("router", DT, E)
        gt = ar.take("gt", 2, 64)
        idx = ar.take("idx", 2, 8).bitcast(U32)
        spread = ar.take("spread", 2, E, P)
        gbc = ar.take("gbc", E, SEQ)
        acc = ar.take("acc", DT, SEQ)
        hid = ar.take("hid", D_FFE // P, SEQ)
        tmp = ar.take("tmp", 4, SEQ)
        self.load([(router, ins["moe_router_2"][0].rearrange("(k p) e -> p k e", p=P))])
        logits, st, ed, turned = self.counted("logits_ready"), self.counted("route_step"), self.counted("route_exp"), self.counted("gates_turned")
        with nc.Block() as block:
            @block.tensor
            def _(pe):
                for t in range(2):
                    for k in range(DT):
                        last = nc.tensor.matmul(self.bank[t][:, 0:E], hT[:, k, SEQ + t * P:SEQ + (t + 1) * P], router[:, k, :], start=k == 0, stop=k == DT - 1)
                    last.then_inc(logits.sem, 1)
                pe.wait_ge(st.sem, st.at(10))
                for b in range(4):
                    for i in range(4):
                        e, t = 2 * b + i // 2, i % 2
                        last = nc.tensor.transpose(self.bank[4 + b][:, i * P:(i + 1) * P], spread[:, t, e], self.tab("ident"))
                    last.then_inc(turned.sem, 1)

            @block.scalar
            def _(act):
                act.wait_ge(st.sem, st.at(4))
                for t in range(2):
                    last = nc.scalar.activation(gt[:, t, 24:25], gt[:, t, 32:33], ACT.Exp)
                last.then_inc(ed.sem, 1)

            @block.vector
            def _(dve):
                n = 0

                def after(last):
                    nonlocal n
                    last.then_inc(st.sem, 1)
                    n += 1
                    dve.wait_ge(st.sem, st.at(n))

                both = (0, 1)
                dve.wait_ge(logits.sem, logits.at(2))
                for t in both:
                    last = nc.vector.tensor_copy(gt[:, t, 0:8], self.bank[t][:, 0:E])
                after(last)
                for t in both:
                    last = nc.vector.max(gt[:, t, 8:16], gt[:, t, 0:8])
                after(last)
                for t in both:
                    last = nc.vector.max_index(idx[:, t], gt[:, t, 8:16], gt[:, t, 0:8])
                after(last)
                for t in both:
                    nc.vector.tensor_copy(gt[:, t, 16:24], idx[:, t])
                    last = nc.vector.tensor_tensor(gt[:, t, 32:33], gt[:, t, 9:10], gt[:, t, 8:9], ALU.subtract)
                after(last)
                dve.wait_ge(ed.sem, ed.at(1))
                for t in both:
                    last = nc.vector.tensor_scalar(gt[:, t, 33:34], gt[:, t, 24:25], 1.0, None, ALU.add)
                after(last)
                for t in both:
                    last = nc.vector.reciprocal(gt[:, t, 25:26], gt[:, t, 33:34])
                after(last)
                for t in both:
                    last = nc.vector.tensor_tensor(gt[:, t, 26:27], gt[:, t, 24:25], gt[:, t, 25:26], ALU.mult)
                after(last)
                for t in both:
                    for i in range(2):
                        last = nc.vector.tensor_scalar(gt[:, t, 40 + 8 * i:48 + 8 * i], self.tab("iota8"), gt[:, t, 16 + i:17 + i],
                                                       gt[:, t, 25 + i:26 + i], ALU.is_equal, ALU.mult)
                after(last)
                for t in both:
                    last = nc.vector.tensor_tensor(gt[:, t, 56:64], gt[:, t, 40:48], gt[:, t, 48:56], ALU.add)
                after(last)
                for t in both:
                    last = nc.vector.tensor_copy(spread[:, t], gt[:, t, 56:64].unsqueeze(2).to_broadcast([P, E, P]))
                after(last)
                nc.vector.memset(acc, 0.0)
                for b in range(4):
                    dve.wait_ge(turned.sem, turned.at(b + 1))
                    nc.vector.tensor_copy(gbc[:, 2 * b:2 * b + 2, :].rearrange("p e t -> p (e t)"), self.bank[4 + b])
                st.n = n
        for q, k in ((logits, 2), (st, st.n), (ed, 1), (turned, 4)):
            q.advance(k)

        n_col, n_in, n_down = D_FFE // GROUP, D // (TILE_K * P), D_FFE // (TILE_K * P)
        per = 2 * n_col * n_in + 2 * n_down
        assert per % WEIGHT_SLOTS == 0
        turns = per // WEIGHT_SLOTS
        t0 = self.taken
        used = self.tile_used
        wg, wu, wd = (ins[f"moe_w_{n}_2"][0] for n in ("gate", "up", "down"))

        def source(j, e):
            if j < 2 * n_col * n_in:
                g, half = divmod(j, n_in)
                w = wg if g % 2 == 0 else wu
                c, r = (g // 2) * GROUP, half * TILE_K * P
            else:
                g, half = divmod(j - 2 * n_col * n_in, n_down)
                w, c, r = wd, g * GROUP, half * TILE_K * P
            rows = w.rearrange("e r c -> (e r) c")
            return rows[bass.ds(e * w.shape[1] + r, TILE_K * P), c:c + GROUP].rearrange("(k p) n -> p k n", p=P)

        sig_s, sig_v, step = self.counted("banks_emptied_by_scalar"), self.counted("banks_emptied_by_vector"), self.counted("weighted")
        with nc.Block() as block:
            @block.sync
            def _(sync):
                def load_tile(j, x):
                    src = source(j, x)
                    sync.wait_ge(used.sem, x * per + (t0 + j - WEIGHT_SLOTS + 1))
                    sync.dma_start(self.ring[:, (t0 + j) % WEIGHT_SLOTS], src).then_inc(self.slot_full[(t0 + j) % WEIGHT_SLOTS].sem, 16)

                for j in range(WEIGHT_SLOTS):
                    load_tile(j, 0)
                with sync.Fori(2, N_EXPERTS + 1) as e:
                    for j in range(WEIGHT_SLOTS, per):
                        load_tile(j, e - 2)
                    for j in range(WEIGHT_SLOTS):
                        load_tile(j, e - 1)
                for j in range(WEIGHT_SLOTS, per):
                    load_tile(j, N_EXPERTS - 1)

            @block.tensor
            def _(pe):
                with pe.Fori(0, N_EXPERTS) as e:
                    j = 0

                    def tile_ready():
                        pe.wait_ge(self.slot_full[(t0 + j) % WEIGHT_SLOTS].sem, e * (16 * turns) + 16 * ((t0 + j) // WEIGHT_SLOTS + 1))
                        return self.ring[:, (t0 + j) % WEIGHT_SLOTS]

                    for g in range(2 * n_col + 2):
                        b = 4 * (g % 2)
                        if g < 2:
                            pe.wait_ge(sig_v.sem, e * (n_col + 2) + sig_v.at(g - 1))
                        elif g % 2 == 0:
                            pe.wait_ge(sig_s.sem, e * n_col + sig_s.at(g // 2))
                        else:
                            pe.wait_ge(sig_v.sem, e * (n_col + 2) + sig_v.at(g // 2))
                        down = g >= 2 * n_col
                        if down:
                            pe.wait_ge(sig_v.sem, e * (n_col + 2) + sig_v.at(n_col))
                        tiles = n_down if down else n_in
                        for i in range(tiles):
                            w = tile_ready()
                            for c in range(4):
                                for k in range(TILE_K):
                                    kk = i * TILE_K + k
                                    x = hid[:, kk] if down else hT[:, kk, LAT]
                                    last = nc.tensor.matmul(self.bank[b + c][:, 0:SEQ], w[:, k, c * P:(c + 1) * P], x,
                                                            start=kk == 0, stop=kk == tiles * TILE_K - 1)
                            last.then_inc(used.sem, 1)
                            j += 1

            @block.scalar
            def _(act):
                with act.Fori(0, N_EXPERTS) as e:
                    for g in range(n_col):
                        act.wait_ge(used.sem, e * per + used.at(2 * g * n_in + n_in))
                        for c in range(4):
                            last = nc.scalar.activation(hid[:, 4 * g + c], self.bank[c][:, 0:SEQ], ACT.Silu)
                        last.then_inc(sig_s.sem, 1)

            @block.vector
            def _(dve):
                with dve.Fori(0, N_EXPERTS) as e:
                    for g in range(n_col):
                        dve.wait_ge(used.sem, e * per + used.at(2 * (g + 1) * n_in))
                        dve.wait_ge(sig_s.sem, e * n_col + sig_s.at(g + 1))
                        for c in range(4):
                            last = nc.vector.tensor_tensor(hid[:, 4 * g + c], self.bank[4 + c][:, 0:SEQ], hid[:, 4 * g + c], ALU.mult)
                        last.then_inc(sig_v.sem, 1)
                    for g in range(2):
                        dve.wait_ge(used.sem, e * per + used.at(2 * n_col * n_in + (g + 1) * n_down))
                        for c in range(4):
                            last = nc.vector.tensor_tensor(tmp[:, c], self.bank[4 * g + c][:, 0:SEQ], gbc[:, bass.ds(e, 1), :].rearrange("p o t -> p (o t)"), ALU.mult)
                        last.then_inc(step.sem, 1)
                        dve.wait_ge(step.sem, e * 2 + step.at(g + 1))
                        nc.vector.tensor_tensor(acc[:, 4 * g:4 * g + 4], acc[:, 4 * g:4 * g + 4], tmp, ALU.add).then_inc(sig_v.sem, 1)
                        dve.wait_ge(sig_v.sem, e * (n_col + 2) + sig_v.at(n_col + g + 1))
                for t in range(DT):
                    nc.vector.scalar_tensor_tensor(xT[:, t, LAT], acc[:, t], gate_column(t), xT[:, t, LAT], ALU.mult, ALU.add)
        ar.free("router", "gt", "idx", "spread", "gbc", "acc", "hid", "tmp")

    def store(self):
        nc = self.nc
        rows = self.arena.take("rows", 2, D)
        turned, moved, stored = self.counted("rows_turned"), self.counted("turned_moved"), self.counted("output_stored")
        with nc.Block() as block:
            @block.tensor
            def _(pe):
                for t in range(2):
                    for k in range(DT):
                        last = nc.tensor.transpose(self.bank[2 * t + k // 4][:, (k % 4) * P:(k % 4 + 1) * P], self.xT[:, k, SEQ + t * P:SEQ + (t + 1) * P], self.tab("ident"))
                    last.then_inc(turned.sem, 1)

            @block.vector
            def _(dve):
                for t in range(2):
                    dve.wait_ge(turned.sem, turned.at(t + 1))
                    for b in range(2):
                        last = nc.vector.tensor_copy(rows[:, t, 512 * b:512 * b + 512], self.bank[2 * t + b])
                    last.then_inc(moved.sem, 1)

            @block.sync
            def _(sync):
                for t in range(2):
                    sync.wait_ge(moved.sem, moved.at(t + 1))
                    sync.dma_start(self.out[0, t * P:(t + 1) * P, :], rows[:, t]).then_inc(stored.sem, 16)
                sync.wait_ge(stored.sem, stored.at(32))


def vector_rows(ins):
    rows = lambda ap: ap.rearrange("(r p) -> r p", p=P)
    out = [("g_mix", rows(ins["g_mix"][0])), ("g_out_dil", rows(ins["g_out_dil"][0])), ("g_out_moba", rows(ins["g_out_moba"][0])),
           ("g_cross", rows(ins["g_cross"][0])), ("g_mem", rows(ins["g_mem"][0])), ("g_ffn", rows(ins["g_ffn"][0])),
           ("g_final", rows(ins["g_final"])), ("conv_b", rows(ins["conv_b"][0]))]
    out += [(f"conv_w{t}", rows(ins["conv_w"][0, t])) for t in range(3)]
    out += [("c", rows(ins["c_2"][0])), ("c_ctx", rows(ins["c_ctx_2"]))]
    for l in range(2):
        out += [(f"norm1_g{l}", rows(ins["norm1_g_2"][l])), (f"norm2_g{l}", rows(ins["norm2_g_2"][l])), (f"mod_b{l}", rows(ins["mod_b_2"][l])),
                (f"mu_prev{l}", rows(ins["rw_mu_prev_2"][l])), (f"mu_next{l}", rows(ins["rw_mu_next_2"][l])),
                (f"w0{l}", ins["rw_w0_2"][l].rearrange("d (r p) -> (d r) p", p=P)), (f"a0{l}", ins["rw_a0_2"][l].rearrange("d (r p) -> (d r) p", p=P)),
                (f"k_k{l}", rows(ins["rw_k_k_2"][l])), (f"k_a{l}", rows(ins["rw_k_a_2"][l])),
                (f"r_k{l}", ins["rw_r_k_2"][l].rearrange("(a b) k -> a (b k)", b=2)),
                (f"gn_g{l}", rows(ins["rw_gn_g_2"][l])), (f"gn_b{l}", rows(ins["rw_gn_b_2"][l])),
                (f"dw_w{l}", ins["cv_dw_w_2"][l].rearrange("t (r p) -> (t r) p", p=P)),
                (f"dw_b{l}", rows(ins["cv_dw_b_2"][l])), (f"ln_g{l}", rows(ins["cv_ln_g_2"][l])), (f"ln_b{l}", rows(ins["cv_ln_b_2"][l]))]
    return out + [("final_g", rows(ins["final_g_2"]))]


def build(nc, ins, out):
    ctx = ExitStack()
    with ctx:
        pr = Program(nc, ins, out, ctx)
        pr.plan(ins["w_in"][0], 0, D, 0, 6 * 512)
        pr.plan(ins["w_out"][0], 0, D, 0, D)
        pr.plan(ins["w_q_mem"][0], 0, D, 0, D)
        pr.plan(ins["w_kv_mem"][0], 0, D, 0, 2 * D)
        pr.plan(ins["w_o_mem"][0], 0, D, 0, D)
        for c in range(0, D_FF, GROUP):
            for w in ("w_gate", "w_up"):
                pr.plan(ins[w][0], 0, D, c, min(GROUP, D_FF - c))
        pr.plan(ins["w_down"][0], 0, D_FF, 0, D)
        for layer in range(2):
            pr.plan(ins["mod_w_2"][layer], 0, D, 0, 6 * D)
            w = ins["w_in_2"][layer]
            for c, n in ((0, 512), (512, 512), (1024, 512), (1536, 1280), (2816, 512)):
                pr.plan(w, 0, D, c, n)
            pr.plan(ins["w_out_2"][layer], 0, D, 0, D)
            if layer == 0:
                for c in range(0, D_FF, GROUP):
                    for n in ("ffn_w_gate_2", "ffn_w_up_2"):
                        pr.plan(ins[n][0], 0, D, c, min(GROUP, D_FF - c))
                pr.plan(ins["ffn_w_down_2"][0], 0, D_FF, 0, D)
        pr.load_vectors(vector_rows(ins))
        for l in range(2):
            for tap in range(CV_LEN):
                pr.vec[f"dw_w{l}_{tap}"] = pr.vec[f"dw_w{l}"] + 2 * tap
        pr.bias_lines()
        pr.block_one()
        pr.block_two()
        pr.store()


_NAMES = ["x", "mem", "w_in", "g_mix", "g_out_dil", "g_out_moba", "w_out", "rel_bias", "g_cross", "g_mem", "w_q_mem",
          "w_kv_mem", "w_o_mem", "g_ffn", "w_gate", "w_up", "conv_w", "conv_b", "w_down", "g_final", "c_2", "ctx_2",
          "c_ctx_2", "norm1_g_2", "norm2_g_2", "mod_w_2", "mod_b_2", "w_in_2", "w_out_2", "na_rpb_2", "rw_mu_prev_2",
          "rw_mu_next_2", "rw_w0_2", "rw_w2_2", "rw_a0_2", "rw_a2_2", "rw_g2_2", "rw_k_k_2", "rw_k_a_2", "rw_r_k_2",
          "rw_gn_g_2", "rw_gn_b_2", "cv_dw_w_2", "cv_dw_b_2", "cv_ln_g_2", "cv_ln_b_2", "ffn_w_gate_2", "ffn_w_up_2",
          "ffn_w_down_2", "moe_router_2", "moe_w_gate_2", "moe_w_up_2", "moe_w_down_2", "final_g_2"]


def kernel(**inputs):
    import concourse.bacc as bacc
    from concourse.bass_utils import run_bass_kernel_spmd

    nc = bacc.Bacc("TRN2", target_bir_lowering=False, num_devices=1)
    arrays, ins = {}, {}
    for name in _NAMES:
        a = np.ascontiguousarray(inputs[name])
        arrays[f"in_{name}"] = a
        ins[name] = nc.dram_tensor(f"in_{name}", a.shape, mybir.dt.from_np(a.dtype), kind="ExternalInput").ap()
    tables = np.concatenate(list(_TABLES.values()), axis=1)
    arrays["shape_tables"] = tables
    ins["tables"] = nc.dram_tensor("shape_tables", tables.shape, F32, kind="ExternalInput").ap()
    out = nc.dram_tensor("out", (1, SEQ, D), F32, kind="ExternalOutput").ap()
    build(nc, ins, out)
    return run_bass_kernel_spmd(nc, [arrays], core_ids=[0]).results[0]["out"]
```

```python
import math
from contextlib import ExitStack

import numpy as np

import concourse.bass as bass
from concourse import mybir

F32 = mybir.dt.float32
U32 = mybir.dt.uint32
ALU = mybir.AluOpType
ACT = mybir.ActivationFunctionType
AX_X = mybir.AxisListType.X

P = 128
SEQ = 256
T2 = 2 * SEQ
D = 1024
DT = D // P
HD = 64
N_BUCKETS = 32
MAX_DISTANCE = 2048
D_FF = 2816
D_FFE = 3584
N_EXPERTS = 8
MAX_ITEMS = N_EXPERTS + (2 * SEQ) // (P + 1)
RW_WIDTH = 256
CV_LEN = 31
GRID_W = 64
NEG = -1e30
EPS = 1e-6
LN_EPS = 1e-5
RW_GN_EPS = 64e-5
CHUNK = 64
DECAY_SCALE = math.exp(-0.5)
WEIGHT_SLOTS = 7
GROUP = 512
TILE_K = 4
CTX = slice(0, SEQ)
LAT = slice(SEQ, T2)
BOTH = slice(0, T2)


def rel_bucket_of(n):
    half = N_BUCKETS // 2
    n = np.maximum(n, 0)
    nf = np.maximum(n, 1).astype(np.float32)
    large = half + (np.log(nf / np.float32(half)) / np.float32(math.log(MAX_DISTANCE / half))
                    * np.float32(N_BUCKETS - half)).astype(np.int32)
    return np.where(n < half, n, np.minimum(large, N_BUCKETS - 1))


def multiplicity(d):
    return (d >= 0) * ((d <= 128).astype(int) + (d % 4 == 0) + (d % 16 == 0))


def shape_tables():
    p = np.arange(P)
    tab = {}
    tab["ident"] = np.eye(P)
    tab["ones"] = np.ones((P, P))
    tab["headones"] = (p[:, None] // HD == p[None, :] // HD).astype(float)
    j = np.arange(T2)
    dist = SEQ - 1 - j
    for name, seen in (("bucket_dil", multiplicity(dist) > 0), ("bucket_moba", dist >= 0)):
        m = np.zeros((P, T2))
        m[rel_bucket_of(dist), j] = seen
        m[N_BUCKETS, :] = ~seen
        tab[name] = m
    t = np.arange(SEQ).reshape(2, P).T[:, :, None]
    tab["count"] = multiplicity(t - np.arange(SEQ)[None, None, :]).reshape(P, 2 * SEQ)
    qc, kc = p % GRID_W, np.arange(SEQ) % GRID_W
    tab["flip"] = np.eye(P)[::-1]
    tab["flip_rows"] = np.kron(np.eye(2), np.eye(GRID_W)[::-1])
    qc = GRID_W - 1 - qc
    start = np.clip(qc - 8, 0, GRID_W - 16)[:, None]
    tab["window"] = np.where((kc >= start) & (kc < start + 16), 0.0, NEG)
    row, col = p[:, None], p[None, :]
    same = row // CHUNK == col // CHUNK
    for d in range(2):
        before = (row < col) if d == 0 else (row > col)
        tab[f"causal{d}"] = np.stack([before & same, (before | (row == col)) & same], 1).reshape(P, 2 * P)
        for lv in range(6):
            s = 1 << lv
            tab[f"level{d}_{lv}"] = before & (row // (2 * s) == col // (2 * s)) & (row // s != col // s)
    tab["restart"] = np.broadcast_to(j % CHUNK != 0, (P, T2))
    tab["earlier"] = row < col
    tab["iota128"] = np.broadcast_to(p, (P, P))
    tab["items"] = np.broadcast_to(np.repeat(np.arange(MAX_ITEMS), N_EXPERTS), (P, MAX_ITEMS * N_EXPERTS))
    tab["iota8"] = np.broadcast_to(np.arange(8), (P, 8))
    return {k: np.asarray(v, np.float32) for k, v in tab.items()}


_TABLES = shape_tables()
RESIDENT = ("ident", "ones", "headones", "iota8")
_TABLES = {**{k: _TABLES[k] for k in RESIDENT}, **_TABLES}
RESIDENT_COLS = sum(_TABLES[k].shape[1] for k in RESIDENT)
TABLE_AT = {}
_at = 0
for _name, _v in _TABLES.items():
    TABLE_AT[_name] = (_at, _v.shape[1])
    _at += _v.shape[1]
TABLE_COLS = _at


class Counted:

    def __init__(self, sem):
        self.sem, self.base = sem, 0

    def at(self, n):
        return self.base + n

    def advance(self, n):
        self.base += n


class Arena:

    def __init__(self, tensor, size):
        self.tensor, self.size, self.used = tensor, size, {}

    def take(self, name, *dims):
        n = 1
        for d in dims:
            n *= d
        at = 0
        for a, k in sorted(self.used.values()):
            if at + n <= a:
                break
            at = max(at, a + k)
        assert at + n <= self.size, (name, n, at, self.size, self.used)
        assert name not in self.used, name
        self.used[name] = (at, n)
        view = self.tensor[:, at:at + n]
        if len(dims) == 2:
            view = view.rearrange("p (a b) -> p a b", a=dims[0])
        if len(dims) == 3:
            view = view.rearrange("p (a b c) -> p a b c", a=dims[0], b=dims[1])
        if len(dims) == 4:
            view = view.rearrange("p (a b c d) -> p a b c d", a=dims[0], b=dims[1], c=dims[2])
        return view

    def free(self, *names):
        for n in names:
            del self.used[n]


class SideProduct:

    HALF = DT // 2

    def __init__(self, pr, layer, first, n):
        self.pr, self.first, self.n, self.layer = pr, first, n, layer
        self.w = pr.ins["mod_w_2"][layer]
        self.tiles = pr.arena.take("mod_tiles", 2, self.HALF, GROUP)
        self.sums = pr.arena.take("mod_sums", n, 2, GROUP)
        self.full = [pr.counted(f"mod_tile{i}_full") for i in range(2)]
        self.step = pr.counted("mod_sum_step")
        self.products = pr.counted("mod_columns_made")
        self.home = {}

    def load(self, pool):
        for i in range(2 * self.n):
            if i >= 2:
                pool.wait_ge(self.step.sem, self.step.at(self.HALF * (i - 1)))
            c, r = (self.first + i // 2) * GROUP, (i % 2) * self.HALF * P
            src = self.w[r:r + self.HALF * P, c:c + GROUP].rearrange("(k p) n -> p k n", p=P)
            pool.dma_start(self.tiles[:, i % 2], src).then_inc(self.full[i % 2].sem, 16)

    def sum_rows(self, dve, s):
        nc, cs = self.pr.nc, self.pr.cs
        for half in range(2):
            f = self.full[half]
            dve.wait_ge(f.sem, f.at(16 * (s + 1)))
            for k in range(self.HALF):
                row = half * self.HALF + k
                if row:
                    dve.wait_ge(self.step.sem, self.step.at(DT * s + row))
                for c in range(2):
                    scale, acc, w = cs[:, row, c:c + 1], self.sums[:, s, c], self.tiles[:, half, k]
                    if row == 0:
                        last = nc.vector.tensor_scalar(acc, w, scale, None, ALU.mult)
                    else:
                        last = nc.vector.scalar_tensor_tensor(acc, w, scale, acc, ALU.mult, ALU.add)
                last.then_inc(self.step.sem, 1)

    def columns(self, pe, s, banks, first_bank):
        nc = self.pr.nc
        pe.wait_ge(self.step.sem, self.step.at(DT * (s + 1)))
        for j in range(4):
            for c in range(2):
                last = nc.tensor.matmul(banks[j][:, 256 + 2 * s + c:257 + 2 * s + c], self.sums[:, s, c, j * P:(j + 1) * P],
                                        self.pr.tab("ones")[:, 0:1], start=True, stop=True)
        last.then_inc(self.products.sem, 1)
        self.home[s] = first_bank

    def finish(self, dve):
        nc, pr = self.pr.nc, self.pr
        dve.wait_ge(self.products.sem, self.products.at(self.n))
        for s in range(self.n):
            for j in range(4):
                tile = 4 * (self.first + s) + j
                nc.vector.tensor_scalar(pr.mod[self.layer][:, tile, :], pr.bank[self.home[s] + j][:, 256 + 2 * s:258 + 2 * s],
                                        pr.col(f"mod_b{self.layer}", tile), None, ALU.add)

    def close(self):
        for f in self.full:
            f.advance(16 * self.n)
        self.step.advance(DT * self.n)
        self.products.advance(self.n)
        self.pr.arena.free("mod_tiles", "mod_sums")


class Program:
    def __init__(self, nc, ins, out, ctx):
        self.nc, self.ins, self.out, self.ctx = nc, ins, out, ctx
        self.counts = {}
        self.ring = self.sb("weight_ring", [P, WEIGHT_SLOTS, TILE_K, GROUP])
        self.xT = self.sb("residual", [P, DT, T2])
        self.hT = self.sb("normed", [P, DT, T2])
        self.table = self.sb("tables", [P, RESIDENT_COLS])
        self.small = self.sb("small", [P, 1024])
        size = nc.sbuf_bytes_remaining // 4 - 64
        self.arena = Arena(self.sb("work", [P, size]), size)
        self.bank = [ctx.enter_context(nc.psum_tensor(f"bank{i}", [P, 512], F32))[:, :] for i in range(8)]
        self.slot_full = [self.counted(f"slot{i}_full") for i in range(WEIGHT_SLOTS)]
        self.tile_used = self.counted("tile_used")
        self.weights = []
        self.issued = 0
        self.taken = 0
        self.small_at = 0
        self.vec = {}

    def sb(self, name, shape, dt=F32):
        return self.ctx.enter_context(self.nc.sbuf_tensor(name, shape, dt))

    def counted(self, name):
        if name not in self.counts:
            self.counts[name] = Counted(self.ctx.enter_context(self.nc.semaphore(name)))
        return self.counts[name]

    def tab(self, name):
        a, n = TABLE_AT[name]
        return self.table[:, a:a + n]

    def table_src(self, first, last=None):
        a = TABLE_AT[first][0]
        b, n = TABLE_AT[last or first]
        return self.ins["tables"][:, a:b + n]

    def smallcols(self, n):
        a = self.small_at
        self.small_at += n
        assert self.small_at <= 1024
        return self.small[:, a:a + n]

    def plan(self, w, row0, rows, col0, cols):
        for c in range(col0, col0 + cols, GROUP):
            width = min(GROUP, col0 + cols - c)
            for r in range(row0, row0 + rows, TILE_K * P):
                nk = min(TILE_K, (row0 + rows - r) // P)
                self.weights.append((w[r:r + nk * P, c:c + width].rearrange("(k p) n -> p k n", p=P), nk, width))

    def load_weights(self, sync, used):
        used_total = self.taken + used
        while self.issued < min(len(self.weights), used_total + WEIGHT_SLOTS):
            i = self.issued
            src, nk, width = self.weights[i]
            if i >= WEIGHT_SLOTS:
                sync.wait_ge(self.tile_used.sem, i - WEIGHT_SLOTS + 1)
            s = self.slot_full[i % WEIGHT_SLOTS]
            sync.dma_start(self.ring[:, i % WEIGHT_SLOTS, 0:nk, 0:width], src).then_inc(s.sem, 16)
            self.issued += 1

    def wait_tile(self, pe, i):
        pe.wait_ge(self.slot_full[i % WEIGHT_SLOTS].sem, 16 * (i // WEIGHT_SLOTS + 1))

    def linear(self, groups, loads=(), side=None):
        nc = self.nc
        used = self.tile_used
        evs = {n: self.counted(f"banks_emptied_by_{n}") for n in ("vector", "scalar")}
        first = self.taken
        start, t = [], first
        for g in groups:
            start.append(t)
            t += -(-g["rows"] // (TILE_K * P))
        end = t
        ends = start[1:] + [end]

        landed = self.counted("next_loads_landed")
        sums = [[] for _ in groups]
        for s in range(side.n if side else 0):
            sums[s * len(groups) // side.n].append(s)

        def banks(gi):
            return self.bank[4 * (gi % 2):4 * (gi % 2) + 4]

        def emptied(gi, name):
            return sum(1 for g in groups[:gi + 1] if name in g["evac"])

        with nc.Block() as block:
            @block.sync
            def _(sync):
                self.load_weights(sync, end - first)

            @block.tensor
            def _(pe):
                for gi, g in enumerate(groups):
                    if gi >= 2:
                        for name in groups[gi - 2]["evac"]:
                            pe.wait_ge(evs[name].sem, evs[name].at(emptied(gi - 2, name)))
                        for s in sums[gi - 2]:
                            side.columns(pe, s, banks(gi), 4 * (gi % 2))
                    total = g["rows"] // P
                    k0 = 0
                    for i in range(start[gi], ends[gi]):
                        _, nk, width = self.weights[i]
                        self.wait_tile(pe, i)
                        w = self.ring[:, i % WEIGHT_SLOTS]
                        if g["kind"] == "F":
                            for j in range(width // P):
                                for k in range(nk):
                                    a = g["act"](k0 + k)
                                    last = nc.tensor.matmul(banks(gi)[j][:, 0:a.shape[-1]], w[:, k, j * P:(j + 1) * P], a,
                                                            start=k0 + k == 0, stop=k0 + k == total - 1)
                        else:
                            n_tok = g["act"](0).shape[-1] // P
                            for j in range(n_tok):
                                for k in range(nk):
                                    a = g["act"](k0 + k)[:, j * P:(j + 1) * P]
                                    last = nc.tensor.matmul(banks(gi)[j][:, 0:width], a, w[:, k, 0:width],
                                                            start=k0 + k == 0, stop=k0 + k == total - 1)
                        last.then_inc(used.sem, 1)
                        k0 += nk
                if side:
                    for gi in range(max(0, len(groups) - 2), len(groups)):
                        if sums[gi]:
                            for name in groups[gi]["evac"]:
                                pe.wait_ge(evs[name].sem, evs[name].at(emptied(gi, name)))
                        for s in sums[gi]:
                            side.columns(pe, s, banks(gi), 4 * (gi % 2))

            @block.gpsimd
            def _(pool):
                if side:
                    side.load(pool)

            @block.vector
            def _(dve):
                for gi, g in enumerate(groups):
                    for s in sums[gi]:
                        side.sum_rows(dve, s)
                    if "vector" in g["evac"]:
                        dve.wait_ge(used.sem, used.at(ends[gi] - first))
                        if g.get("vector_after_scalar"):
                            dve.wait_ge(evs["scalar"].sem, evs["scalar"].at(emptied(gi, "scalar")))
                        g["evac"]["vector"](dve, banks(gi)).then_inc(evs["vector"].sem, 1)
                if side:
                    side.finish(dve)

            @block.scalar
            def _(act):
                for dst, src in loads:
                    act.dma_start(dst, src).then_inc(landed.sem, 16)
                for gi, g in enumerate(groups):
                    if "scalar" in g["evac"]:
                        act.wait_ge(used.sem, used.at(ends[gi] - first))
                        if g.get("scalar_after_vector"):
                            act.wait_ge(evs["vector"].sem, evs["vector"].at(emptied(gi - 1, "vector")))
                        g["evac"]["scalar"](act, banks(gi)).then_inc(evs["scalar"].sem, 1)
                if loads:
                    act.wait_ge(landed.sem, landed.at(16 * len(loads)))

        landed.advance(16 * len(loads))
        if side:
            side.close()
        n = len(groups)
        for name, s in evs.items():
            s.advance(emptied(n - 1, name))
        used.advance(end - first)
        self.taken = end

    def transpose_in(self, jobs):
        nc = self.nc
        landed, turned, moved = self.counted("rows_landed"), self.counted("rows_turned"), self.counted("turned_moved")
        n = len(jobs)
        rows = self.arena.take("rows", n, 2, D)
        ident = self.tab("ident")
        with nc.Block() as block:
            @block.sync
            def _(sync):
                for i, (src, _) in enumerate(jobs):
                    sync.dma_start(rows[:, i], src.rearrange("(t p) d -> p t d", p=P)).then_inc(landed.sem, 16)
                self.load_weights(sync, 0)

            @block.tensor
            def _(pe):
                pe.wait_ge(landed.sem, landed.at(16 * n))
                for i in range(n):
                    for k in range(DT):
                        step = i * DT + k
                        if step >= 8:
                            pe.wait_ge(moved.sem, moved.at(step - 7))
                        for t in range(2):
                            last = nc.tensor.transpose(self.bank[step % 8][:, t * P:(t + 1) * P], rows[:, i, t, k * P:(k + 1) * P], ident)
                        last.then_inc(turned.sem, 1)

            @block.vector
            def _(dve):
                for i, (_, dst) in enumerate(jobs):
                    for k in range(DT):
                        step = i * DT + k
                        dve.wait_ge(turned.sem, turned.at(step + 1))
                        nc.vector.tensor_copy(dst[:, k, :], self.bank[step % 8][:, 0:SEQ]).then_inc(moved.sem, 1)
        landed.advance(16 * n)
        turned.advance(n * DT)
        moved.advance(n * DT)
        self.arena.free("rows")

    def rmsnorm(self, src, n_tiles, tokens, parts, eps=EPS):
        nc = self.nc
        squared, summed = self.counted("squared"), self.counted("squares_summed")
        chain, scaled, shifted = self.counted("mean_ready"), self.counted("scaled"), self.counted("shifted")
        rooted = self.counted("rooted")
        sq = self.arena.take("sq", 2, tokens)
        rstd = self.arena.take("rstd", tokens)
        n = len(parts) * n_tiles
        with nc.Block() as block:
            @block.scalar
            def _(act):
                for k in range(n_tiles):
                    if k >= 2:
                        act.wait_ge(summed.sem, summed.at(k - 1))
                    nc.scalar.activation(sq[:, k % 2], src(k), ACT.Square).then_inc(squared.sem, 1)
                act.wait_ge(chain.sem, chain.at(2))
                nc.scalar.activation(rstd, rstd, ACT.Sqrt).then_inc(rooted.sem, 1)
                i = 0
                for _, dst, _, shift in parts:
                    for k in range(n_tiles):
                        i += 1
                        if shift is not None:
                            act.wait_ge(scaled.sem, scaled.at(i))
                            nc.scalar.activation(dst(k), dst(k), ACT.Identity, bias=shift(k)).then_inc(shifted.sem, 1)

            @block.tensor
            def _(pe):
                for k in range(n_tiles):
                    pe.wait_ge(squared.sem, squared.at(k + 1))
                    nc.tensor.matmul(self.bank[0][:, 0:tokens], self.tab("ones"), sq[:, k % 2], start=k == 0,
                                     stop=k == n_tiles - 1).then_inc(summed.sem, 1)

            @block.vector
            def _(dve):
                dve.wait_ge(summed.sem, summed.at(n_tiles))
                nc.vector.tensor_scalar(rstd, self.bank[0][:, 0:tokens], 1.0 / (n_tiles * P), eps, ALU.mult, ALU.add).then_inc(chain.sem, 1)
                dve.wait_ge(chain.sem, chain.at(1))
                dve.wait_ge(chain.sem, chain.at(1))
                nc.vector.reciprocal(rstd, rstd).then_inc(chain.sem, 1)
                dve.wait_ge(rooted.sem, rooted.at(1))
                for sl, dst, scale, _ in parts:
                    for k in range(n_tiles):
                        nc.vector.scalar_tensor_tensor(dst(k), src(k)[:, sl], scale(k), rstd[:, sl], ALU.mult, ALU.mult).then_inc(scaled.sem, 1)
        squared.advance(n_tiles)
        summed.advance(n_tiles)
        chain.advance(2)
        rooted.advance(1)
        scaled.advance(n)
        shifted.advance(sum(n_tiles for p in parts if p[3] is not None))
        self.arena.free("sq", "rstd")

    def attention(self, units, flip=None):
        nc = self.nc
        scored, probs_ready = self.counted("scores_ready"), self.counted("probs_ready")
        dstep, expd, turned, tmoved = self.counted("softmax_step"), self.counted("exp_done"), self.counted("probs_turned"), self.counted("probsT_ready")
        mixed, outm, biased = self.counted("values_mixed"), self.counted("mixed_moved"), self.counted("max_ready")
        keys = max(u["k"][0].shape[-1] for u in units)
        pr = self.arena.take("pr", 2, keys)
        pt = self.arena.take("pt", 2, keys)
        st = self.arena.take("st", 2, 4)
        ident = self.tab("ident")
        S = self.bank[0:3]
        PT = self.bank[3:6]
        O = self.bank[6:8]
        n = len(units)
        with nc.Block() as block:
            @block.tensor
            def _(pe):
                def scores(i):
                    u = units[i]
                    nk = u["k"][0].shape[-1]
                    if i >= 3:
                        pe.wait_ge(expd.sem, expd.at(i - 2))
                    for b in range(len(u["q"])):
                        last = nc.tensor.matmul(S[i % 3][:, 0:nk], u["q"][b], u["k"][b], start=b == 0,
                                                stop=u["bias"] is None and b == len(u["q"]) - 1)
                    if u["bias"] is not None:
                        last = nc.tensor.matmul(S[i % 3][:, nk - u["bias"].shape[-1]:nk], flip, u["bias"], start=False, stop=True)
                    last.then_inc(scored.sem, 1)

                scores(0)
                if n > 1:
                    scores(1)
                for i, u in enumerate(units):
                    if i + 2 < n:
                        scores(i + 2)
                    nkt = u["k"][0].shape[-1] // P
                    pe.wait_ge(probs_ready.sem, probs_ready.at(i + 1))
                    if i >= 3:
                        pe.wait_ge(tmoved.sem, tmoved.at(i - 2))
                    for t in range(nkt):
                        last = nc.tensor.transpose(PT[i % 3][:, t * P:(t + 1) * P], pr[:, i % 2, t * P:(t + 1) * P], ident)
                    last.then_inc(turned.sem, 1)
                    pe.wait_ge(tmoved.sem, tmoved.at(i + 1))
                    if i >= 2:
                        pe.wait_ge(outm.sem, outm.at(i - 1))
                    hw = u["v"][0].shape[-1]
                    a = u["out_part"]
                    for b in range(-(-hw // P)):
                        w = min(P, hw)
                        for t in range(nkt):
                            last = nc.tensor.matmul(O[i % 2][a:a + w, b * P:(b + 1) * P], u["v"][t][:, b * P:b * P + w],
                                                    pt[:, i % 2, t * P:(t + 1) * P], start=t == 0, stop=t == nkt - 1)
                    last.then_inc(mixed.sem, 1)

            @block.vector
            def _(dve):
                c = 0

                def head(i):
                    u = units[i]
                    nk = u["k"][0].shape[-1]
                    dve.wait_ge(scored.sem, scored.at(i + 1))
                    if i >= 2:
                        dve.wait_ge(probs_ready.sem, probs_ready.at(i - 1))
                    nc.vector.tensor_reduce(st[:, i % 2, 0:1], S[i % 3][:, 0:nk], AX_X, ALU.max, negate=True).then_inc(biased.sem, 1)

                def tail(i):
                    nonlocal c
                    u = units[i]
                    e = pr[:, i % 2, 0:u["k"][0].shape[-1]]
                    den = st[:, i % 2, 1:2]
                    dve.wait_ge(expd.sem, expd.at(i + 1))
                    if u["count"] is not None:
                        nc.vector.scalar_tensor_tensor(e, e, 1.0, u["count"], ALU.mult, ALU.mult, accum_out=den).then_inc(dstep.sem, 1)
                        c += 1
                        dve.wait_ge(dstep.sem, dstep.at(c))
                    nc.vector.reciprocal(st[:, i % 2, 3:4], den).then_inc(dstep.sem, 1)
                    c += 1
                    dve.wait_ge(dstep.sem, dstep.at(c))
                    nc.vector.tensor_scalar(e, e, st[:, i % 2, 3:4], None, ALU.mult).then_inc(probs_ready.sem, 1)

                def move_out(i):
                    u = units[i]
                    dve.wait_ge(mixed.sem, mixed.at(i + 1))
                    a, w = u["out_part"], min(P, u["v"][0].shape[-1])
                    for b, o in enumerate(u["out"]):
                        last = nc.vector.tensor_copy(o, O[i % 2][a:a + w, b * P:(b + 1) * P])
                    last.then_inc(outm.sem, 1)

                head(0)
                for i in range(n):
                    if i + 1 < n:
                        head(i + 1)
                    tail(i)
                    if i >= 1:
                        move_out(i - 1)
                move_out(n - 1)
                dstep.count = c

            @block.scalar
            def _(act):
                def exponent(i):
                    u = units[i]
                    nk = u["k"][0].shape[-1]
                    act.wait_ge(biased.sem, biased.at(i + 1))
                    if i >= 2:
                        act.wait_ge(turned.sem, turned.at(i - 1))
                    nc.scalar.activation(pr[:, i % 2, 0:nk], S[i % 3][:, 0:nk], ACT.Exp, bias=st[:, i % 2, 0:1],
                                         accum_out=st[:, i % 2, 1:2]).then_inc(expd.sem, 1)

                exponent(0)
                for i, u in enumerate(units):
                    if i + 1 < n:
                        exponent(i + 1)
                    nk = u["k"][0].shape[-1]
                    act.wait_ge(turned.sem, turned.at(i + 1))
                    if i >= 2:
                        act.wait_ge(mixed.sem, mixed.at(i - 1))
                    nc.scalar.activation(pt[:, i % 2, 0:nk], PT[i % 3][:, 0:nk], ACT.Copy).then_inc(tmoved.sem, 1)
        for s in (scored, probs_ready, expd, turned, tmoved, mixed, outm, biased):
            s.advance(n)
        dstep.advance(dstep.count)
        self.arena.free("pr", "pt", "st")

    def load(self, pairs):
        nc = self.nc
        landed = self.counted("loads_landed")
        with nc.Block() as block:
            @block.sync
            def _(sync):
                for dst, src in pairs:
                    sync.dma_start(dst, src).then_inc(landed.sem, 16)
                sync.wait_ge(landed.sem, landed.at(16 * len(pairs)))
        landed.advance(16 * len(pairs))

    def load_vectors(self, specs):
        nc = self.nc
        groups, at = 0, 0
        places = []
        for name, src in specs:
            n = src.shape[0]
            if at % P + n > P:
                at += P - at % P
            places.append((name, src, at, n))
            self.vec[name] = at
            at += n
        groups = -(-at // P)
        self.vectors = self.arena.take("vectors", groups * P)
        rows = self.arena.take("vector_rows", groups, P)
        cleared, landed, turned = self.counted("rows_cleared"), self.counted("loads_landed"), self.counted("rows_turned")
        with nc.Block() as block:
            @block.vector
            def _(dve):
                nc.vector.memset(rows, 0.0).then_inc(cleared.sem, 1)
                dve.wait_ge(turned.sem, turned.at(groups))
                for g in range(groups):
                    nc.vector.tensor_copy(self.vectors[:, g * P:(g + 1) * P], self.bank[g][:, 0:P])

            @block.scalar
            def _(act):
                act.dma_start(self.table[:, :], self.ins["tables"][:, 0:RESIDENT_COLS]).then_inc(landed.sem, 16)
                act.wait_ge(cleared.sem, cleared.at(1))
                for _, src, a, n in places:
                    act.dma_start(rows[a % P:a % P + n, a // P, :], src).then_inc(landed.sem, 16)

            @block.sync
            def _(sync):
                self.load_weights(sync, 0)

            @block.tensor
            def _(pe):
                pe.wait_ge(landed.sem, landed.at(16 * (len(places) + 1)))
                for g in range(groups):
                    nc.tensor.transpose(self.bank[g][:, 0:P], rows[:, g, :], self.tab("ident")).then_inc(turned.sem, 1)
        cleared.advance(1)
        landed.advance(16 * (len(places) + 1))
        turned.advance(groups)
        self.arena.free("vector_rows")

    def col(self, name, i=0):
        a = self.vec[name] + i
        return self.vectors[:, a:a + 1]

    def cols(self, name, n, i=0):
        a = self.vec[name] + i
        return self.vectors[:, a:a + n]

    def bias_lines(self):
        nc, ins = self.nc, self.ins
        self.bias_dram = nc.dram_tensor("bias_lines", (16, T2), F32, kind="Internal")
        self.rpb_dram = nc.dram_tensor("rpb_lines", (2 * 8 * 15, 127), F32, kind="Internal")
        tabs = self.arena.take("buckets", 2, T2)
        rb = self.arena.take("rel_bias", 16)
        lines = self.arena.take("lines", 2, T2)
        zero = self.arena.take("zero", 254)
        ready, landed, made, moved, stored = (self.counted(n) for n in
                                              ("rel_bias_cleared", "loads_landed", "lines_made", "lines_moved", "lines_stored"))
        n_load = 2
        with nc.Block() as block:
            @block.vector
            def _(dve):
                nc.vector.memset(rb[0:64, :], NEG).then_inc(ready.sem, 1)
                nc.vector.memset(zero, 0.0).then_inc(ready.sem, 1)
                dve.wait_ge(made.sem, made.at(2))
                nc.vector.tensor_copy(lines[0:8, 0], self.bank[0][0:8, :]).then_inc(moved.sem, 1)
                nc.vector.tensor_copy(lines[0:8, 1], self.bank[1][0:8, :]).then_inc(moved.sem, 1)

            @block.sync
            def _(sync):
                sync.dma_start(tabs.rearrange("p a b -> p (a b)"), self.table_src("bucket_dil", "bucket_moba")).then_inc(landed.sem, 16)
                sync.wait_ge(ready.sem, ready.at(2))
                sync.dma_start(rb[0:N_BUCKETS, :], ins["rel_bias"].rearrange("h b -> b h"), allow_slow_non_contiguous=True).then_inc(landed.sem, 16)
                n = 2 * 8 * 15
                sync.dma_start(bass.AP(self.rpb_dram, 0, [[254, n // 2], [1, 254]]), zero[0:n // 2, :]).then_inc(stored.sem, 16)
                sync.wait_ge(stored.sem, stored.at(16))
                sync.dma_start(self.rpb_dram.ap()[:, 48:79], ins["na_rpb_2"].rearrange("l h r c -> (l h r) c")).then_inc(stored.sem, 16)
                sync.wait_ge(moved.sem, moved.at(2))
                for i in range(2):
                    sync.dma_start(self.bias_dram.ap()[8 * i:8 * i + 8, :], lines[0:8, i]).then_inc(stored.sem, 16)
                sync.wait_ge(stored.sem, stored.at(64))

            @block.tensor
            def _(pe):
                pe.wait_ge(landed.sem, landed.at(32))
                for i in range(2):
                    nc.tensor.matmul(self.bank[i][0:8, :], rb[0:N_BUCKETS + 1, 8 * i:8 * i + 8], tabs[0:N_BUCKETS + 1, i],
                                     start=True, stop=True).then_inc(made.sem, 1)
        ready.advance(2)
        landed.advance(32)
        made.advance(2)
        moved.advance(2)
        stored.advance(64)
        self.arena.free("buckets", "rel_bias", "lines", "zero")

    def copy_f(self, dst, j0, sl=BOTH, scale=None):
        def fn(eng, banks):
            for j in range(4):
                if scale is None:
                    last = self.nc.vector.tensor_copy(dst(j0 + j), banks[j][:, sl])
                else:
                    last = self.nc.vector.tensor_scalar(dst(j0 + j), banks[j][:, sl], scale, None, ALU.mult)
            return last
        return fn

    def residual(self, group, sl, gates=None):
        def fn(eng, banks):
            for j in range(4):
                t = 4 * group + j
                if gates is None:
                    last = self.nc.vector.tensor_tensor(self.xT[:, t, sl], banks[j][:, 0:sl.stop - sl.start], self.xT[:, t, sl], ALU.add)
                else:
                    for tok, column in gates:
                        src = banks[j][:, tok.start - sl.start:tok.stop - sl.start]
                        last = self.nc.vector.scalar_tensor_tensor(self.xT[:, t, tok], src, column(t), self.xT[:, t, tok], ALU.mult, ALU.add)
            return last
        return fn

    def conditioning(self):
        nc = self.nc
        self.mod = [self.smallcols(96).rearrange("p (j c) -> p j c", c=2) for _ in range(2)]
        self.cs = self.smallcols(2 * DT).rearrange("p (k c) -> p k c", c=2)
        self.keep = self.smallcols(20)
        step = self.counted("keep_step")
        with nc.Block() as block:
            @block.scalar
            def _(act):
                nc.scalar.activation(self.cs[:, :, 0], self.cols("c", DT), ACT.Silu)
                nc.scalar.activation(self.cs[:, :, 1], self.cols("c_ctx", DT), ACT.Silu)

            @block.vector
            def _(dve):
                for l in range(2):
                    last = nc.vector.tensor_tensor(self.keep[:, 10 * l:10 * l + 10], self.cols(f"mu_prev{l}", 10), self.cols(f"mu_next{l}", 10), ALU.add)
                last.then_inc(step.sem, 1)
                dve.wait_ge(step.sem, step.at(1))
                nc.vector.tensor_scalar(self.keep, self.keep, -1.0, 1.0, ALU.mult, ALU.add)
        step.advance(1)

    def block_one(self):
        nc, ins, ar = self.nc, self.ins, self.arena
        xT, hT = self.xT, self.hT
        x = lambda k: xT[:, k, LAT]
        h = lambda k: hT[:, k, LAT]
        memT = ar.take("memT", DT, SEQ)
        self.transpose_in([(ins["x"][0], xT[:, :, LAT]), (ins["mem"][0], memT), (ins["ctx_2"][0], xT[:, :, CTX])])

        bias = ar.take("bias", 16, 2, SEQ)
        count = ar.take("count", 2, SEQ)
        loads = [(count.rearrange("p a b -> p (a b)"), self.table_src("count"))]
        for hd in range(16):
            loads.append((bias[:, hd], bass.AP(self.bias_dram, hd * T2, [[1, P], [P, 2], [1, SEQ]])))
        flip = ar.take("flip", P)
        loads.append((flip, self.table_src("flip")))

        self.rmsnorm(x, DT, SEQ, [(slice(0, SEQ), h, lambda k: self.col("g_mix", k), None)])
        qk = ar.take("qk", 16, SEQ)
        v = ar.take("v", 2, D)

        def v_evac(c):
            def fn(eng, banks):
                for t in range(2):
                    last = nc.vector.tensor_copy(v[:, t, c:c + 512], banks[t][:, :])
                return last
            return fn

        F = lambda rows, act, evac, **kw: dict(kind="F", rows=rows, act=act, evac=evac, **kw)
        T = lambda rows, act, evac, **kw: dict(kind="T", rows=rows, act=act, evac=evac, **kw)
        at = lambda a: (lambda j: a[:, j])
        half = slice(0, SEQ)
        self.linear([F(D, h, {"vector": self.copy_f(at(qk), 0, half, HD ** -0.5)}), F(D, h, {"vector": self.copy_f(at(qk), 4, half)}),
                     T(D, h, {"vector": v_evac(0)}),
                     F(D, h, {"vector": self.copy_f(at(qk), 8, half, HD ** -0.5)}), F(D, h, {"vector": self.copy_f(at(qk), 12, half)}),
                     T(D, h, {"vector": v_evac(512)})], loads=loads)
        y = ar.take("y", DT, SEQ)
        units = []
        for hd in range(16):
            g, a = 8 * (hd // 8), (hd % 2) * HD
            ft = (hd % 8) // 2
            for i in range(2):
                tq = slice(i * P, (i + 1) * P)
                units.append(dict(q=[qk[a:a + HD, g + ft, tq]], k=[qk[a:a + HD, g + 4 + ft, :]],
                                  v=[v[:, t, hd * HD:(hd + 1) * HD] for t in range(2)],
                                  out=[y[a:a + HD, hd // 2, tq]], out_part=a, bias=bias[:, hd, 1 - i],
                                  count=count[:, i] if hd < 8 else None))
        self.attention(units, flip)
        ar.free("bias", "count", "qk", "v", "flip")
        half_w = DT // 2
        for n, name in enumerate(("g_out_dil", "g_out_moba")):
            self.rmsnorm(lambda k: y[:, n * half_w + k], half_w, SEQ,
                         [(slice(0, SEQ), lambda k: h(n * half_w + k), lambda k: self.col(name, k), None)])
        ar.free("y")
        self.linear([F(D, h, {"vector": self.residual(g, LAT)}) for g in range(2)])

        self.rmsnorm(x, DT, SEQ, [(slice(0, SEQ), h, lambda k: self.col("g_cross", k), None)])
        self.rmsnorm(at(memT), DT, SEQ, [(slice(0, SEQ), at(memT), lambda k: self.col("g_mem", k), None)])
        q, km, v = ar.take("q", DT, SEQ), ar.take("km", DT, SEQ), ar.take("v", 2, D)
        self.linear([T(D, at(memT), {"vector": v_evac(0)}), T(D, at(memT), {"vector": v_evac(512)}),
                     F(D, h, {"vector": self.copy_f(at(q), 0, half, 256 ** -0.5)}), F(D, h, {"vector": self.copy_f(at(q), 4, half, 256 ** -0.5)}),
                     F(D, at(memT), {"vector": self.copy_f(at(km), 0, half)}), F(D, at(memT), {"vector": self.copy_f(at(km), 4, half)})],
                    side=SideProduct(self, 1, 0, 6))
        units = []
        for hd in range(4):
            for i in range(2):
                tq = slice(i * P, (i + 1) * P)
                units.append(dict(q=[q[:, 2 * hd + b, tq] for b in range(2)], k=[km[:, 2 * hd + b] for b in range(2)],
                                  v=[v[:, t, hd * 256:(hd + 1) * 256] for t in range(2)],
                                  out=[hT[:, 2 * hd + b, SEQ + i * P:SEQ + (i + 1) * P] for b in range(2)],
                                  out_part=0, bias=None, count=None))
        self.attention(units)
        ar.free("q", "km", "v", "memT")
        self.linear([F(D, h, {"vector": self.residual(g, LAT)}) for g in range(2)])

        self.rmsnorm(x, DT, SEQ, [(slice(0, SEQ), h, lambda k: self.col("g_ffn", k), None)])
        hidden = ar.take("hidden", D_FF // P, SEQ)
        conv = self.counted("conv_step")
        n_conv = 0

        def conv_evac(j0, n):
            def fn(dve, banks):
                nonlocal n_conv
                for tap in (2, 1, 0):
                    lag = 2 - tap
                    for j in range(n):
                        w = self.col(f"conv_w{tap}", j0 + j)
                        if lag == 0:
                            last = nc.vector.tensor_scalar(hidden[:, j0 + j], banks[j][:, 0:SEQ], w, None, ALU.mult)
                        else:
                            last = nc.vector.scalar_tensor_tensor(hidden[:, j0 + j, lag:SEQ], banks[j][:, 0:SEQ - lag], w,
                                                                  hidden[:, j0 + j, lag:SEQ], ALU.mult, ALU.add)
                    if lag < 2:
                        last.then_inc(conv.sem, 1)
                        n_conv += 1
                        dve.wait_ge(conv.sem, conv.at(n_conv))
                return last
            return fn

        def silu_evac(j0, n):
            def fn(act, banks):
                for j in range(j0, j0 + n):
                    last = nc.scalar.activation(hidden[:, j], hidden[:, j], ACT.Silu, bias=self.col("conv_b", j))
                return last
            return fn

        def up_evac(j0, n):
            def fn(dve, banks):
                for j in range(n):
                    last = nc.vector.tensor_tensor(hidden[:, j0 + j], banks[j][:, 0:SEQ], hidden[:, j0 + j], ALU.mult)
                return last
            return fn

        groups = []
        for j0 in range(0, D_FF // P, 4):
            n = min(4, D_FF // P - j0)
            groups.append(F(D, h, {"vector": conv_evac(j0, n)}))
            groups.append(F(D, h, {"scalar": silu_evac(j0, n), "vector": up_evac(j0, n)}, scalar_after_vector=True, vector_after_scalar=True))
        self.linear(groups, side=SideProduct(self, 0, 0, 12))
        conv.advance(n_conv)
        self.linear([F(D_FF, at(hidden), {"vector": self.residual(g, LAT)}) for g in range(2)], side=SideProduct(self, 1, 6, 6))
        ar.free("hidden")
        self.rmsnorm(x, DT, SEQ, [(slice(0, SEQ), x, lambda k: self.col("g_final", k), None)])

    def norm_gains(self, layer):
        nc, mod = self.nc, self.mod[layer]
        gain = self.smallcols(32).rearrange("p (n k c) -> p n k c", n=2, c=2)
        with nc.Block() as block:
            @block.vector
            def _(dve):
                for n in range(2):
                    for k in range(DT):
                        g = self.col(f"norm{n + 1}_g{layer}", k)
                        nc.vector.tensor_scalar(gain[:, n, k, :], mod[:, (3 * n + 1) * DT + k, :], 1.0, g, ALU.add, ALU.mult)
        return mod, gain

    def modulated_norm(self, mod, gain, n, ctx):
        parts, base, tokens = [], 0, T2
        if not ctx:
            base, tokens = SEQ, SEQ
        for c, sl in ((1, CTX), (0, LAT)):
            if c == 1 and not ctx:
                continue
            parts.append((slice(sl.start - base, sl.stop - base), lambda k, sl=sl: self.hT[:, k, sl],
                          lambda k, c=c: gain[:, n, k, c:c + 1], lambda k, c=c: mod[:, 3 * n * DT + k, c:c + 1]))
        self.rmsnorm(lambda k: self.xT[:, k, base:T2], DT, tokens, parts)

    def rwkv(self, rwpad, layer):
        nc, ar, ins = self.nc, self.arena, self.ins
        restart = ar.take("restart", T2)
        w2a2 = ar.take("w2a2", 2, RW_WIDTH)
        g2 = ar.take("g2", 2, RW_WIDTH)
        sh = ar.take("sh", 10, T2)
        self.load([(restart, self.table_src("restart")),
                   (w2a2[0:HD], ins["rw_w2_2"][layer].rearrange("d r n -> r d n")),
                   (w2a2[HD:P], ins["rw_a2_2"][layer].rearrange("d r n -> r d n")),
                   (g2, ins["rw_g2_2"][layer].rearrange("d r n -> r d n"))])
        kept, step = self.counted("shift_kept"), self.counted("shift_step")
        with nc.Block() as block:
            @block.scalar
            def _(act):
                for j in range(10):
                    nc.scalar.activation(sh[:, j, :].rearrange("p (s t) -> p s t", s=2), rwpad[:, j, :, 1:SEQ + 1], ACT.Copy,
                                         scale=self.keep[:, 10 * layer + j:10 * layer + j + 1]).then_inc(kept.sem, 1)

            @block.vector
            def _(dve):
                for j in range(10):
                    s = sh[:, j, :].rearrange("p (s t) -> p s t", s=2)
                    dve.wait_ge(kept.sem, kept.at(j + 1))
                    nc.vector.scalar_tensor_tensor(s, rwpad[:, j, :, 0:SEQ], self.col(f"mu_prev{layer}", j), s, ALU.mult, ALU.add).then_inc(step.sem, 1)
                    dve.wait_ge(step.sem, step.at(j + 1))
                    nc.vector.scalar_tensor_tensor(s, rwpad[:, j, :, 2:SEQ + 2], self.col(f"mu_next{layer}", j), s, ALU.mult, ALU.add)
        kept.advance(10)
        step.advance(10)
        ar.free("rwpad")
        r, k, v = sh[:, 0:2], sh[:, 2:4], sh[:, 4:6]

        kk = ar.take("kk", 2, T2)
        sq = ar.take("sq", 2, T2)
        vtok = ar.take("vtok", 4, RW_WIDTH)
        step, summed, turned = self.counted("kk_step"), self.counted("kk_summed"), self.counted("v_turned")
        rooted = self.counted("rooted")
        with nc.Block() as block:
            @block.vector
            def _(dve):
                for f in range(2):
                    nc.vector.tensor_scalar(kk[:, f], k[:, f], self.col(f"k_k{layer}", f), None, ALU.mult).then_inc(step.sem, 1)
                dve.wait_ge(step.sem, step.at(2))
                nc.vector.tensor_tensor(sq, kk, kk, ALU.mult).then_inc(step.sem, 1)
                dve.wait_ge(summed.sem, summed.at(2))
                for f in range(2):
                    nc.vector.tensor_scalar(sq[:, f], self.bank[f], 1e-12, None, ALU.add).then_inc(step.sem, 1)
                dve.wait_ge(step.sem, step.at(5))
                nc.vector.reciprocal(sq, sq).then_inc(step.sem, 1)
                dve.wait_ge(rooted.sem, rooted.at(1))
                nc.vector.tensor_tensor(kk, kk, sq, ALU.mult)

            @block.tensor
            def _(pe):
                for t in range(4):
                    for f in range(2):
                        last = nc.tensor.transpose(self.bank[4 + t][:, f * P:(f + 1) * P], v[:, f, t * P:(t + 1) * P], self.tab("ident"))
                    last.then_inc(turned.sem, 1)
                pe.wait_ge(step.sem, step.at(3))
                for f in range(2):
                    nc.tensor.matmul(self.bank[f], self.tab("headones"), sq[:, f], start=True, stop=True).then_inc(summed.sem, 1)

            @block.scalar
            def _(act):
                for t in range(4):
                    act.wait_ge(turned.sem, turned.at(t + 1))
                    nc.scalar.activation(vtok[:, t], self.bank[4 + t][:, 0:RW_WIDTH], ACT.Copy)
                act.wait_ge(step.sem, step.at(6))
                nc.scalar.activation(sq, sq, ACT.Sqrt).then_inc(rooted.sem, 1)
        step.advance(6)
        rooted.advance(1)
        summed.advance(2)
        turned.advance(4)
        ar.free("sq")

        zr, bm, km, gate, pc = [], [], [], [], []
        for d in range(2):
            self.rwkv_direction(layer, d, sh, kk, restart, w2a2, g2, zr, bm, km, gate, pc)
        ar.free("sh", "kk", "restart", "w2a2", "g2")
        ytok = self.rwkv_scan(zr, bm, km, pc, vtok)
        ar.free("zr0", "zr1", "bm0", "bm1", "km0", "km1", "pc0", "pc1", "vtok")
        for d in range(2):
            self.rwkv_out(layer, ytok[:, d], gate[d])
        ar.free("ytok", "gate0", "gate1")

    def rwkv_direction(self, layer, d, sh, kk, restart, w2a2, g2, zr, bm, km, gate, pc):
        nc, ar = self.nc, self.arena
        r, k, v = sh[:, 0:2], sh[:, 2:4], sh[:, 4:6]
        lo = 6 + 2 * d
        z = ar.take(f"zr{d}", 2, 2, T2)
        b_, k_, g_ = ar.take(f"bm{d}", 2, T2), ar.take(f"km{d}", 2, T2), ar.take(f"gate{d}", 2, T2)
        pc_ = ar.take(f"pc{d}", 2, T2 // CHUNK)
        zr.append(z), bm.append(b_), km.append(k_), gate.append(g_), pc.append(pc_)
        ld, L, a, kd = (ar.take(n, 2, T2) for n in ("ld", "L", "a", "kd"))
        e = ar.take("e", 2, T2)
        lora, ranked, opened = self.counted("lora_ready"), self.counted("lora_summed"), self.counted("lora_opened")
        st, ex, bs = self.counted("factor_step"), self.counted("factor_exp"), self.counted("bonus_summed")
        n_chunk = T2 // CHUNK
        per_chunk = lambda x: x.rearrange("p (c t) -> p c t", t=CHUNK)
        with nc.Block() as block:
            @block.scalar
            def _(act):
                nc.scalar.activation(sh[0:HD, lo], sh[0:HD, lo], ACT.Tanh).then_inc(lora.sem, 1)
                nc.scalar.activation(sh[:, lo + 1], sh[:, lo + 1], ACT.Sigmoid).then_inc(lora.sem, 1)
                act.wait_ge(ranked.sem, ranked.at(1))
                for f in range(2):
                    nc.scalar.activation(ld[:, f], self.bank[f], ACT.Sigmoid, bias=self.col(f"w0{layer}", 2 * d + f))
                    last = nc.scalar.activation(a[:, f], self.bank[2 + f], ACT.Sigmoid, bias=self.col(f"a0{layer}", 2 * d + f))
                last.then_inc(opened.sem, 1)
                for f in range(2):
                    nc.scalar.activation(g_[:, f], self.bank[4 + f], ACT.Copy)
                act.wait_ge(st.sem, st.at(6))
                nc.scalar.activation(e, L, ACT.Exp).then_inc(ex.sem, 1)
                nc.scalar.activation(ld, ld, ACT.Exp).then_inc(ex.sem, 1)
                act.wait_ge(st.sem, st.at(7))
                nc.scalar.activation(e, L, ACT.Exp, scale=-1.0).then_inc(ex.sem, 1)

            @block.tensor
            def _(pe):
                pe.wait_ge(lora.sem, lora.at(2))
                for f in range(2):
                    c = slice(f * P, (f + 1) * P)
                    nc.tensor.matmul(self.bank[f], w2a2[0:HD, d, c], sh[0:HD, lo], start=True, stop=True)
                    nc.tensor.matmul(self.bank[2 + f], w2a2[HD:P, d, c], sh[HD:P, lo], start=True, stop=True)
                    last = nc.tensor.matmul(self.bank[4 + f], g2[:, d, c], sh[:, lo + 1], start=True, stop=True)
                last.then_inc(ranked.sem, 1)
                pe.wait_ge(st.sem, st.at(11))
                for f in range(2):
                    last = nc.tensor.matmul(self.bank[6 + f], self.tab("headones"), a[:, f], start=True, stop=True)
                last.then_inc(bs.sem, 1)

            @block.vector
            def _(dve):
                n = 0

                def after(last):
                    nonlocal n
                    last.then_inc(st.sem, 1)
                    n += 1
                    dve.wait_ge(st.sem, st.at(n))

                dve.wait_ge(opened.sem, opened.at(1))
                after(nc.vector.tensor_scalar(ld, ld, -DECAY_SCALE, None, ALU.mult))
                for f in range(2):
                    last = nc.vector.tensor_tensor_scan(L[:, f], restart, ld[:, f], 0.0, ALU.mult, ALU.add)
                after(last)
                for f in range(2):
                    total = per_chunk(L[:, f])[:, :, CHUNK - 1:CHUNK]
                    last = nc.vector.tensor_copy(pc_[:, f, :], total[:, :, 0])
                after(last)
                if d == 1:
                    for f in range(2):
                        last = nc.vector.tensor_tensor(per_chunk(L[:, f]), pc_[:, f, :].unsqueeze(2).to_broadcast([P, n_chunk, CHUNK]),
                                                       per_chunk(L[:, f]), ALU.subtract)
                after(last if d == 1 else nc.vector.tensor_copy(e[:, 0, 0:1], L[:, 0, 0:1]))
                if d == 1:
                    after(nc.vector.tensor_tensor(L, L, ld, ALU.add))
                else:
                    after(nc.vector.tensor_copy(e[:, 0, 0:1], L[:, 0, 0:1]))
                after(nc.vector.tensor_tensor(ld, L, ld, ALU.subtract))
                for f in range(2):
                    last = nc.vector.tensor_scalar(kd[:, f], a[:, f], -1.0, self.col(f"k_a{layer}", f), ALU.add, ALU.mult)
                dve.wait_ge(ex.sem, ex.at(2))
                nc.vector.tensor_tensor(z[:, :, 1], r, e, ALU.mult)
                after(nc.vector.scalar_tensor_tensor(z[:, :, 0], kk, -1.0, ld, ALU.mult, ALU.mult))
                after(nc.vector.scalar_tensor_tensor(kd, kd, 1.0, k, ALU.add, ALU.mult))
                after(nc.vector.tensor_tensor(b_, kk, a, ALU.mult))
                dve.wait_ge(ex.sem, ex.at(3))
                nc.vector.tensor_tensor(b_, b_, e, ALU.mult)
                after(nc.vector.tensor_tensor(k_, kd, e, ALU.mult))
                for f in range(2):
                    last = nc.vector.scalar_tensor_tensor(a[:, f], r[:, f], self.col(f"r_k{layer}", f), kd[:, f], ALU.mult, ALU.mult)
                after(last)
                dve.wait_ge(bs.sem, bs.at(1))
                for f in range(2):
                    last = nc.vector.tensor_tensor(ld[:, f], self.bank[6 + f], v[:, f], ALU.mult)
                after(last)
                out = self.hT[:, 4:6, :]
                if d == 0:
                    nc.vector.tensor_tensor(out, ld, g_, ALU.mult)
                else:
                    after(nc.vector.tensor_tensor(ld, ld, g_, ALU.mult))
                    nc.vector.tensor_tensor(out, out, ld, ALU.add)
                st.n = n
        lora.advance(2)
        for s in (ranked, opened, bs):
            s.advance(1)
        ex.advance(3)
        st.advance(st.n)
        with nc.Block() as block:
            @block.scalar
            def _(act):
                nc.scalar.activation(pc_, pc_, ACT.Exp)
        ar.free("ld", "L", "a", "kd", "e")

    def rwkv_scan(self, zr, bm, km, pc, vtok):
        nc, ar = self.nc, self.arena
        ytok = ar.take("ytok", 2, 4, RW_WIDTH)
        causal = ar.take("causal", 2, 2 * P)
        levels = ar.take("levels", 2, 6, P)
        state = ar.take("state", 4, P)
        A = ar.take("A", 8, 4, P)
        X, XT, N, H = (ar.take(n, 8, P) for n in ("X", "XT", "N", "H"))
        btok = ar.take("btok", 4, RW_WIDTH)
        Dm, U = ar.take("Dm", 2, RW_WIDTH), ar.take("U", 2, RW_WIDTH)
        W = ar.take("W", 2, RW_WIDTH)
        decay = ar.take("decay", 4, P)
        pairs = []
        for d in range(2):
            pairs.append((causal[:, d], self.table_src(f"causal{d}")))
            pairs.append((levels[:, d].rearrange("p a b -> p (a b)"), self.table_src(f"level{d}_0", f"level{d}_5")))
        self.load(pairs)
        ident, headones = self.tab("ident"), self.tab("headones")
        with nc.Block() as block:
            @block.vector
            def _(dve):
                nc.vector.memset(state, 0.0)

        order = ((0, 1, 2, 3), (1, 0, 3, 2))
        for s in range(4):
            tile = (order[0][s], order[1][s])
            tk = [slice(t * P, (t + 1) * P) for t in tile]
            made, masked = self.counted("pairs_made"), self.counted("pairs_masked")
            turned, wsum = self.counted("bk_turned"), self.counted("w_summed")
            with nc.Block() as block:
                @block.tensor
                def _(pe):
                    for i in range(8):
                        d, hd = i // 4, i % 4
                        f, a = hd // 2, (hd % 2) * HD
                        if i >= 4:
                            pe.wait_ge(masked.sem, masked.at(i - 3))
                        zr_h = zr[d][a:a + HD, f, :, tk[d]]
                        nc.tensor.matmul(self.bank[i % 4][:, 0:2 * P], bm[d][a:a + HD, f, tk[d]], zr_h, start=True, stop=True)
                        nc.tensor.matmul(self.bank[i % 4][:, 2 * P:4 * P], km[d][a:a + HD, f, tk[d]], zr_h, start=True, stop=True).then_inc(made.sem, 1)
                    for d in range(2):
                        for i, src in enumerate((bm[d], km[d])):
                            for f in range(2):
                                last = nc.tensor.transpose(self.bank[4 + 2 * d + i][:, f * P:(f + 1) * P], src[:, f, tk[d]], ident)
                            last.then_inc(turned.sem, 1)
                    pe.wait_ge(masked.sem, masked.at(8))
                    for i in range(8):
                        hc = slice((i % 4) * HD, (i % 4 + 1) * HD)
                        last = nc.tensor.matmul(self.bank[0][:, i * HD:(i + 1) * HD], A[:, i, 2], vtok[:, tile[i // 4], hc], start=True, stop=True)
                    last.then_inc(wsum.sem, 1)

                @block.vector
                def _(dve):
                    for i in range(8):
                        dve.wait_ge(made.sem, made.at(i + 1))
                        m = causal[:, i // 4].unsqueeze(1).to_broadcast([P, 2, 2 * P])
                        nc.vector.tensor_tensor(A[:, i].rearrange("p (a b) t -> p a (b t)", a=2),
                                                self.bank[i % 4].rearrange("p (a b) -> p a b", a=2), m, ALU.mult).then_inc(masked.sem, 1)

                @block.scalar
                def _(act):
                    for j in range(4):
                        act.wait_ge(turned.sem, turned.at(j + 1))
                        nc.scalar.activation(btok[:, j], self.bank[4 + j][:, 0:RW_WIDTH], ACT.Copy)
                    act.wait_ge(wsum.sem, wsum.at(1))
                    nc.scalar.activation(W.rearrange("p d n -> p (d n)"), self.bank[0], ACT.Copy)
            made.advance(8)
            wsum.advance(1)
            masked.advance(8)
            turned.advance(4)

            self.rwkv_solve(A, X, XT, N, H, levels)

            half = ((0, 1), (1, 0))
            dsum, dmoved, usum, umoved = (self.counted(n) for n in ("d_summed", "d_moved", "u_summed", "u_moved"))
            ysum, ymoved, ssum, smoved = (self.counted(n) for n in ("y_summed", "y_moved", "state_summed", "state_step"))
            dready, csum = self.counted("decay_ready"), self.counted("own_summed")
            with nc.Block() as block:
                @block.gpsimd
                def _(pool):
                    for c in range(2):
                        if c == 1:
                            pool.wait_ge(smoved.sem, smoved.at(1))
                        for d in range(2):
                            ch = 2 * tile[d] + half[d][c]
                            for f in range(2):
                                last = nc.gpsimd.tensor_scalar(decay[:, 2 * d + f], headones, pc[d][:, f, ch:ch + 1], None, ALU.mult)
                        last.then_inc(dready.sem, 1)

                D_, Y_, C_ = (self.bank[i].rearrange("p (d n) -> p d n", d=2) for i in (0, 3, 4))
                U_ = (self.bank[1], self.bank[4])
                S_ = [self.bank[i] for i in (2, 5, 6, 7)]

                @block.tensor
                def _(pe):
                    for c in range(2):
                        hf = [slice(half[d][c] * HD, half[d][c] * HD + HD) for d in range(2)]
                        if c == 1:
                            pe.wait_ge(smoved.sem, smoved.at(1))
                        for d in range(2):
                            for f in range(2):
                                last = nc.tensor.matmul(D_[:, d, f * P:(f + 1) * P], zr[d][:, f, 0, tk[d]], state[:, 2 * d + f], start=True, stop=True)
                        last.then_inc(dsum.sem, 1)
                        for d in range(2):
                            for f in range(2):
                                fc = slice(f * P, (f + 1) * P)
                                nc.tensor.matmul(S_[2 * d + f][:, 0:P], btok[hf[d], 2 * d + 1, fc], vtok[hf[d], tile[d], fc], start=True, stop=False)
                                nc.tensor.matmul(S_[2 * d + f][:, 0:P], ident, state[:, 2 * d + f], start=False, stop=False)
                        pe.wait_ge(dmoved.sem, dmoved.at(c + 1))
                        for d in range(2):
                            for hd in range(4):
                                hc = slice(hd * HD, (hd + 1) * HD)
                                last = nc.tensor.matmul(U_[d][:, hc], XT[hf[d], 4 * d + hd], Dm[hf[d], d, hc], start=True, stop=True)
                        last.then_inc(usum.sem, 1)
                        if c == 1:
                            pe.wait_ge(ymoved.sem, ymoved.at(1))
                        for d in range(2):
                            for f in range(2):
                                last = nc.tensor.matmul(Y_[:, d, f * P:(f + 1) * P], zr[d][:, f, 1, tk[d]], state[:, 2 * d + f], start=True, stop=True)
                        last.then_inc(ysum.sem, 1)
                        pe.wait_ge(umoved.sem, umoved.at(c + 1))
                        for d in range(2):
                            for f in range(2):
                                fc = slice(f * P, (f + 1) * P)
                                last = nc.tensor.matmul(S_[2 * d + f][:, 0:P], btok[hf[d], 2 * d, fc], U[hf[d], d, fc], start=False, stop=True)
                        last.then_inc(ssum.sem, 1)
                    for d in range(2):
                        for hd in range(4):
                            hc = slice(hd * HD, (hd + 1) * HD)
                            nc.tensor.matmul(C_[:, d, hc], A[:, 4 * d + hd, 1], U[:, d, hc], start=True, stop=False)
                            last = nc.tensor.matmul(C_[:, d, hc], A[:, 4 * d + hd, 3], vtok[:, tile[d], hc], start=False, stop=True)
                    last.then_inc(csum.sem, 1)

                @block.vector
                def _(dve):
                    for c in range(2):
                        hf = [slice(half[d][c] * HD, half[d][c] * HD + HD) for d in range(2)]
                        dve.wait_ge(dsum.sem, dsum.at(c + 1))
                        for d in range(2):
                            last = nc.vector.tensor_tensor(Dm[hf[d], d], D_[hf[d], d], W[hf[d], d], ALU.add)
                        last.then_inc(dmoved.sem, 1)
                        dve.wait_ge(usum.sem, usum.at(c + 1))
                        for d in range(2):
                            last = nc.vector.tensor_copy(U[hf[d], d], U_[d][hf[d], 0:RW_WIDTH])
                        last.then_inc(umoved.sem, 1)
                        dve.wait_ge(ssum.sem, ssum.at(c + 1))
                        dve.wait_ge(dready.sem, dready.at(c + 1))
                        for i in range(4):
                            last = nc.vector.tensor_tensor(state[:, i], S_[i][:, 0:P], decay[:, i], ALU.mult)
                        last.then_inc(smoved.sem, 1)
                    dve.wait_ge(csum.sem, csum.at(1))
                    dve.wait_ge(ymoved.sem, ymoved.at(2))
                    for d in range(2):
                        nc.vector.tensor_tensor(ytok[:, d, tile[d]], C_[:, d], ytok[:, d, tile[d]], ALU.add)

                @block.scalar
                def _(act):
                    for c in range(2):
                        act.wait_ge(ysum.sem, ysum.at(c + 1))
                        for d in range(2):
                            hf = slice(half[d][c] * HD, half[d][c] * HD + HD)
                            last = nc.scalar.activation(ytok[hf, d, tile[d]], Y_[hf, d], ACT.Copy)
                        last.then_inc(ymoved.sem, 1)
            for q in (dsum, dmoved, usum, umoved, ysum, ymoved, ssum, smoved, dready):
                q.advance(2)
            csum.advance(1)
        ar.free("causal", "levels", "state", "A", "X", "XT", "N", "H", "btok", "Dm", "U", "decay", "W")
        return ytok

    def rwkv_solve(self, A, X, XT, N, H, levels):
        nc = self.nc
        ident = self.tab("ident")
        picked, turned, hs, hm, xs, xm = (self.counted(n) for n in ("level_picked", "x_turned", "h_summed", "h_moved", "x_summed", "x_added"))
        idb = ident.unsqueeze(1).to_broadcast([P, 4, P])
        bank4 = lambda b: self.bank[b].rearrange("p (h t) -> p h t", h=4)
        with nc.Block() as block:
            @block.gpsimd
            def _(pool):
                for lv in range(6):
                    for d in range(2):
                        if lv == 1:
                            pool.wait_ge(turned.sem, turned.at(d + 1))
                            pool.wait_ge(xm.sem, xm.at(2 * d + 1))
                        if lv >= 2:
                            pool.wait_ge(hs.sem, hs.at(2 * (lv - 2) + d + 1))
                        g = slice(4 * d, 4 * d + 4)
                        m = levels[:, d, lv].unsqueeze(1).to_broadcast([P, 4, P])
                        nc.gpsimd.tensor_tensor(N[:, g], A[:, g, 0], m, ALU.mult).then_inc(picked.sem, 1)

            @block.vector
            def _(dve):
                for d in range(2):
                    g = slice(4 * d, 4 * d + 4)
                    dve.wait_ge(picked.sem, picked.at(d + 1))
                    nc.vector.tensor_tensor(XT[:, g], N[:, g], idb, ALU.add).then_inc(xm.sem, 1)
                    dve.wait_ge(turned.sem, turned.at(d + 1))
                    nc.vector.tensor_tensor(X[:, g], bank4(d), idb, ALU.add).then_inc(xm.sem, 1)
                for lv in range(1, 6):
                    for d in range(2):
                        g = slice(4 * d, 4 * d + 4)
                        dve.wait_ge(xs.sem, xs.at(2 * (lv - 1) + d + 1))
                        nc.vector.tensor_tensor(XT[:, g], bank4(2 + d), XT[:, g], ALU.add).then_inc(xm.sem, 1)
                        if lv < 5:
                            nc.vector.tensor_tensor(X[:, g], bank4(4 + d), X[:, g], ALU.add).then_inc(xm.sem, 1)

            @block.scalar
            def _(act):
                for i in range(10):
                    d = i % 2
                    act.wait_ge(hs.sem, hs.at(i + 1))
                    nc.scalar.activation(H[:, 4 * d:4 * d + 4], bank4(6 + d), ACT.Copy).then_inc(hm.sem, 1)

            @block.tensor
            def _(pe):
                for d in range(2):
                    pe.wait_ge(picked.sem, picked.at(d + 1))
                    for hd in range(4):
                        last = nc.tensor.transpose(self.bank[d][:, hd * P:(hd + 1) * P], N[:, 4 * d + hd], ident)
                    last.then_inc(turned.sem, 1)
                for lv in range(1, 6):
                    for d in range(2):
                        i = 2 * (lv - 1) + d
                        pe.wait_ge(picked.sem, picked.at(2 * lv + d + 1))
                        pe.wait_ge(xm.sem, xm.at(2 * (i + 1)))
                        for hd in range(4):
                            last = nc.tensor.matmul(self.bank[6 + d][:, hd * P:(hd + 1) * P], N[:, 4 * d + hd], X[:, 4 * d + hd], start=True, stop=True)
                        last.then_inc(hs.sem, 1)
                    for d in range(2):
                        pe.wait_ge(hm.sem, hm.at(2 * (lv - 1) + d + 1))
                        for hd in range(4):
                            c, q = slice(hd * P, (hd + 1) * P), 4 * d + hd
                            last = nc.tensor.matmul(self.bank[2 + d][:, c], H[:, q], XT[:, q], start=True, stop=True)
                            if lv < 5:
                                last = nc.tensor.matmul(self.bank[4 + d][:, c], XT[:, q], H[:, q], start=True, stop=True)
                        last.then_inc(xs.sem, 1)
        picked.advance(12)
        turned.advance(2)
        hs.advance(10)
        hm.advance(10)
        xs.advance(10)
        xm.advance(22)

    def rwkv_out(self, layer, y, gate):
        nc, ar = self.nc, self.arena
        yT, sq, o = ar.take("yT", 2, T2), ar.take("sq", 2, T2), ar.take("o", 2, T2)
        turned, st, summed = self.counted("y_turned"), self.counted("headnorm_step"), self.counted("headnorm_summed")
        rooted = self.counted("rooted")
        with nc.Block() as block:
            @block.tensor
            def _(pe):
                for f in range(2):
                    for t in range(4):
                        last = nc.tensor.transpose(self.bank[f][:, t * P:(t + 1) * P], y[:, t, f * P:(f + 1) * P], self.tab("ident"))
                last.then_inc(turned.sem, 1)
                for n, (src, want) in enumerate(((yT, 1), (sq, 3))):
                    pe.wait_ge(st.sem, st.at(want))
                    for f in range(2):
                        last = nc.tensor.matmul(self.bank[2 + 2 * n + f], self.tab("headones"), src[:, f], start=True, stop=True)
                    last.then_inc(summed.sem, 1)

            @block.vector
            def _(dve):
                n = 0

                def after(last):
                    nonlocal n
                    last.then_inc(st.sem, 1)
                    n += 1
                    dve.wait_ge(st.sem, st.at(n))

                dve.wait_ge(turned.sem, turned.at(1))
                for f in range(2):
                    last = nc.vector.tensor_copy(yT[:, f], self.bank[f])
                after(last)
                dve.wait_ge(summed.sem, summed.at(1))
                for f in range(2):
                    last = nc.vector.scalar_tensor_tensor(o[:, f], self.bank[2 + f], -1.0 / HD, yT[:, f], ALU.mult, ALU.add)
                after(last)
                after(nc.vector.tensor_tensor(sq, o, o, ALU.mult))
                dve.wait_ge(summed.sem, summed.at(2))
                for f in range(2):
                    last = nc.vector.tensor_scalar(yT[:, f], self.bank[4 + f], 1.0 / HD, RW_GN_EPS, ALU.mult, ALU.add)
                after(last)
                after(nc.vector.reciprocal(yT, yT))
                dve.wait_ge(rooted.sem, rooted.at(1))
                for f in range(2):
                    last = nc.vector.scalar_tensor_tensor(o[:, f], o[:, f], self.col(f"gn_g{layer}", f), yT[:, f], ALU.mult, ALU.mult)
                after(last)
                for f in range(2):
                    last = nc.vector.scalar_tensor_tensor(o[:, f], o[:, f], self.col(f"gn_b{layer}", f), gate[:, f], ALU.add, ALU.mult)
                after(last)
                nc.vector.tensor_tensor(self.hT[:, 4:6, :], self.hT[:, 4:6, :], o, ALU.add)
                st.n = n

            @block.scalar
            def _(act):
                act.wait_ge(st.sem, st.at(5))
                nc.scalar.activation(yT, yT, ACT.Sqrt).then_inc(rooted.sem, 1)
        rooted.advance(1)
        turned.advance(1)
        summed.advance(2)
        st.advance(st.n)
        ar.free("yT", "sq", "o")

    def conformer(self, cv, layer, seqs):
        nc, ar = self.nc, self.arena
        pad = CV_LEN // 2
        ns, t0 = len(seqs), seqs[0].start
        tokens = slice(t0, T2)
        nt = T2 - t0
        h, o, tmp = ar.take("cvpad", 2, ns, SEQ + 2 * pad), ar.take("o", 2, nt), ar.take("tmp", 2, nt)
        opened, st, summed, done = self.counted("cv_opened"), self.counted("cv_step"), self.counted("cv_summed"), self.counted("cv_out")
        rooted = self.counted("rooted")
        per_seq = lambda x: x.rearrange("p (s t) -> p s t", s=ns)
        with nc.Block() as block:
            @block.scalar
            def _(act):
                nc.scalar.activation(cv[:, 2:4, tokens], cv[:, 2:4, tokens], ACT.Sigmoid).then_inc(opened.sem, 1)
                act.wait_ge(st.sem, st.at(6 + CV_LEN))
                nc.scalar.activation(tmp[:, 0], tmp[:, 0], ACT.Sqrt).then_inc(rooted.sem, 1)
                act.wait_ge(done.sem, done.at(1))
                for f in range(2):
                    nc.scalar.activation(self.hT[:, 6 + f, tokens], o[:, f], ACT.Silu, bias=self.col(f"ln_b{layer}", f))

            @block.tensor
            def _(pe):
                for n in range(2):
                    pe.wait_ge(st.sem, st.at(2 + CV_LEN if n == 0 else 4 + CV_LEN))
                    src = o if n == 0 else tmp
                    for f in range(2):
                        last = nc.tensor.matmul(self.bank[n][:, 0:nt], self.tab("ones"), src[:, f], start=f == 0, stop=f == 1)
                    last.then_inc(summed.sem, 1)

            @block.vector
            def _(dve):
                n = 0

                def after(last):
                    nonlocal n
                    last.then_inc(st.sem, 1)
                    n += 1
                    dve.wait_ge(st.sem, st.at(n))

                after(nc.vector.memset(h, 0.0))
                dve.wait_ge(opened.sem, opened.at(1))
                for f in range(2):
                    last = nc.vector.tensor_tensor(h[:, f, :, pad:pad + SEQ], per_seq(cv[:, f, tokens]), per_seq(cv[:, 2 + f, tokens]), ALU.mult)
                after(last)
                for tap in range(CV_LEN):
                    for f in range(2):
                        w, src = self.col(f"dw_w{layer}_{tap}", f), h[:, f, :, tap:tap + SEQ]
                        if tap == 0:
                            last = nc.vector.tensor_scalar(per_seq(o[:, f]), src, w, self.col(f"dw_b{layer}", f), ALU.mult, ALU.add)
                        else:
                            last = nc.vector.scalar_tensor_tensor(per_seq(o[:, f]), src, w, per_seq(o[:, f]), ALU.mult, ALU.add)
                    after(last)
                dve.wait_ge(summed.sem, summed.at(1))
                for f in range(2):
                    last = nc.vector.scalar_tensor_tensor(o[:, f], self.bank[0][:, 0:nt], -1.0 / RW_WIDTH, o[:, f], ALU.mult, ALU.add)
                after(last)
                after(nc.vector.tensor_tensor(tmp, o, o, ALU.mult))
                dve.wait_ge(summed.sem, summed.at(2))
                after(nc.vector.tensor_scalar(tmp[:, 0], self.bank[1][:, 0:nt], 1.0 / RW_WIDTH, LN_EPS, ALU.mult, ALU.add))
                after(nc.vector.reciprocal(tmp[:, 0], tmp[:, 0]))
                dve.wait_ge(rooted.sem, rooted.at(1))
                for f in range(2):
                    last = nc.vector.scalar_tensor_tensor(o[:, f], o[:, f], self.col(f"ln_g{layer}", f), tmp[:, 0], ALU.mult, ALU.mult)
                last.then_inc(done.sem, 1)
                st.n = n
        rooted.advance(1)
        opened.advance(1)
        summed.advance(2)
        done.advance(1)
        st.advance(st.n)
        ar.free("cvpad", "o", "tmp")

    def block_two(self):
        nc, ins, ar = self.nc, self.ins, self.arena
        xT, hT = self.xT, self.hT
        at = lambda a: (lambda j: a[:, j])
        for layer in range(2):
            ctx = layer == 0
            seqs = [CTX, LAT] if ctx else [LAT]
            own = BOTH if ctx else LAT
            mod, gain = self.norm_gains(layer)
            self.modulated_norm(mod, gain, 0, True)

            qk = ar.take("qk", 8, T2)
            v = ar.take("v", 4, 512)
            cv = ar.take("cv", 4, T2)
            rwpad = ar.take("rwpad", 10, 2, SEQ + 2)
            with nc.Block() as block:
                @block.vector
                def _(dve):
                    for edge in (0, SEQ + 1):
                        nc.vector.memset(rwpad[:, :, :, edge:edge + 1], 0.0)

            bias = ar.take("bias", 8, 2, SEQ)
            window = ar.take("window", SEQ)
            flip = ar.take("flip", P)
            loads = [(window, self.table_src("window")), (flip, self.table_src("flip_rows"))]
            for hd in range(8):
                for row in range(4):
                    off = ((layer * 8 + hd) * 15 + 7 - row) * 127
                    loads.append((bias[(row % 2) * GRID_W:(row % 2 + 1) * GRID_W, hd, row // 2].rearrange("p (r c) -> p r c", r=4),
                                  bass.AP(self.rpb_dram, off, [[1, GRID_W], [127, 4], [1, GRID_W]])))

            def copy_own(dst, j0, scale, n=4):
                def fn(dve, banks):
                    for j in range(n):
                        last = nc.vector.tensor_scalar(dst[:, j0 + j, own], banks[j][:, 0:own.stop - own.start], scale, None, ALU.mult)
                    return last
                return fn

            def v_evac(dve, banks):
                for t in range(4):
                    last = nc.vector.tensor_copy(v[:, t], banks[t])
                return last

            def rw_evac(j0, n):
                def fn(dve, banks):
                    for j in range(n):
                        last = nc.vector.tensor_copy(rwpad[:, j0 + j, :, 1:SEQ + 1], banks[j].rearrange("p (s t) -> p s t", s=2))
                    return last
                return fn

            F = lambda rows, act, evac, **kw: dict(kind="F", rows=rows, act=act, evac=evac, **kw)
            h_all = lambda k: hT[:, k, :]
            h_own = lambda k: hT[:, k, own]
            self.linear([F(D, h_own, {"vector": copy_own(qk, 0, HD ** -0.5)}), F(D, h_all, {"vector": self.copy_f(at(qk), 4)}),
                         dict(kind="T", rows=D, act=h_all, evac={"vector": v_evac}),
                         F(D, h_all, {"vector": rw_evac(0, 4)}), F(D, h_all, {"vector": rw_evac(4, 4)}),
                         F(D, h_all, {"vector": rw_evac(8, 2)}), F(D, h_own, {"vector": copy_own(cv, 0, 1.0)})], loads=loads)

            with nc.Block() as block:
                @block.vector
                def _(dve):
                    for hd in range(8):
                        nc.vector.tensor_tensor(bias[:, hd], bias[:, hd], window.unsqueeze(1).to_broadcast([P, 2, SEQ]), ALU.add)
            units = []
            for hd in range(8):
                a, ft = (hd % 2) * HD, hd // 2
                for i in range(2):
                    tq = slice(SEQ + i * P, SEQ + (i + 1) * P)
                    units.append(dict(q=[qk[a:a + HD, ft, tq]], k=[qk[a:a + HD, 4 + ft, :]],
                                      v=[v[:, t, hd * HD:(hd + 1) * HD] for t in range(4)],
                                      out=[hT[a:a + HD, ft, tq]], out_part=a, bias=bias[:, hd, i], count=None))
            if ctx:
                for hd in range(8):
                    a, ft = (hd % 2) * HD, hd // 2
                    for i in range(2):
                        tq = slice(i * P, (i + 1) * P)
                        units.append(dict(q=[qk[a:a + HD, ft, tq]], k=[qk[a:a + HD, 4 + ft, CTX]],
                                          v=[v[:, t, hd * HD:(hd + 1) * HD] for t in range(2)],
                                          out=[hT[a:a + HD, ft, tq]], out_part=a, bias=None, count=None))
            self.attention(units, flip)
            ar.free("qk", "v", "bias", "window", "flip")
            self.conformer(cv, layer, seqs)
            ar.free("cv")
            self.rwkv(rwpad, layer)

            def gates(n):
                out = [(LAT, lambda t: mod[:, (3 * n + 2) * DT + t, 0:1])]
                if ctx:
                    out.insert(0, (CTX, lambda t: mod[:, (3 * n + 2) * DT + t, 1:2]))
                return out

            self.linear([F(D, h_own, {"vector": self.residual(g, own, gates(0))}) for g in range(2)])
            self.modulated_norm(mod, gain, 1, ctx)
            if layer == 0:
                hidden = ar.take("hidden", D_FF // P, T2)
                groups = []
                for j0 in range(0, D_FF // P, 4):
                    n = min(4, D_FF // P - j0)

                    def silu_evac(act, banks, j0=j0, n=n):
                        for j in range(n):
                            last = nc.scalar.activation(hidden[:, j0 + j], banks[j], ACT.Silu)
                        return last

                    def up_evac(dve, banks, j0=j0, n=n):
                        for j in range(n):
                            last = nc.vector.tensor_tensor(hidden[:, j0 + j], banks[j], hidden[:, j0 + j], ALU.mult)
                        return last

                    groups.append(F(D, h_all, {"scalar": silu_evac}))
                    groups.append(F(D, h_all, {"vector": up_evac}, vector_after_scalar=True))
                self.linear(groups)
                self.linear([F(D_FF, at(hidden), {"vector": self.residual(g, BOTH, gates(1))}) for g in range(2)])
                ar.free("hidden")
            else:
                self.experts(gates(1)[0][1])

        self.rmsnorm(lambda k: xT[:, k, LAT], DT, SEQ, [(slice(0, SEQ), lambda k: xT[:, k, LAT], lambda k: self.col("final_g", k), None)])

    def experts(self, gate_column):
        nc, ar, ins = self.nc, self.arena, self.ins
        hT, xT = self.hT, self.xT
        E, I = N_EXPERTS, MAX_ITEMS
        ident = self.tab("ident")
        router = ar.take("router", DT, E)
        gt = ar.take("gt", 2, 88)
        idx = ar.take("idx", 2, 8).bitcast(U32)
        sh = ar.take("shares", 4, E)
        oh = ar.take("oh", 3, I, E)
        it = ar.take("it", 8, I)
        number = ar.take("number", 16).bitcast(mybir.dt.int32)
        earlier, iota, items = ar.take("earlier", P), ar.take("iota", P), ar.take("items", I, E)
        xtok = ar.take("xtok", 2, D)
        pick = ar.take("pick", 2, I, P)
        spread = ar.take("spread", I, SEQ)
        gated = ar.take("gated", 4, P)
        self.load([(router, ins["moe_router_2"][0].rearrange("(k p) e -> p k e", p=P)),
                   (earlier, self.table_src("earlier")), (iota, self.table_src("iota128")),
                   (items.rearrange("p i e -> p (i e)"), self.table_src("items"))])
        logits, st, ed = self.counted("logits_ready"), self.counted("route_step"), self.counted("route_exp")
        placed, rows, rowsm = self.counted("places_summed"), self.counted("h_turned"), self.counted("h_rows_ready")
        gready, gturned, gmoved = self.counted("gated_ready"), self.counted("gated_turned"), self.counted("gated_moved")
        LG, TOP, IX, E1, G0, G1, DL, DN, M0, M1, MS, GS, PM = 0, 8, 16, 24, 25, 26, 27, 28, 32, 40, 48, 56, 64
        with nc.Block() as block:
            @block.tensor
            def _(pe):
                for t in range(2):
                    for k in range(DT):
                        last = nc.tensor.matmul(self.bank[t][:, 0:E], hT[:, k, SEQ + t * P:SEQ + (t + 1) * P], router[:, k, :], start=k == 0, stop=k == DT - 1)
                    last.then_inc(logits.sem, 1)
                for t in range(2):
                    for k in range(DT):
                        last = nc.tensor.transpose(self.bank[4 + 2 * t + k // 4][:, (k % 4) * P:(k % 4 + 1) * P], hT[:, k, SEQ + t * P:SEQ + (t + 1) * P], ident)
                last.then_inc(rows.sem, 1)
                pe.wait_ge(st.sem, st.at(8))
                nc.tensor.matmul(self.bank[2][:, 0:E], earlier, gt[:, 0, MS:MS + E], start=True, stop=True)
                nc.tensor.matmul(self.bank[2][:, 8:8 + E], earlier, gt[:, 1, MS:MS + E], start=True, stop=False)
                nc.tensor.matmul(self.bank[2][:, 8:8 + E], self.tab("ones"), gt[:, 0, MS:MS + E], start=False, stop=True)
                nc.tensor.matmul(self.bank[2][:, 16:16 + E], self.tab("ones"), gt[:, 0, MS:MS + E], start=True, stop=False)
                nc.tensor.matmul(self.bank[2][:, 16:16 + E], self.tab("ones"), gt[:, 1, MS:MS + E], start=False, stop=True).then_inc(placed.sem, 1)
                pe.wait_ge(rowsm.sem, rowsm.at(1))
                for i in range(2 * I):
                    pe.wait_ge(gready.sem, gready.at(i + 1))
                    if i >= 4:
                        pe.wait_ge(gmoved.sem, gmoved.at(i - 3))
                    nc.tensor.transpose(self.bank[4 + i % 4][:, 0:P], gated[:, i % 4], ident).then_inc(gturned.sem, 1)

            @block.scalar
            def _(act):
                act.wait_ge(rows.sem, rows.at(1))
                for t in range(2):
                    for b in range(2):
                        last = nc.scalar.activation(xtok[:, t, 512 * b:512 * b + 512], self.bank[4 + 2 * t + b], ACT.Copy)
                last.then_inc(rowsm.sem, 1)
                act.wait_ge(st.sem, st.at(4))
                for t in range(2):
                    last = nc.scalar.activation(gt[:, t, E1:E1 + 1], gt[:, t, DL:DL + 1], ACT.Exp)
                last.then_inc(ed.sem, 1)
                for i in range(2 * I):
                    act.wait_ge(gturned.sem, gturned.at(i + 1))
                    nc.scalar.activation(spread[:, i // 2, (i % 2) * P:(i % 2 + 1) * P], self.bank[4 + i % 4][:, 0:P], ACT.Copy).then_inc(gmoved.sem, 1)

            @block.vector
            def _(dve):
                n = 0

                def after(last):
                    nonlocal n
                    last.then_inc(st.sem, 1)
                    n += 1
                    dve.wait_ge(st.sem, st.at(n))

                both = (0, 1)
                wide = lambda x: x.unsqueeze(1).to_broadcast([P, I, E])
                dve.wait_ge(logits.sem, logits.at(2))
                for t in both:
                    last = nc.vector.tensor_copy(gt[:, t, LG:LG + E], self.bank[t][:, 0:E])
                after(last)
                for t in both:
                    last = nc.vector.max(gt[:, t, TOP:TOP + 8], gt[:, t, LG:LG + E])
                after(last)
                for t in both:
                    last = nc.vector.max_index(idx[:, t], gt[:, t, TOP:TOP + 8], gt[:, t, LG:LG + E])
                after(last)
                for t in both:
                    nc.vector.tensor_copy(gt[:, t, IX:IX + 8], idx[:, t])
                    last = nc.vector.tensor_tensor(gt[:, t, DL:DL + 1], gt[:, t, TOP + 1:TOP + 2], gt[:, t, TOP:TOP + 1], ALU.subtract)
                after(last)
                dve.wait_ge(ed.sem, ed.at(1))
                for t in both:
                    last = nc.vector.tensor_scalar(gt[:, t, DN:DN + 1], gt[:, t, E1:E1 + 1], 1.0, None, ALU.add)
                    for i, m in ((0, M0), (1, M1)):
                        last = nc.vector.tensor_scalar(gt[:, t, m:m + E], self.tab("iota8"), gt[:, t, IX + i:IX + i + 1], None, ALU.is_equal)
                after(last)
                for t in both:
                    last = nc.vector.reciprocal(gt[:, t, G0:G0 + 1], gt[:, t, DN:DN + 1])
                after(last)
                for t in both:
                    last = nc.vector.tensor_tensor(gt[:, t, G1:G1 + 1], gt[:, t, E1:E1 + 1], gt[:, t, G0:G0 + 1], ALU.mult)
                after(last)
                for t in both:
                    last = nc.vector.tensor_tensor(gt[:, t, MS:MS + E], gt[:, t, M0:M0 + E], gt[:, t, M1:M1 + E], ALU.add)
                after(last)
                for t in both:
                    last = nc.vector.tensor_scalar(gt[:, t, M0:M0 + E], gt[:, t, M0:M0 + E], gt[:, t, G0:G0 + 1], None, ALU.mult)
                after(last)
                for t in both:
                    last = nc.vector.scalar_tensor_tensor(gt[:, t, GS:GS + E], gt[:, t, M1:M1 + E], gt[:, t, G1:G1 + 1], gt[:, t, M0:M0 + E], ALU.mult, ALU.add)
                dve.wait_ge(placed.sem, placed.at(1))
                for t in both:
                    last = nc.vector.scalar_tensor_tensor(gt[:, t, PM:PM + E], self.bank[2][:, 8 * t:8 * t + E], 1000.0, gt[:, t, MS:MS + E], ALU.add, ALU.mult)
                    last = nc.vector.tensor_scalar(sh[:, t], self.bank[2][:, 16:16 + E], 1.0 if t == 0 else P + 1.0, None, ALU.is_ge)
                after(last)
                for t in both:
                    nc.vector.tensor_scalar(gt[:, t, PM:PM + E], gt[:, t, PM:PM + E], -1000.0, None, ALU.add)
                after(nc.vector.tensor_tensor(sh[:, 1], sh[:, 0], sh[:, 1], ALU.add))
                after(nc.vector.tensor_tensor_scan(sh[:, 2], self.tab("ones")[:, 0:E], sh[:, 1], 0.0, ALU.mult, ALU.add))
                after(nc.vector.tensor_tensor(sh[:, 3], sh[:, 2], sh[:, 1], ALU.subtract))
                nc.vector.tensor_tensor(oh[:, 0], items, wide(sh[:, 3]), ALU.is_ge)
                after(nc.vector.tensor_tensor(oh[:, 1], items, wide(sh[:, 2]), ALU.is_lt))
                nc.vector.tensor_tensor(oh[:, 2], items, wide(sh[:, 3]), ALU.subtract)
                after(nc.vector.tensor_tensor(oh[:, 0], oh[:, 0], oh[:, 1], ALU.mult))
                nc.vector.tensor_tensor(oh[:, 2], oh[:, 2], oh[:, 0], ALU.mult)
                after(nc.vector.tensor_tensor(oh[:, 1], wide(self.tab("iota8")), oh[:, 0], ALU.mult))
                nc.vector.tensor_reduce(it[:, 0], oh[:, 1], AX_X, ALU.add)
                after(nc.vector.tensor_reduce(it[:, 1], oh[:, 2], AX_X, ALU.add))
                nc.vector.tensor_copy(number[:, 0:I], it[:, 0])
                nc.vector.tensor_copy(number[:, I:I + 1], sh[:, 2, E - 1:E])
                after(nc.vector.tensor_scalar(it[:, 1], it[:, 1], float(P), None, ALU.mult))
                for src, col in ((PM, 2), (GS, 4)):
                    for t in both:
                        after(nc.vector.tensor_tensor(oh[:, 1], wide(gt[:, t, src:src + E]), oh[:, 0], ALU.mult))
                        after(nc.vector.tensor_reduce(it[:, col + t], oh[:, 1], AX_X, ALU.add))
                for t in both:
                    last = nc.vector.tensor_tensor(it[:, 2 + t], it[:, 2 + t], it[:, 1], ALU.subtract)
                after(last)
                for i in range(2 * I):
                    item, t = i // 2, i % 2
                    slot, gate = it[:, 2 + t, item:item + 1], it[:, 4 + t, item:item + 1]
                    if i >= 4:
                        dve.wait_ge(gturned.sem, gturned.at(i - 3))
                    nc.vector.tensor_scalar(gated[:, i % 4], iota, slot, gate, ALU.is_equal, ALU.mult).then_inc(gready.sem, 1)
                    nc.vector.tensor_scalar(pick[:, t, item], iota, slot, None, ALU.is_equal)
                st.n = n
        for q, k in ((logits, 2), (st, st.n), (ed, 1), (placed, 1), (rows, 1), (rowsm, 1), (gready, 2 * I), (gturned, 2 * I), (gmoved, 2 * I)):
            q.advance(k)
        ar.free("router", "gt", "idx", "shares", "oh", "it", "earlier", "iota", "items", "gated")

        acc = ar.take("acc", DT, SEQ)
        xg = ar.take("xg", DT, P)
        hk = ar.take("hk", 2, GROUP)
        hid = ar.take("hid", D_FFE // P, P)
        y = ar.take("y", D)
        n_col, n_in, n_down = D_FFE // GROUP, D // (TILE_K * P), D_FFE // (TILE_K * P)
        per = 2 * n_col * n_in + 2 * n_down
        assert per % WEIGHT_SLOTS == 0
        turns = per // WEIGHT_SLOTS
        t0 = self.taken
        used = self.tile_used
        wg, wu, wd = (ins[f"moe_w_{n}_2"][0] for n in ("gate", "up", "down"))

        def source(j, e):
            if j < 2 * n_col * n_in:
                g, half = divmod(j, n_in)
                w = wg if g % 2 == 0 else wu
                c, r = (g // 2) * GROUP, half * TILE_K * P
            else:
                g, half = divmod(j - 2 * n_col * n_in, n_down)
                w, c, r = wd, g * GROUP, half * TILE_K * P
            rows = w.rearrange("e r c -> (e r) c")
            return rows[bass.ds(e * w.shape[1] + r, TILE_K * P), c:c + GROUP].rearrange("(k p) n -> p k n", p=P)

        gathered, xready = self.counted("tokens_gathered"), self.counted("tokens_ready")
        silu, mult, turned, moved = (self.counted(n) for n in ("gate_silu", "gate_times_up", "hidden_turned", "hidden_ready"))
        ymoved, scattered, added = self.counted("outputs_moved"), self.counted("outputs_scattered"), self.counted("outputs_added")
        with nc.Block() as block:
            @block.sync
            def _(sync):
                def load_tile(j, x, e):
                    src = source(j, e)
                    sync.wait_ge(used.sem, x * per + (t0 + j - WEIGHT_SLOTS + 1))
                    sync.dma_start(self.ring[:, (t0 + j) % WEIGHT_SLOTS], src).then_inc(self.slot_full[(t0 + j) % WEIGHT_SLOTS].sem, 16)

                def expert_of(x):
                    return sync.value_load(number[0:1, bass.ds(x, 1)], min_val=0, max_val=E - 1)

                n_items = sync.value_load(number[0:1, I:I + 1], min_val=2, max_val=I)
                first = expert_of(0)
                for j in range(WEIGHT_SLOTS):
                    load_tile(j, 0, first)
                with sync.Fori(1, n_items) as x:
                    now, then = expert_of(x - 1), expert_of(x)
                    for j in range(WEIGHT_SLOTS, per):
                        load_tile(j, x - 1, now)
                    for j in range(WEIGHT_SLOTS):
                        load_tile(j, x, then)
                final = expert_of(n_items - 1)
                for j in range(WEIGHT_SLOTS, per):
                    load_tile(j, n_items - 1, final)

            @block.tensor
            def _(pe):
                n_items = pe.value_load(number[0:1, I:I + 1], min_val=2, max_val=I)
                pe.wait_ge(added.sem, added.at(2))
                with pe.Fori(0, n_items) as x:
                    j = 0

                    def next_tile():
                        nonlocal j
                        pe.wait_ge(self.slot_full[(t0 + j) % WEIGHT_SLOTS].sem, x * (16 * turns) + 16 * ((t0 + j) // WEIGHT_SLOTS + 1))
                        j += 1
                        return self.ring[:, (t0 + j - 1) % WEIGHT_SLOTS]

                    def turn_hidden(q):
                        pe.wait_ge(mult.sem, x * n_col + mult.at(q + 1))
                        if q >= 2:
                            pe.wait_ge(moved.sem, x * n_col + moved.at(q - 1))
                        else:
                            pe.wait_ge(added.sem, x * 2 + added.at(2))
                        for c in range(4):
                            last = nc.tensor.transpose(self.bank[4 + q % 2][:, c * P:(c + 1) * P], hk[:, q % 2, c * P:(c + 1) * P], ident)
                        last.then_inc(turned.sem, 1)

                    for f in range(DT):
                        for t in range(2):
                            last = nc.tensor.matmul(self.bank[f // 4][:, (f % 4) * P:(f % 4 + 1) * P], xtok[:, t, f * P:(f + 1) * P],
                                                    pick[:, t, bass.ds(x, 1), :].rearrange("p o s -> p (o s)"), start=t == 0, stop=t == 1)
                    last.then_inc(gathered.sem, 1)
                    for q in range(n_col):
                        if q == 0:
                            pe.wait_ge(xready.sem, x + xready.at(1))
                        elif q == 1:
                            pe.wait_ge(ymoved.sem, x * 2 + ymoved.at(2))
                        else:
                            pe.wait_ge(mult.sem, x * n_col + mult.at(q - 1))
                        for b in (2 * (q % 2), 2 * (q % 2) + 1):
                            for i in range(n_in):
                                w = next_tile()
                                for k in range(TILE_K):
                                    kk = i * TILE_K + k
                                    last = nc.tensor.matmul(self.bank[b], xg[:, kk], w[:, k], start=kk == 0, stop=kk == DT - 1)
                                last.then_inc(used.sem, 1)
                        if q >= 1:
                            turn_hidden(q - 1)
                    for b in range(2):
                        for i in range(n_down):
                            w = next_tile()
                            if b == 0:
                                pe.wait_ge(moved.sem, x * n_col + moved.at(i + 1))
                            for k in range(TILE_K):
                                kk = i * TILE_K + k
                                last = nc.tensor.matmul(self.bank[2 + b], hid[:, kk], w[:, k], start=kk == 0, stop=kk == n_down * TILE_K - 1)
                            last.then_inc(used.sem, 1)
                            if b == 0 and i == 0:
                                turn_hidden(n_col - 1)
                    for b in range(2):
                        pe.wait_ge(ymoved.sem, x * 2 + ymoved.at(2 + b + 1))
                        for f in range(4 * b, 4 * b + 4):
                            last = nc.tensor.matmul(self.bank[4 + f // 2][:, (f % 2) * SEQ:(f % 2 + 1) * SEQ], y[:, f * P:(f + 1) * P],
                                                    spread[:, bass.ds(x, 1), :].rearrange("p o t -> p (o t)"), start=True, stop=True)
                        last.then_inc(scattered.sem, 1)

            @block.scalar
            def _(act):
                n_items = act.value_load(number[0:1, I:I + 1], min_val=2, max_val=I)
                nc.scalar.activation(y[:, 0:1], self.tab("ones")[:, 0:1], ACT.Copy).then_inc(ymoved.sem, 2)
                with act.Fori(0, n_items) as x:
                    def move_hidden(q):
                        act.wait_ge(turned.sem, x * n_col + turned.at(q + 1))
                        nc.scalar.activation(hid[:, 4 * q:4 * q + 4].rearrange("p k s -> p (k s)"), self.bank[4 + q % 2], ACT.Copy).then_inc(moved.sem, 1)

                    act.wait_ge(gathered.sem, x + gathered.at(1))
                    for b in range(2):
                        last = nc.scalar.activation(xg[:, 4 * b:4 * b + 4].rearrange("p k s -> p (k s)"), self.bank[b], ACT.Copy)
                    last.then_inc(xready.sem, 1)
                    for q in range(n_col):
                        act.wait_ge(used.sem, x * per + used.at(2 * q * n_in + n_in))
                        nc.scalar.activation(hk[:, q % 2], self.bank[2 * (q % 2)], ACT.Silu).then_inc(silu.sem, 1)
                        if q >= 1:
                            move_hidden(q - 1)
                    move_hidden(n_col - 1)
                    for b in range(2):
                        act.wait_ge(used.sem, x * per + used.at(2 * n_col * n_in + (b + 1) * n_down))
                        nc.scalar.activation(y[:, 512 * b:512 * b + 512], self.bank[2 + b], ACT.Copy).then_inc(ymoved.sem, 1)

            @block.vector
            def _(dve):
                n_items = dve.value_load(number[0:1, I:I + 1], min_val=2, max_val=I)
                nc.vector.memset(acc, 0.0).then_inc(added.sem, 2)
                dve.wait_ge(added.sem, added.at(2))
                with dve.Fori(0, n_items) as x:
                    for q in range(n_col):
                        dve.wait_ge(used.sem, x * per + used.at(2 * (q + 1) * n_in))
                        dve.wait_ge(silu.sem, x * n_col + silu.at(q + 1))
                        nc.vector.tensor_tensor(hk[:, q % 2], self.bank[2 * (q % 2) + 1], hk[:, q % 2], ALU.mult).then_inc(mult.sem, 1)
                    for b in range(2):
                        dve.wait_ge(scattered.sem, x * 2 + scattered.at(b + 1))
                        for i in range(2 * b, 2 * b + 2):
                            a = acc[:, 2 * i:2 * i + 2].rearrange("p k t -> p (k t)")
                            last = nc.vector.tensor_tensor(a, self.bank[4 + i], a, ALU.add)
                        last.then_inc(added.sem, 1)
                dve.wait_ge(added.sem, n_items * 2 + added.at(2))
                for t in range(DT):
                    nc.vector.scalar_tensor_tensor(xT[:, t, LAT], acc[:, t], gate_column(t), xT[:, t, LAT], ALU.mult, ALU.add)
        ar.free("number", "xtok", "pick", "spread", "acc", "xg", "hk", "hid", "y")

    def store(self):
        nc = self.nc
        rows = self.arena.take("rows", 2, D)
        turned, moved, stored = self.counted("rows_turned"), self.counted("turned_moved"), self.counted("output_stored")
        with nc.Block() as block:
            @block.tensor
            def _(pe):
                for t in range(2):
                    for k in range(DT):
                        last = nc.tensor.transpose(self.bank[2 * t + k // 4][:, (k % 4) * P:(k % 4 + 1) * P], self.xT[:, k, SEQ + t * P:SEQ + (t + 1) * P], self.tab("ident"))
                    last.then_inc(turned.sem, 1)

            @block.vector
            def _(dve):
                for t in range(2):
                    dve.wait_ge(turned.sem, turned.at(t + 1))
                    for b in range(2):
                        last = nc.vector.tensor_copy(rows[:, t, 512 * b:512 * b + 512], self.bank[2 * t + b])
                    last.then_inc(moved.sem, 1)

            @block.sync
            def _(sync):
                for t in range(2):
                    sync.wait_ge(moved.sem, moved.at(t + 1))
                    sync.dma_start(self.out[0, t * P:(t + 1) * P, :], rows[:, t]).then_inc(stored.sem, 16)
                sync.wait_ge(stored.sem, stored.at(32))


def vector_rows(ins):
    rows = lambda ap: ap.rearrange("(r p) -> r p", p=P)
    out = [("g_mix", rows(ins["g_mix"][0])), ("g_out_dil", rows(ins["g_out_dil"][0])), ("g_out_moba", rows(ins["g_out_moba"][0])),
           ("g_cross", rows(ins["g_cross"][0])), ("g_mem", rows(ins["g_mem"][0])), ("g_ffn", rows(ins["g_ffn"][0])),
           ("g_final", rows(ins["g_final"])), ("conv_b", rows(ins["conv_b"][0]))]
    out += [(f"conv_w{t}", rows(ins["conv_w"][0, t])) for t in range(3)]
    out += [("c", rows(ins["c_2"][0])), ("c_ctx", rows(ins["c_ctx_2"]))]
    for l in range(2):
        out += [(f"norm1_g{l}", rows(ins["norm1_g_2"][l])), (f"norm2_g{l}", rows(ins["norm2_g_2"][l])), (f"mod_b{l}", rows(ins["mod_b_2"][l])),
                (f"mu_prev{l}", rows(ins["rw_mu_prev_2"][l])), (f"mu_next{l}", rows(ins["rw_mu_next_2"][l])),
                (f"w0{l}", ins["rw_w0_2"][l].rearrange("d (r p) -> (d r) p", p=P)), (f"a0{l}", ins["rw_a0_2"][l].rearrange("d (r p) -> (d r) p", p=P)),
                (f"k_k{l}", rows(ins["rw_k_k_2"][l])), (f"k_a{l}", rows(ins["rw_k_a_2"][l])),
                (f"r_k{l}", ins["rw_r_k_2"][l].rearrange("(a b) k -> a (b k)", b=2)),
                (f"gn_g{l}", rows(ins["rw_gn_g_2"][l])), (f"gn_b{l}", rows(ins["rw_gn_b_2"][l])),
                (f"dw_w{l}", ins["cv_dw_w_2"][l].rearrange("t (r p) -> (t r) p", p=P)),
                (f"dw_b{l}", rows(ins["cv_dw_b_2"][l])), (f"ln_g{l}", rows(ins["cv_ln_g_2"][l])), (f"ln_b{l}", rows(ins["cv_ln_b_2"][l]))]
    return out + [("final_g", rows(ins["final_g_2"]))]


def build(nc, ins, out):
    ctx = ExitStack()
    with ctx:
        pr = Program(nc, ins, out, ctx)
        pr.plan(ins["w_in"][0], 0, D, 0, 6 * 512)
        pr.plan(ins["w_out"][0], 0, D, 0, D)
        pr.plan(ins["w_kv_mem"][0], 0, D, D, D)
        pr.plan(ins["w_q_mem"][0], 0, D, 0, D)
        pr.plan(ins["w_kv_mem"][0], 0, D, 0, D)
        pr.plan(ins["w_o_mem"][0], 0, D, 0, D)
        for c in range(0, D_FF, GROUP):
            for w in ("w_gate", "w_up"):
                pr.plan(ins[w][0], 0, D, c, min(GROUP, D_FF - c))
        pr.plan(ins["w_down"][0], 0, D_FF, 0, D)
        for layer in range(2):
            w = ins["w_in_2"][layer]
            for c, n in ((0, 512), (512, 512), (1024, 512), (1536, 1280), (2816, 512)):
                pr.plan(w, 0, D, c, n)
            pr.plan(ins["w_out_2"][layer], 0, D, 0, D)
            if layer == 0:
                for c in range(0, D_FF, GROUP):
                    for n in ("ffn_w_gate_2", "ffn_w_up_2"):
                        pr.plan(ins[n][0], 0, D, c, min(GROUP, D_FF - c))
                pr.plan(ins["ffn_w_down_2"][0], 0, D_FF, 0, D)
        pr.load_vectors(vector_rows(ins))
        for l in range(2):
            for tap in range(CV_LEN):
                pr.vec[f"dw_w{l}_{tap}"] = pr.vec[f"dw_w{l}"] + 2 * tap
        pr.bias_lines()
        pr.conditioning()
        pr.block_one()
        pr.block_two()
        pr.store()


_NAMES = ["x", "mem", "w_in", "g_mix", "g_out_dil", "g_out_moba", "w_out", "rel_bias", "g_cross", "g_mem", "w_q_mem",
          "w_kv_mem", "w_o_mem", "g_ffn", "w_gate", "w_up", "conv_w", "conv_b", "w_down", "g_final", "c_2", "ctx_2",
          "c_ctx_2", "norm1_g_2", "norm2_g_2", "mod_w_2", "mod_b_2", "w_in_2", "w_out_2", "na_rpb_2", "rw_mu_prev_2",
          "rw_mu_next_2", "rw_w0_2", "rw_w2_2", "rw_a0_2", "rw_a2_2", "rw_g2_2", "rw_k_k_2", "rw_k_a_2", "rw_r_k_2",
          "rw_gn_g_2", "rw_gn_b_2", "cv_dw_w_2", "cv_dw_b_2", "cv_ln_g_2", "cv_ln_b_2", "ffn_w_gate_2", "ffn_w_up_2",
          "ffn_w_down_2", "moe_router_2", "moe_w_gate_2", "moe_w_up_2", "moe_w_down_2", "final_g_2"]


def kernel(**inputs):
    import concourse.bacc as bacc
    from concourse.bass_utils import run_bass_kernel_spmd

    nc = bacc.Bacc("TRN2", target_bir_lowering=False, num_devices=1)
    arrays, ins = {}, {}
    for name in _NAMES:
        a = np.ascontiguousarray(inputs[name])
        arrays[f"in_{name}"] = a
        ins[name] = nc.dram_tensor(f"in_{name}", a.shape, mybir.dt.from_np(a.dtype), kind="ExternalInput").ap()
    tables = np.concatenate(list(_TABLES.values()), axis=1)
    arrays["shape_tables"] = tables
    ins["tables"] = nc.dram_tensor("shape_tables", tables.shape, F32, kind="ExternalInput").ap()
    out = nc.dram_tensor("out", (1, SEQ, D), F32, kind="ExternalOutput").ap()
    build(nc, ins, out)
    return run_bass_kernel_spmd(nc, [arrays], core_ids=[0]).results[0]["out"]
```

```python
import math
from contextlib import ExitStack

import numpy as np

import concourse.bass as bass
from concourse import mybir

F32 = mybir.dt.float32
U32 = mybir.dt.uint32
ALU = mybir.AluOpType
ACT = mybir.ActivationFunctionType
AX_X = mybir.AxisListType.X

P = 128
SEQ = 256
T2 = 2 * SEQ
D = 1024
DT = D // P
HD = 64
N_BUCKETS = 32
MAX_DISTANCE = 2048
D_FF = 2816
D_FFE = 3584
N_EXPERTS = 8
MAX_ITEMS = N_EXPERTS + (2 * SEQ) // (P + 1)
RW_WIDTH = 256
CV_LEN = 31
GRID_W = 64
NEG = -1e30
EPS = 1e-6
LN_EPS = 1e-5
RW_GN_EPS = 64e-5
CHUNK = 64
DECAY_SCALE = math.exp(-0.5)
WEIGHT_SLOTS = 7
GROUP = 512
TILE_K = 4
CTX = slice(0, SEQ)
LAT = slice(SEQ, T2)
BOTH = slice(0, T2)


def rel_bucket_of(n):
    half = N_BUCKETS // 2
    n = np.maximum(n, 0)
    nf = np.maximum(n, 1).astype(np.float32)
    large = half + (np.log(nf / np.float32(half)) / np.float32(math.log(MAX_DISTANCE / half))
                    * np.float32(N_BUCKETS - half)).astype(np.int32)
    return np.where(n < half, n, np.minimum(large, N_BUCKETS - 1))


def multiplicity(d):
    return (d >= 0) * ((d <= 128).astype(int) + (d % 4 == 0) + (d % 16 == 0))


def shape_tables():
    p = np.arange(P)
    tab = {}
    tab["ident"] = np.eye(P)
    tab["ones"] = np.ones((P, P))
    tab["headones"] = (p[:, None] // HD == p[None, :] // HD).astype(float)
    j = np.arange(T2)
    dist = SEQ - 1 - j
    for name, seen in (("bucket_dil", multiplicity(dist) > 0), ("bucket_moba", dist >= 0)):
        m = np.zeros((P, T2))
        m[rel_bucket_of(dist), j] = seen
        m[N_BUCKETS, :] = ~seen
        tab[name] = m
    t = np.arange(SEQ).reshape(2, P).T[:, :, None]
    tab["count"] = multiplicity(t - np.arange(SEQ)[None, None, :]).reshape(P, 2 * SEQ)
    qc, kc = p % GRID_W, np.arange(SEQ) % GRID_W
    tab["flip"] = np.eye(P)[::-1]
    tab["flip_rows"] = np.kron(np.eye(2), np.eye(GRID_W)[::-1])
    qc = GRID_W - 1 - qc
    start = np.clip(qc - 8, 0, GRID_W - 16)[:, None]
    tab["window"] = np.where((kc >= start) & (kc < start + 16), 0.0, NEG)
    row, col = p[:, None], p[None, :]
    same = row // CHUNK == col // CHUNK
    for d in range(2):
        before = (row < col) if d == 0 else (row > col)
        tab[f"causal{d}"] = np.stack([before & same, (before | (row == col)) & same], 1).reshape(P, 2 * P)
        for lv in range(6):
            s = 1 << lv
            tab[f"level{d}_{lv}"] = before & (row // (2 * s) == col // (2 * s)) & (row // s != col // s)
    tab["restart"] = np.broadcast_to(j % CHUNK != 0, (P, T2))
    tab["earlier"] = row < col
    tab["iota128"] = np.broadcast_to(p, (P, P))
    tab["items"] = np.broadcast_to(np.repeat(np.arange(MAX_ITEMS), N_EXPERTS), (P, MAX_ITEMS * N_EXPERTS))
    tab["iota8"] = np.broadcast_to(np.arange(8), (P, 8))
    return {k: np.asarray(v, np.float32) for k, v in tab.items()}


_TABLES = shape_tables()
RESIDENT = ("ident", "ones", "headones", "iota8")
_TABLES = {**{k: _TABLES[k] for k in RESIDENT}, **_TABLES}
RESIDENT_COLS = sum(_TABLES[k].shape[1] for k in RESIDENT)
TABLE_AT = {}
_at = 0
for _name, _v in _TABLES.items():
    TABLE_AT[_name] = (_at, _v.shape[1])
    _at += _v.shape[1]
TABLE_COLS = _at


class Counted:

    def __init__(self, sem):
        self.sem, self.base = sem, 0

    def at(self, n):
        return self.base + n

    def advance(self, n):
        self.base += n


class Arena:

    def __init__(self, tensor, size):
        self.tensor, self.size, self.used = tensor, size, {}

    def take(self, name, *dims):
        n = 1
        for d in dims:
            n *= d
        at = 0
        for a, k in sorted(self.used.values()):
            if at + n <= a:
                break
            at = max(at, a + k)
        assert at + n <= self.size, (name, n, at, self.size, self.used)
        assert name not in self.used, name
        self.used[name] = (at, n)
        view = self.tensor[:, at:at + n]
        if len(dims) == 2:
            view = view.rearrange("p (a b) -> p a b", a=dims[0])
        if len(dims) == 3:
            view = view.rearrange("p (a b c) -> p a b c", a=dims[0], b=dims[1])
        if len(dims) == 4:
            view = view.rearrange("p (a b c d) -> p a b c d", a=dims[0], b=dims[1], c=dims[2])
        return view

    def free(self, *names):
        for n in names:
            del self.used[n]


class SideProduct:

    HALF = DT // 2

    def __init__(self, pr, layer, first, n):
        self.pr, self.first, self.n, self.layer = pr, first, n, layer
        self.w = pr.ins["mod_w_2"][layer]
        self.tiles = pr.arena.take("mod_tiles", 2, self.HALF, GROUP)
        self.sums = pr.arena.take("mod_sums", n, 2, GROUP)
        self.full = [pr.counted(f"mod_tile{i}_full") for i in range(2)]
        self.step = pr.counted("mod_sum_step")
        self.products = pr.counted("mod_columns_made")
        self.banks = {}

    def load(self, pool):
        for i in range(2 * self.n):
            if i >= 2:
                pool.wait_ge(self.step.sem, self.step.at(self.HALF * (i - 1)))
            c, r = (self.first + i // 2) * GROUP, (i % 2) * self.HALF * P
            src = self.w[r:r + self.HALF * P, c:c + GROUP].rearrange("(k p) n -> p k n", p=P)
            pool.dma_start(self.tiles[:, i % 2], src).then_inc(self.full[i % 2].sem, 16)

    def sum_rows(self, dve, s):
        nc, cs = self.pr.nc, self.pr.cs
        for half in range(2):
            f = self.full[half]
            dve.wait_ge(f.sem, f.at(16 * (s + 1)))
            for k in range(self.HALF):
                row = half * self.HALF + k
                if row:
                    dve.wait_ge(self.step.sem, self.step.at(DT * s + row))
                for c in range(2):
                    scale, acc, w = cs[:, row, c:c + 1], self.sums[:, s, c], self.tiles[:, half, k]
                    if row == 0:
                        last = nc.vector.tensor_scalar(acc, w, scale, None, ALU.mult)
                    else:
                        last = nc.vector.scalar_tensor_tensor(acc, w, scale, acc, ALU.mult, ALU.add)
                last.then_inc(self.step.sem, 1)

    def place(self, s, j):
        at = 256 + 2 * (4 * s + j)
        return self.pr.bank[self.banks[s][j % len(self.banks[s])]][:, at:at + 2]

    def columns(self, pe, s, banks):
        nc = self.pr.nc
        self.banks[s] = banks
        pe.wait_ge(self.step.sem, self.step.at(DT * (s + 1)))
        for j in range(4):
            for c in range(2):
                last = nc.tensor.matmul(self.place(s, j)[:, c:c + 1], self.sums[:, s, c, j * P:(j + 1) * P],
                                        self.pr.tab("ones")[:, 0:1], start=True, stop=True)
        last.then_inc(self.products.sem, 1)

    def finish(self, dve):
        nc, pr = self.pr.nc, self.pr
        dve.wait_ge(self.products.sem, self.products.at(self.n))
        for s in range(self.n):
            for j in range(4):
                tile = 4 * (self.first + s) + j
                nc.vector.tensor_scalar(pr.mod[self.layer][:, tile, :], self.place(s, j), pr.col(f"mod_b{self.layer}", tile), None, ALU.add)

    def close(self):
        for f in self.full:
            f.advance(16 * self.n)
        self.step.advance(DT * self.n)
        self.products.advance(self.n)
        self.pr.arena.free("mod_tiles", "mod_sums")


class Program:
    def __init__(self, nc, ins, out, ctx):
        self.nc, self.ins, self.out, self.ctx = nc, ins, out, ctx
        self.counts = {}
        self.ring = self.sb("weight_ring", [P, WEIGHT_SLOTS, TILE_K, GROUP])
        self.xT = self.sb("residual", [P, DT, T2])
        self.hT = self.sb("normed", [P, DT, T2])
        self.table = self.sb("tables", [P, RESIDENT_COLS])
        self.small = self.sb("small", [P, 1024])
        size = nc.sbuf_bytes_remaining // 4 - 64
        self.arena = Arena(self.sb("work", [P, size]), size)
        self.bank = [ctx.enter_context(nc.psum_tensor(f"bank{i}", [P, 512], F32))[:, :] for i in range(8)]
        self.slot_full = [self.counted(f"slot{i}_full") for i in range(WEIGHT_SLOTS)]
        self.tile_used = self.counted("tile_used")
        self.weights = []
        self.issued = 0
        self.taken = 0
        self.small_at = 0
        self.vec = {}

    def sb(self, name, shape, dt=F32):
        return self.ctx.enter_context(self.nc.sbuf_tensor(name, shape, dt))

    def counted(self, name):
        if name not in self.counts:
            self.counts[name] = Counted(self.ctx.enter_context(self.nc.semaphore(name)))
        return self.counts[name]

    def tab(self, name):
        a, n = TABLE_AT[name]
        return self.table[:, a:a + n]

    def table_src(self, first, last=None):
        a = TABLE_AT[first][0]
        b, n = TABLE_AT[last or first]
        return self.ins["tables"][:, a:b + n]

    def smallcols(self, n):
        a = self.small_at
        self.small_at += n
        assert self.small_at <= 1024
        return self.small[:, a:a + n]

    def plan(self, w, row0, rows, col0, cols):
        for c in range(col0, col0 + cols, GROUP):
            width = min(GROUP, col0 + cols - c)
            for r in range(row0, row0 + rows, TILE_K * P):
                nk = min(TILE_K, (row0 + rows - r) // P)
                self.weights.append((w[r:r + nk * P, c:c + width].rearrange("(k p) n -> p k n", p=P), nk, width))

    def load_weights(self, sync, used):
        used_total = self.taken + used
        while self.issued < min(len(self.weights), used_total + WEIGHT_SLOTS):
            i = self.issued
            src, nk, width = self.weights[i]
            if i >= WEIGHT_SLOTS:
                sync.wait_ge(self.tile_used.sem, i - WEIGHT_SLOTS + 1)
            s = self.slot_full[i % WEIGHT_SLOTS]
            sync.dma_start(self.ring[:, i % WEIGHT_SLOTS, 0:nk, 0:width], src).then_inc(s.sem, 16)
            self.issued += 1

    def wait_tile(self, pe, i):
        pe.wait_ge(self.slot_full[i % WEIGHT_SLOTS].sem, 16 * (i // WEIGHT_SLOTS + 1))

    def linear(self, groups, loads=(), side=None):
        nc = self.nc
        used = self.tile_used
        evs = {n: self.counted(f"banks_emptied_by_{n}") for n in ("vector", "scalar")}
        first = self.taken
        start, t = [], first
        for g in groups:
            start.append(t)
            t += -(-g["rows"] // (TILE_K * P))
        end = t
        ends = start[1:] + [end]

        landed = self.counted("next_loads_landed")
        full = bool(side) and groups[0]["kind"] == "F" and groups[0]["act"](0).shape[-1] > SEQ
        sums = [[] for _ in groups]
        for s in range(side.n if side else 0):
            sums[s * (len(groups) - 2 * full) // side.n].append(s)
        columns = [[] for _ in range(len(groups) + 2)]
        for gi in range(len(groups)):
            for i, s in enumerate(sums[gi]):
                columns[max(gi + 2, len(groups) - 2 + (s >= side.n // 2)) if full else gi + 2].append(s)

        def banks(gi):
            return self.bank[4 * (gi % 2):4 * (gi % 2) + 4]

        def emptied(gi, name):
            return sum(1 for g in groups[:gi + 1] if name in g["evac"])

        with nc.Block() as block:
            @block.sync
            def _(sync):
                self.load_weights(sync, end - first)

            @block.tensor
            def _(pe):
                for gi, g in enumerate(groups):
                    if gi >= 2:
                        for name in groups[gi - 2]["evac"]:
                            pe.wait_ge(evs[name].sem, evs[name].at(emptied(gi - 2, name)))
                    for s in columns[gi]:
                        side.columns(pe, s, [4 * (gi % 2) + j for j in range(2 if full else 0, 4)])
                    total = g["rows"] // P
                    k0 = 0
                    for i in range(start[gi], ends[gi]):
                        _, nk, width = self.weights[i]
                        self.wait_tile(pe, i)
                        w = self.ring[:, i % WEIGHT_SLOTS]
                        if g["kind"] == "F":
                            for j in range(width // P):
                                for k in range(nk):
                                    a = g["act"](k0 + k)
                                    last = nc.tensor.matmul(banks(gi)[j][:, 0:a.shape[-1]], w[:, k, j * P:(j + 1) * P], a,
                                                            start=k0 + k == 0, stop=k0 + k == total - 1)
                        else:
                            n_tok = g["act"](0).shape[-1] // P
                            for j in range(n_tok):
                                for k in range(nk):
                                    a = g["act"](k0 + k)[:, j * P:(j + 1) * P]
                                    last = nc.tensor.matmul(banks(gi)[j][:, 0:width], a, w[:, k, 0:width],
                                                            start=k0 + k == 0, stop=k0 + k == total - 1)
                        last.then_inc(used.sem, 1)
                        k0 += nk
                if side:
                    for gi in range(max(0, len(groups) - 2), len(groups)):
                        if columns[gi + 2]:
                            for name in groups[gi]["evac"]:
                                pe.wait_ge(evs[name].sem, evs[name].at(emptied(gi, name)))
                        for s in columns[gi + 2]:
                            side.columns(pe, s, [4 * (gi % 2) + j for j in range(4)])

            @block.gpsimd
            def _(pool):
                if side:
                    side.load(pool)

            @block.vector
            def _(dve):
                for gi, g in enumerate(groups):
                    for s in sums[gi]:
                        side.sum_rows(dve, s)
                    if "vector" in g["evac"]:
                        dve.wait_ge(used.sem, used.at(ends[gi] - first))
                        if g.get("vector_after_scalar"):
                            dve.wait_ge(evs["scalar"].sem, evs["scalar"].at(emptied(gi, "scalar")))
                        g["evac"]["vector"](dve, banks(gi)).then_inc(evs["vector"].sem, 1)
                if side:
                    side.finish(dve)

            @block.scalar
            def _(act):
                for dst, src in loads:
                    act.dma_start(dst, src).then_inc(landed.sem, 16)
                for gi, g in enumerate(groups):
                    if "scalar" in g["evac"]:
                        act.wait_ge(used.sem, used.at(ends[gi] - first))
                        if g.get("scalar_after_vector"):
                            act.wait_ge(evs["vector"].sem, evs["vector"].at(emptied(gi - 1, "vector")))
                        g["evac"]["scalar"](act, banks(gi)).then_inc(evs["scalar"].sem, 1)
                if loads:
                    act.wait_ge(landed.sem, landed.at(16 * len(loads)))

        landed.advance(16 * len(loads))
        if side:
            side.close()
        n = len(groups)
        for name, s in evs.items():
            s.advance(emptied(n - 1, name))
        used.advance(end - first)
        self.taken = end

    def transpose_in(self, jobs):
        nc = self.nc
        landed, turned, moved = self.counted("rows_landed"), self.counted("rows_turned"), self.counted("turned_moved")
        n = len(jobs)
        rows = self.arena.take("rows", n, 2, D)
        ident = self.tab("ident")
        with nc.Block() as block:
            @block.sync
            def _(sync):
                for i, (src, _) in enumerate(jobs):
                    sync.dma_start(rows[:, i], src.rearrange("(t p) d -> p t d", p=P)).then_inc(landed.sem, 16)
                self.load_weights(sync, 0)

            @block.tensor
            def _(pe):
                pe.wait_ge(landed.sem, landed.at(16 * n))
                for i in range(n):
                    for k in range(DT):
                        step = i * DT + k
                        if step >= 8:
                            pe.wait_ge(moved.sem, moved.at(step - 7))
                        for t in range(2):
                            last = nc.tensor.transpose(self.bank[step % 8][:, t * P:(t + 1) * P], rows[:, i, t, k * P:(k + 1) * P], ident)
                        last.then_inc(turned.sem, 1)

            @block.vector
            def _(dve):
                for i, (_, dst) in enumerate(jobs):
                    for k in range(DT):
                        step = i * DT + k
                        dve.wait_ge(turned.sem, turned.at(step + 1))
                        nc.vector.tensor_copy(dst[:, k, :], self.bank[step % 8][:, 0:SEQ]).then_inc(moved.sem, 1)
        landed.advance(16 * n)
        turned.advance(n * DT)
        moved.advance(n * DT)
        self.arena.free("rows")

    def rmsnorm(self, src, n_tiles, tokens, parts, eps=EPS):
        nc = self.nc
        squared, summed = self.counted("squared"), self.counted("squares_summed")
        chain, scaled, shifted = self.counted("mean_ready"), self.counted("scaled"), self.counted("shifted")
        rooted = self.counted("rooted")
        sq = self.arena.take("sq", 2, tokens)
        rstd = self.arena.take("rstd", tokens)
        n = len(parts) * n_tiles
        with nc.Block() as block:
            @block.scalar
            def _(act):
                for k in range(n_tiles):
                    if k >= 2:
                        act.wait_ge(summed.sem, summed.at(k - 1))
                    nc.scalar.activation(sq[:, k % 2], src(k), ACT.Square).then_inc(squared.sem, 1)
                act.wait_ge(chain.sem, chain.at(2))
                nc.scalar.activation(rstd, rstd, ACT.Sqrt).then_inc(rooted.sem, 1)
                i = 0
                for _, dst, _, shift in parts:
                    for k in range(n_tiles):
                        i += 1
                        if shift is not None:
                            act.wait_ge(scaled.sem, scaled.at(i))
                            nc.scalar.activation(dst(k), dst(k), ACT.Identity, bias=shift(k)).then_inc(shifted.sem, 1)

            @block.tensor
            def _(pe):
                for k in range(n_tiles):
                    pe.wait_ge(squared.sem, squared.at(k + 1))
                    nc.tensor.matmul(self.bank[0][:, 0:tokens], self.tab("ones"), sq[:, k % 2], start=k == 0,
                                     stop=k == n_tiles - 1).then_inc(summed.sem, 1)

            @block.vector
            def _(dve):
                dve.wait_ge(summed.sem, summed.at(n_tiles))
                nc.vector.tensor_scalar(rstd, self.bank[0][:, 0:tokens], 1.0 / (n_tiles * P), eps, ALU.mult, ALU.add).then_inc(chain.sem, 1)
                dve.wait_ge(chain.sem, chain.at(1))
                dve.wait_ge(chain.sem, chain.at(1))
                nc.vector.reciprocal(rstd, rstd).then_inc(chain.sem, 1)
                dve.wait_ge(rooted.sem, rooted.at(1))
                for sl, dst, scale, _ in parts:
                    for k in range(n_tiles):
                        nc.vector.scalar_tensor_tensor(dst(k), src(k)[:, sl], scale(k), rstd[:, sl], ALU.mult, ALU.mult).then_inc(scaled.sem, 1)
        squared.advance(n_tiles)
        summed.advance(n_tiles)
        chain.advance(2)
        rooted.advance(1)
        scaled.advance(n)
        shifted.advance(sum(n_tiles for p in parts if p[3] is not None))
        self.arena.free("sq", "rstd")

    def attention(self, units, flip=None, beside=()):
        nc = self.nc
        scored, probs_ready = self.counted("scores_ready"), self.counted("probs_ready")
        dstep, expd, turned, tmoved = self.counted("softmax_step"), self.counted("exp_done"), self.counted("probs_turned"), self.counted("probsT_ready")
        mixed, outm, biased = self.counted("values_mixed"), self.counted("mixed_moved"), self.counted("max_ready")
        keys = max(u["k"][0].shape[-1] for u in units)
        pr = self.arena.take("pr", 2, keys)
        pt = self.arena.take("pt", 2, keys)
        st = self.arena.take("st", 2, 4)
        ident = self.tab("ident")
        S = self.bank[0:3]
        PT = self.bank[3:6]
        O = self.bank[6:8]
        n = len(units)
        with nc.Block() as block:
            @block.tensor
            def _(pe):
                def scores(i):
                    u = units[i]
                    nk = u["k"][0].shape[-1]
                    if i >= 3:
                        pe.wait_ge(expd.sem, expd.at(i - 2))
                    for b in range(len(u["q"])):
                        last = nc.tensor.matmul(S[i % 3][:, 0:nk], u["q"][b], u["k"][b], start=b == 0,
                                                stop=u["bias"] is None and b == len(u["q"]) - 1)
                    if u["bias"] is not None:
                        last = nc.tensor.matmul(S[i % 3][:, nk - u["bias"].shape[-1]:nk], flip, u["bias"], start=False, stop=True)
                    last.then_inc(scored.sem, 1)

                def mix(i):
                    u = units[i]
                    nkt = u["k"][0].shape[-1] // P
                    pe.wait_ge(tmoved.sem, tmoved.at(i + 1))
                    if i >= 2:
                        pe.wait_ge(outm.sem, outm.at(i - 1))
                    hw = u["v"][0].shape[-1]
                    a = u["out_part"]
                    for b in range(-(-hw // P)):
                        w = min(P, hw)
                        for t in range(nkt):
                            last = nc.tensor.matmul(O[i % 2][a:a + w, b * P:(b + 1) * P], u["v"][t][:, b * P:b * P + w],
                                                    pt[:, i % 2, t * P:(t + 1) * P], start=t == 0, stop=t == nkt - 1)
                    last.then_inc(mixed.sem, 1)

                scores(0)
                if n > 1:
                    scores(1)
                for i, u in enumerate(units):
                    if i + 2 < n:
                        scores(i + 2)
                    nkt = u["k"][0].shape[-1] // P
                    pe.wait_ge(probs_ready.sem, probs_ready.at(i + 1))
                    if i >= 3:
                        pe.wait_ge(tmoved.sem, tmoved.at(i - 2))
                    for t in range(nkt):
                        last = nc.tensor.transpose(PT[i % 3][:, t * P:(t + 1) * P], pr[:, i % 2, t * P:(t + 1) * P], ident)
                    last.then_inc(turned.sem, 1)
                    if i >= 1:
                        mix(i - 1)
                mix(n - 1)

            @block.vector
            def _(dve):
                c = 0

                def head(i):
                    u = units[i]
                    nk = u["k"][0].shape[-1]
                    dve.wait_ge(scored.sem, scored.at(i + 1))
                    if i >= 2:
                        dve.wait_ge(probs_ready.sem, probs_ready.at(i - 1))
                    nc.vector.tensor_reduce(st[:, i % 2, 0:1], S[i % 3][:, 0:nk], AX_X, ALU.max, negate=True).then_inc(biased.sem, 1)

                def tail(i):
                    nonlocal c
                    u = units[i]
                    e = pr[:, i % 2, 0:u["k"][0].shape[-1]]
                    den = st[:, i % 2, 1:2]
                    dve.wait_ge(expd.sem, expd.at(i + 1))
                    if u["count"] is not None:
                        nc.vector.scalar_tensor_tensor(e, e, 1.0, u["count"], ALU.mult, ALU.mult, accum_out=den).then_inc(dstep.sem, 1)
                        c += 1
                        dve.wait_ge(dstep.sem, dstep.at(c))
                    nc.vector.reciprocal(st[:, i % 2, 3:4], den).then_inc(dstep.sem, 1)
                    c += 1
                    dve.wait_ge(dstep.sem, dstep.at(c))
                    nc.vector.tensor_scalar(e, e, st[:, i % 2, 3:4], None, ALU.mult).then_inc(probs_ready.sem, 1)

                def move_out(i):
                    u = units[i]
                    dve.wait_ge(mixed.sem, mixed.at(i + 1))
                    a, w = u["out_part"], min(P, u["v"][0].shape[-1])
                    for b, o in enumerate(u["out"]):
                        last = nc.vector.tensor_copy(o, O[i % 2][a:a + w, b * P:(b + 1) * P])
                    last.then_inc(outm.sem, 1)

                head(0)
                for i in range(n):
                    if i + 1 < n:
                        head(i + 1)
                    tail(i)
                    if i >= 2:
                        move_out(i - 2)
                    for b in range(i * len(beside) // n, (i + 1) * len(beside) // n):
                        beside[b](dve)
                for i in range(n - 2, n):
                    move_out(i)
                dstep.count = c

            @block.scalar
            def _(act):
                def exponent(i):
                    u = units[i]
                    nk = u["k"][0].shape[-1]
                    act.wait_ge(biased.sem, biased.at(i + 1))
                    if i >= 2:
                        act.wait_ge(turned.sem, turned.at(i - 1))
                    nc.scalar.activation(pr[:, i % 2, 0:nk], S[i % 3][:, 0:nk], ACT.Exp, bias=st[:, i % 2, 0:1],
                                         accum_out=st[:, i % 2, 1:2]).then_inc(expd.sem, 1)

                exponent(0)
                for i, u in enumerate(units):
                    if i + 1 < n:
                        exponent(i + 1)
                    nk = u["k"][0].shape[-1]
                    act.wait_ge(turned.sem, turned.at(i + 1))
                    if i >= 2:
                        act.wait_ge(mixed.sem, mixed.at(i - 1))
                    nc.scalar.activation(pt[:, i % 2, 0:nk], PT[i % 3][:, 0:nk], ACT.Copy).then_inc(tmoved.sem, 1)
        for s in (scored, probs_ready, expd, turned, tmoved, mixed, outm, biased):
            s.advance(n)
        dstep.advance(dstep.count)
        self.arena.free("pr", "pt", "st")

    def load(self, pairs):
        nc = self.nc
        landed = self.counted("loads_landed")
        with nc.Block() as block:
            @block.sync
            def _(sync):
                for dst, src in pairs:
                    sync.dma_start(dst, src).then_inc(landed.sem, 16)
                sync.wait_ge(landed.sem, landed.at(16 * len(pairs)))
        landed.advance(16 * len(pairs))

    def load_vectors(self, specs):
        nc = self.nc
        groups, at = 0, 0
        places = []
        for name, src in specs:
            n = src.shape[0]
            if at % P + n > P:
                at += P - at % P
            places.append((name, src, at, n))
            self.vec[name] = at
            at += n
        groups = -(-at // P)
        self.vectors = self.arena.take("vectors", groups * P)
        rows = self.arena.take("vector_rows", groups, P)
        odd_landed = self.counted("odd_vectors_landed")
        cleared, landed, turned = self.counted("rows_cleared"), self.counted("loads_landed"), self.counted("rows_turned")
        with nc.Block() as block:
            @block.vector
            def _(dve):
                nc.vector.memset(rows, 0.0).then_inc(cleared.sem, 1)
                dve.wait_ge(turned.sem, turned.at(groups))
                for g in range(groups):
                    nc.vector.tensor_copy(self.vectors[:, g * P:(g + 1) * P], self.bank[g][:, 0:P])

            @block.scalar
            def _(act):
                act.dma_start(self.table[:, :], self.ins["tables"][:, 0:RESIDENT_COLS]).then_inc(landed.sem, 16)
                act.wait_ge(cleared.sem, cleared.at(1))
                for _, src, a, n in places[0::2]:
                    act.dma_start(rows[a % P:a % P + n, a // P, :], src).then_inc(landed.sem, 16)

            @block.gpsimd
            def _(pool):
                pool.wait_ge(cleared.sem, cleared.at(1))
                for _, src, a, n in places[1::2]:
                    pool.dma_start(rows[a % P:a % P + n, a // P, :], src).then_inc(odd_landed.sem, 16)

            @block.sync
            def _(sync):
                self.load_weights(sync, 0)

            @block.tensor
            def _(pe):
                pe.wait_ge(landed.sem, landed.at(16 * (len(places[0::2]) + 1)))
                pe.wait_ge(odd_landed.sem, odd_landed.at(16 * len(places[1::2])))
                for g in range(groups):
                    nc.tensor.transpose(self.bank[g][:, 0:P], rows[:, g, :], self.tab("ident")).then_inc(turned.sem, 1)
        cleared.advance(1)
        landed.advance(16 * (len(places[0::2]) + 1))
        odd_landed.advance(16 * len(places[1::2]))
        turned.advance(groups)
        self.arena.free("vector_rows")

    def col(self, name, i=0):
        a = self.vec[name] + i
        return self.vectors[:, a:a + 1]

    def cols(self, name, n, i=0):
        a = self.vec[name] + i
        return self.vectors[:, a:a + n]

    def bias_lines(self):
        nc, ins = self.nc, self.ins
        self.bias_dram = nc.dram_tensor("bias_lines", (16, T2), F32, kind="Internal")
        self.rpb_dram = nc.dram_tensor("rpb_lines", (2 * 8 * 15, 127), F32, kind="Internal")
        tabs = self.arena.take("buckets", 2, T2)
        rb = self.arena.take("rel_bias", 16)
        lines = self.arena.take("lines", 2, T2)
        zero = self.arena.take("zero", 254)
        ready, landed, made, moved, stored = (self.counted(n) for n in
                                              ("rel_bias_cleared", "loads_landed", "lines_made", "lines_moved", "lines_stored"))
        n_load = 2
        with nc.Block() as block:
            @block.vector
            def _(dve):
                nc.vector.memset(rb[0:64, :], NEG).then_inc(ready.sem, 1)
                nc.vector.memset(zero, 0.0).then_inc(ready.sem, 1)
                dve.wait_ge(made.sem, made.at(2))
                nc.vector.tensor_copy(lines[0:8, 0], self.bank[0][0:8, :]).then_inc(moved.sem, 1)
                nc.vector.tensor_copy(lines[0:8, 1], self.bank[1][0:8, :]).then_inc(moved.sem, 1)

            @block.sync
            def _(sync):
                sync.dma_start(tabs.rearrange("p a b -> p (a b)"), self.table_src("bucket_dil", "bucket_moba")).then_inc(landed.sem, 16)
                sync.wait_ge(ready.sem, ready.at(2))
                sync.dma_start(rb[0:N_BUCKETS, :], ins["rel_bias"].rearrange("h b -> b h"), allow_slow_non_contiguous=True).then_inc(landed.sem, 16)
                n = 2 * 8 * 15
                sync.dma_start(bass.AP(self.rpb_dram, 0, [[254, n // 2], [1, 254]]), zero[0:n // 2, :]).then_inc(stored.sem, 16)
                sync.wait_ge(stored.sem, stored.at(16))
                sync.dma_start(self.rpb_dram.ap()[:, 48:79], ins["na_rpb_2"].rearrange("l h r c -> (l h r) c")).then_inc(stored.sem, 16)
                sync.wait_ge(moved.sem, moved.at(2))
                for i in range(2):
                    sync.dma_start(self.bias_dram.ap()[8 * i:8 * i + 8, :], lines[0:8, i]).then_inc(stored.sem, 16)
                sync.wait_ge(stored.sem, stored.at(64))

            @block.tensor
            def _(pe):
                pe.wait_ge(landed.sem, landed.at(32))
                for i in range(2):
                    nc.tensor.matmul(self.bank[i][0:8, :], rb[0:N_BUCKETS + 1, 8 * i:8 * i + 8], tabs[0:N_BUCKETS + 1, i],
                                     start=True, stop=True).then_inc(made.sem, 1)
        ready.advance(2)
        landed.advance(32)
        made.advance(2)
        moved.advance(2)
        stored.advance(64)
        self.arena.free("buckets", "rel_bias", "lines", "zero")

    def copy_f(self, dst, j0, sl=BOTH, scale=None):
        def fn(eng, banks):
            for j in range(4):
                if scale is None:
                    last = self.nc.vector.tensor_copy(dst(j0 + j), banks[j][:, sl])
                else:
                    last = self.nc.vector.tensor_scalar(dst(j0 + j), banks[j][:, sl], scale, None, ALU.mult)
            return last
        return fn

    def residual(self, group, sl, gates=None):
        def fn(eng, banks):
            for j in range(4):
                t = 4 * group + j
                if gates is None:
                    last = self.nc.vector.tensor_tensor(self.xT[:, t, sl], banks[j][:, 0:sl.stop - sl.start], self.xT[:, t, sl], ALU.add)
                else:
                    for tok, column in gates:
                        src = banks[j][:, tok.start - sl.start:tok.stop - sl.start]
                        last = self.nc.vector.scalar_tensor_tensor(self.xT[:, t, tok], src, column(t), self.xT[:, t, tok], ALU.mult, ALU.add)
            return last
        return fn

    def conditioning(self):
        nc = self.nc
        self.mod = [self.smallcols(96).rearrange("p (j c) -> p j c", c=2) for _ in range(2)]
        self.cs = self.smallcols(2 * DT).rearrange("p (k c) -> p k c", c=2)
        self.keep = self.smallcols(20)
        step = self.counted("keep_step")
        with nc.Block() as block:
            @block.scalar
            def _(act):
                nc.scalar.activation(self.cs[:, :, 0], self.cols("c", DT), ACT.Silu)
                nc.scalar.activation(self.cs[:, :, 1], self.cols("c_ctx", DT), ACT.Silu)

            @block.vector
            def _(dve):
                for l in range(2):
                    last = nc.vector.tensor_tensor(self.keep[:, 10 * l:10 * l + 10], self.cols(f"mu_prev{l}", 10), self.cols(f"mu_next{l}", 10), ALU.add)
                last.then_inc(step.sem, 1)
                dve.wait_ge(step.sem, step.at(1))
                nc.vector.tensor_scalar(self.keep, self.keep, -1.0, 1.0, ALU.mult, ALU.add)
        step.advance(1)

    def block_one(self):
        nc, ins, ar = self.nc, self.ins, self.arena
        xT, hT = self.xT, self.hT
        x = lambda k: xT[:, k, LAT]
        h = lambda k: hT[:, k, LAT]
        memT = ar.take("memT", DT, SEQ)
        self.transpose_in([(ins["x"][0], xT[:, :, LAT]), (ins["mem"][0], memT), (ins["ctx_2"][0], xT[:, :, CTX])])

        bias = ar.take("bias", 16, 2, SEQ)
        count = ar.take("count", 2, SEQ)
        loads = [(count.rearrange("p a b -> p (a b)"), self.table_src("count"))]
        for hd in range(16):
            loads.append((bias[:, hd], bass.AP(self.bias_dram, hd * T2, [[1, P], [P, 2], [1, SEQ]])))
        flip = ar.take("flip", P)
        loads.append((flip, self.table_src("flip")))

        self.rmsnorm(x, DT, SEQ, [(slice(0, SEQ), h, lambda k: self.col("g_mix", k), None)])
        qk = ar.take("qk", 16, SEQ)
        v = ar.take("v", 2, D)

        def v_evac(c):
            def fn(eng, banks):
                for t in range(2):
                    last = nc.vector.tensor_copy(v[:, t, c:c + 512], banks[t][:, :])
                return last
            return fn

        F = lambda rows, act, evac, **kw: dict(kind="F", rows=rows, act=act, evac=evac, **kw)
        T = lambda rows, act, evac, **kw: dict(kind="T", rows=rows, act=act, evac=evac, **kw)
        at = lambda a: (lambda j: a[:, j])
        half = slice(0, SEQ)
        self.linear([F(D, h, {"vector": self.copy_f(at(qk), 0, half, HD ** -0.5)}), F(D, h, {"vector": self.copy_f(at(qk), 4, half)}),
                     T(D, h, {"vector": v_evac(0)}),
                     F(D, h, {"vector": self.copy_f(at(qk), 8, half, HD ** -0.5)}), F(D, h, {"vector": self.copy_f(at(qk), 12, half)}),
                     T(D, h, {"vector": v_evac(512)})], loads=loads)
        y = ar.take("y", DT, SEQ)
        units = []
        for hd in range(16):
            g, a = 8 * (hd // 8), (hd % 2) * HD
            ft = (hd % 8) // 2
            for i in range(2):
                tq = slice(i * P, (i + 1) * P)
                units.append(dict(q=[qk[a:a + HD, g + ft, tq]], k=[qk[a:a + HD, g + 4 + ft, :]],
                                  v=[v[:, t, hd * HD:(hd + 1) * HD] for t in range(2)],
                                  out=[y[a:a + HD, hd // 2, tq]], out_part=a, bias=bias[:, hd, 1 - i],
                                  count=count[:, i] if hd < 8 else None))
        self.attention(units, flip)
        ar.free("bias", "count", "qk", "v", "flip")
        half_w = DT // 2
        for n, name in enumerate(("g_out_dil", "g_out_moba")):
            self.rmsnorm(lambda k: y[:, n * half_w + k], half_w, SEQ,
                         [(slice(0, SEQ), lambda k: h(n * half_w + k), lambda k: self.col(name, k), None)])
        ar.free("y")
        self.linear([F(D, h, {"vector": self.residual(g, LAT)}) for g in range(2)])

        self.rmsnorm(x, DT, SEQ, [(slice(0, SEQ), h, lambda k: self.col("g_cross", k), None)])
        self.rmsnorm(at(memT), DT, SEQ, [(slice(0, SEQ), at(memT), lambda k: self.col("g_mem", k), None)])
        q, km, v = ar.take("q", DT, SEQ), ar.take("km", DT, SEQ), ar.take("v", 2, D)
        self.linear([T(D, at(memT), {"vector": v_evac(0)}), T(D, at(memT), {"vector": v_evac(512)}),
                     F(D, h, {"vector": self.copy_f(at(q), 0, half, 256 ** -0.5)}), F(D, h, {"vector": self.copy_f(at(q), 4, half, 256 ** -0.5)}),
                     F(D, at(memT), {"vector": self.copy_f(at(km), 0, half)}), F(D, at(memT), {"vector": self.copy_f(at(km), 4, half)})],
                    side=SideProduct(self, 1, 0, 6))
        units = []
        for hd in range(4):
            for i in range(2):
                tq = slice(i * P, (i + 1) * P)
                units.append(dict(q=[q[:, 2 * hd + b, tq] for b in range(2)], k=[km[:, 2 * hd + b] for b in range(2)],
                                  v=[v[:, t, hd * 256:(hd + 1) * 256] for t in range(2)],
                                  out=[hT[:, 2 * hd + b, SEQ + i * P:SEQ + (i + 1) * P] for b in range(2)],
                                  out_part=0, bias=None, count=None))
        self.attention(units)
        ar.free("q", "km", "v", "memT")
        self.linear([F(D, h, {"vector": self.residual(g, LAT)}) for g in range(2)])

        self.rmsnorm(x, DT, SEQ, [(slice(0, SEQ), h, lambda k: self.col("g_ffn", k), None)])
        hidden = ar.take("hidden", D_FF // P, SEQ)
        conv = self.counted("conv_step")
        n_conv = 0

        def conv_evac(j0, n):
            def fn(dve, banks):
                nonlocal n_conv
                for tap in (2, 1, 0):
                    lag = 2 - tap
                    for j in range(n):
                        w = self.col(f"conv_w{tap}", j0 + j)
                        if lag == 0:
                            last = nc.vector.tensor_scalar(hidden[:, j0 + j], banks[j][:, 0:SEQ], w, None, ALU.mult)
                        else:
                            last = nc.vector.scalar_tensor_tensor(hidden[:, j0 + j, lag:SEQ], banks[j][:, 0:SEQ - lag], w,
                                                                  hidden[:, j0 + j, lag:SEQ], ALU.mult, ALU.add)
                    if lag < 2:
                        last.then_inc(conv.sem, 1)
                        n_conv += 1
                        dve.wait_ge(conv.sem, conv.at(n_conv))
                return last
            return fn

        def silu_evac(j0, n):
            def fn(act, banks):
                for j in range(j0, j0 + n):
                    last = nc.scalar.activation(hidden[:, j], hidden[:, j], ACT.Silu, bias=self.col("conv_b", j))
                return last
            return fn

        def up_evac(j0, n):
            def fn(dve, banks):
                for j in range(n):
                    last = nc.vector.tensor_tensor(hidden[:, j0 + j], banks[j][:, 0:SEQ], hidden[:, j0 + j], ALU.mult)
                return last
            return fn

        groups = []
        for j0 in range(0, D_FF // P, 4):
            n = min(4, D_FF // P - j0)
            groups.append(F(D, h, {"vector": conv_evac(j0, n)}))
            groups.append(F(D, h, {"scalar": silu_evac(j0, n), "vector": up_evac(j0, n)}, scalar_after_vector=True, vector_after_scalar=True))
        self.linear(groups, side=SideProduct(self, 0, 0, 8))
        conv.advance(n_conv)
        self.linear([F(D_FF, at(hidden), {"vector": self.residual(g, LAT)}) for g in range(2)], side=SideProduct(self, 0, 8, 4))
        ar.free("hidden")
        self.rmsnorm(x, DT, SEQ, [(slice(0, SEQ), x, lambda k: self.col("g_final", k), None)])

    def norm_gains(self, layer):
        nc, mod = self.nc, self.mod[layer]
        gain = self.smallcols(32).rearrange("p (n k c) -> p n k c", n=2, c=2)
        with nc.Block() as block:
            @block.vector
            def _(dve):
                for n in range(2):
                    for k in range(DT):
                        g = self.col(f"norm{n + 1}_g{layer}", k)
                        nc.vector.tensor_scalar(gain[:, n, k, :], mod[:, (3 * n + 1) * DT + k, :], 1.0, g, ALU.add, ALU.mult)
        return mod, gain

    def modulated_norm(self, mod, gain, n, ctx):
        parts, base, tokens = [], 0, T2
        if not ctx:
            base, tokens = SEQ, SEQ
        for c, sl in ((1, CTX), (0, LAT)):
            if c == 1 and not ctx:
                continue
            parts.append((slice(sl.start - base, sl.stop - base), lambda k, sl=sl: self.hT[:, k, sl],
                          lambda k, c=c: gain[:, n, k, c:c + 1], lambda k, c=c: mod[:, 3 * n * DT + k, c:c + 1]))
        self.rmsnorm(lambda k: self.xT[:, k, base:T2], DT, tokens, parts)

    def rwkv_loads(self, layer):
        ar, ins = self.arena, self.ins
        restart = ar.take("restart", T2)
        w2a2 = ar.take("w2a2", 2, RW_WIDTH)
        g2 = ar.take("g2", 2, RW_WIDTH)
        causal = ar.take("causal", 2, 2 * P)
        levels = ar.take("levels", 2, 6, P)
        loads = [(restart, self.table_src("restart")),
                 (w2a2[0:HD], ins["rw_w2_2"][layer].rearrange("d r n -> r d n")),
                 (w2a2[HD:P], ins["rw_a2_2"][layer].rearrange("d r n -> r d n")),
                 (g2, ins["rw_g2_2"][layer].rearrange("d r n -> r d n"))]
        for d in range(2):
            loads.append((causal[:, d], self.table_src(f"causal{d}")))
            loads.append((levels[:, d].rearrange("p a b -> p (a b)"), self.table_src(f"level{d}_0", f"level{d}_5")))
        return (restart, w2a2, g2, causal, levels), loads

    def rwkv(self, rwpad, layer, tables):
        nc, ar, ins = self.nc, self.arena, self.ins
        restart, w2a2, g2 = tables[0:3]
        sh = ar.take("sh", 10, T2)
        kept, step = self.counted("shift_kept"), self.counted("shift_step")
        with nc.Block() as block:
            @block.scalar
            def _(act):
                for j in range(10):
                    nc.scalar.activation(sh[:, j, :].rearrange("p (s t) -> p s t", s=2), rwpad[:, j, :, 1:SEQ + 1], ACT.Copy,
                                         scale=self.keep[:, 10 * layer + j:10 * layer + j + 1]).then_inc(kept.sem, 1)

            @block.vector
            def _(dve):
                for j in range(10):
                    s = sh[:, j, :].rearrange("p (s t) -> p s t", s=2)
                    dve.wait_ge(kept.sem, kept.at(j + 1))
                    nc.vector.scalar_tensor_tensor(s, rwpad[:, j, :, 0:SEQ], self.col(f"mu_prev{layer}", j), s, ALU.mult, ALU.add).then_inc(step.sem, 1)
                    dve.wait_ge(step.sem, step.at(j + 1))
                    nc.vector.scalar_tensor_tensor(s, rwpad[:, j, :, 2:SEQ + 2], self.col(f"mu_next{layer}", j), s, ALU.mult, ALU.add)
        kept.advance(10)
        step.advance(10)
        ar.free("rwpad")
        r, k, v = sh[:, 0:2], sh[:, 2:4], sh[:, 4:6]

        kk = ar.take("kk", 2, T2)
        sq = ar.take("sq", 2, T2)
        vtok = ar.take("vtok", 4, RW_WIDTH)
        step, summed, turned = self.counted("kk_step"), self.counted("kk_summed"), self.counted("v_turned")
        rooted = self.counted("rooted")
        with nc.Block() as block:
            @block.vector
            def _(dve):
                for f in range(2):
                    nc.vector.tensor_scalar(kk[:, f], k[:, f], self.col(f"k_k{layer}", f), None, ALU.mult).then_inc(step.sem, 1)
                dve.wait_ge(step.sem, step.at(2))
                nc.vector.tensor_tensor(sq, kk, kk, ALU.mult).then_inc(step.sem, 1)
                dve.wait_ge(summed.sem, summed.at(2))
                for f in range(2):
                    nc.vector.tensor_scalar(sq[:, f], self.bank[f], 1e-12, None, ALU.add).then_inc(step.sem, 1)
                dve.wait_ge(step.sem, step.at(5))
                nc.vector.reciprocal(sq, sq).then_inc(step.sem, 1)
                dve.wait_ge(rooted.sem, rooted.at(1))
                nc.vector.tensor_tensor(kk, kk, sq, ALU.mult)

            @block.tensor
            def _(pe):
                for t in range(4):
                    for f in range(2):
                        last = nc.tensor.transpose(self.bank[4 + t][:, f * P:(f + 1) * P], v[:, f, t * P:(t + 1) * P], self.tab("ident"))
                    last.then_inc(turned.sem, 1)
                pe.wait_ge(step.sem, step.at(3))
                for f in range(2):
                    nc.tensor.matmul(self.bank[f], self.tab("headones"), sq[:, f], start=True, stop=True).then_inc(summed.sem, 1)

            @block.scalar
            def _(act):
                for t in range(4):
                    act.wait_ge(turned.sem, turned.at(t + 1))
                    nc.scalar.activation(vtok[:, t], self.bank[4 + t][:, 0:RW_WIDTH], ACT.Copy)
                act.wait_ge(step.sem, step.at(6))
                nc.scalar.activation(sq, sq, ACT.Sqrt).then_inc(rooted.sem, 1)
        step.advance(6)
        rooted.advance(1)
        summed.advance(2)
        turned.advance(4)
        ar.free("sq")

        zr, bm, km, gate, pc = self.rwkv_factors(layer, sh, kk, restart, w2a2, g2)
        ar.free("sh", "kk", "restart", "w2a2", "g2")
        ytok = self.rwkv_scan(zr, bm, km, pc, vtok, *tables[3:5])
        ar.free("zr0", "zr1", "bm0", "bm1", "km0", "km1", "pc0", "pc1", "vtok")
        self.rwkv_out(layer, ytok, gate)
        ar.free("ytok", "gate0", "gate1")

    def rwkv_factors(self, layer, sh, kk, restart, w2a2, g2):
        nc, ar = self.nc, self.arena
        r, k, v = sh[:, 0:2], sh[:, 2:4], sh[:, 4:6]
        both = range(2)
        zr = [ar.take(f"zr{d}", 2, 2, T2) for d in both]
        bm, km, gate = ([ar.take(f"{n}{d}", 2, T2) for d in both] for n in ("bm", "km", "gate"))
        pc = [ar.take(f"pc{d}", 2, T2 // CHUNK) for d in both]
        ld, L, a = ([ar.take(f"{n}{d}", 2, T2) for d in both] for n in ("ld", "L", "a"))
        lora, ranked, opened = self.counted("lora_ready"), self.counted("lora_summed"), self.counted("lora_opened")
        gated = self.counted("gates_moved")
        st, ex, bs = self.counted("factor_step"), self.counted("factor_exp"), self.counted("bonus_summed")
        n_chunk = T2 // CHUNK
        per_chunk = lambda x: x.rearrange("p (c t) -> p c t", t=CHUNK)
        decay_b, a_b, gate_b, bonus_b = (0, 6), (2, 0), (4, 2), (4, 6)
        with nc.Block() as block:
            @block.scalar
            def _(act):
                for d in both:
                    nc.scalar.activation(sh[0:HD, 6 + 2 * d], sh[0:HD, 6 + 2 * d], ACT.Tanh)
                    nc.scalar.activation(sh[:, 7 + 2 * d], sh[:, 7 + 2 * d], ACT.Sigmoid).then_inc(lora.sem, 1)
                for d in both:
                    act.wait_ge(ranked.sem, ranked.at(d + 1))
                    for f in range(2):
                        nc.scalar.activation(ld[d][:, f], self.bank[decay_b[d] + f], ACT.Sigmoid, bias=self.col(f"w0{layer}", 2 * d + f))
                        last = nc.scalar.activation(a[d][:, f], self.bank[a_b[d] + f], ACT.Sigmoid, bias=self.col(f"a0{layer}", 2 * d + f))
                    last.then_inc(opened.sem, 1)
                    for f in range(2):
                        last = nc.scalar.activation(gate[d][:, f], self.bank[gate_b[d] + f], ACT.Copy)
                    last.then_inc(gated.sem, 1)
                for d in both:
                    act.wait_ge(st.sem, st.at(3 if d == 0 else 6))
                    nc.scalar.activation(bm[d], L[d], ACT.Exp)
                    nc.scalar.activation(ld[d], ld[d], ACT.Exp).then_inc(ex.sem, 1)
                for d in both:
                    nc.scalar.activation(L[d], L[d], ACT.Exp, scale=-1.0).then_inc(ex.sem, 1)
                for d in both:
                    nc.scalar.activation(pc[d], pc[d], ACT.Exp)

            @block.tensor
            def _(pe):
                for d in both:
                    pe.wait_ge(lora.sem, lora.at(d + 1))
                    lo = 6 + 2 * d
                    for f in range(2):
                        nc.tensor.matmul(self.bank[decay_b[d] + f], w2a2[0:HD, d, f * P:(f + 1) * P], sh[0:HD, lo], start=True, stop=True)
                    if d == 1:
                        pe.wait_ge(opened.sem, opened.at(1))
                    for f in range(2):
                        nc.tensor.matmul(self.bank[a_b[d] + f], w2a2[HD:P, d, f * P:(f + 1) * P], sh[HD:P, lo], start=True, stop=True)
                        last = nc.tensor.matmul(self.bank[gate_b[d] + f], g2[:, d, f * P:(f + 1) * P], sh[:, lo + 1], start=True, stop=True)
                    last.then_inc(ranked.sem, 1)
                pe.wait_ge(gated.sem, gated.at(1))
                pe.wait_ge(st.sem, st.at(11))
                for d in both:
                    for f in range(2):
                        last = nc.tensor.matmul(self.bank[bonus_b[d] + f], self.tab("headones"), a[d][:, f], start=True, stop=True)
                last.then_inc(bs.sem, 1)

            @block.vector
            def _(dve):
                n = 0

                def after(last):
                    nonlocal n
                    last.then_inc(st.sem, 1)
                    n += 1
                    dve.wait_ge(st.sem, st.at(n))

                for d in both:
                    dve.wait_ge(opened.sem, opened.at(d + 1))
                    last = nc.vector.tensor_scalar(ld[d], ld[d], -DECAY_SCALE, None, ALU.mult)
                after(last)
                for d in both:
                    for f in range(2):
                        last = nc.vector.tensor_tensor_scan(L[d][:, f], restart, ld[d][:, f], 0.0, ALU.mult, ALU.add)
                after(last)
                for d in both:
                    for f in range(2):
                        nc.vector.tensor_copy(pc[d][:, f, :], per_chunk(L[d][:, f])[:, :, CHUNK - 1])
                after(nc.vector.tensor_tensor(ld[0], L[0], ld[0], ALU.subtract))
                for f in range(2):
                    last = nc.vector.tensor_tensor(per_chunk(L[1][:, f]), pc[1][:, f, :].unsqueeze(2).to_broadcast([P, n_chunk, CHUNK]),
                                                   per_chunk(L[1][:, f]), ALU.subtract)
                after(last)
                after(nc.vector.tensor_tensor(L[1], L[1], ld[1], ALU.add))
                after(nc.vector.tensor_tensor(ld[1], L[1], ld[1], ALU.subtract))
                for d in both:
                    for f in range(2):
                        last = nc.vector.tensor_scalar(km[d][:, f], a[d][:, f], -1.0, self.col(f"k_a{layer}", f), ALU.add, ALU.mult)
                after(last)
                for d in both:
                    last = nc.vector.scalar_tensor_tensor(km[d], km[d], 1.0, k, ALU.add, ALU.mult)
                after(last)
                for d in both:
                    dve.wait_ge(ex.sem, ex.at(d + 1))
                    nc.vector.tensor_tensor(zr[d][:, :, 1], r, bm[d], ALU.mult)
                    last = nc.vector.scalar_tensor_tensor(zr[d][:, :, 0], kk, -1.0, ld[d], ALU.mult, ALU.mult)
                after(last)
                for d in both:
                    last = nc.vector.tensor_tensor(bm[d], kk, a[d], ALU.mult)
                after(last)
                for d in both:
                    for f in range(2):
                        last = nc.vector.scalar_tensor_tensor(a[d][:, f], r[:, f], self.col(f"r_k{layer}", f), km[d][:, f], ALU.mult, ALU.mult)
                after(last)
                for d in both:
                    dve.wait_ge(ex.sem, ex.at(d + 3))
                    nc.vector.tensor_tensor(bm[d], bm[d], L[d], ALU.mult)
                    last = nc.vector.tensor_tensor(km[d], km[d], L[d], ALU.mult)
                dve.wait_ge(bs.sem, bs.at(1))
                for d in both:
                    for f in range(2):
                        last = nc.vector.tensor_tensor(ld[d][:, f], self.bank[bonus_b[d] + f], v[:, f], ALU.mult)
                after(last)
                dve.wait_ge(gated.sem, gated.at(2))
                out = self.hT[:, 4:6, :]
                nc.vector.tensor_tensor(out, ld[0], gate[0], ALU.mult)
                after(nc.vector.tensor_tensor(ld[1], ld[1], gate[1], ALU.mult))
                nc.vector.tensor_tensor(out, out, ld[1], ALU.add)
                st.n = n
        for q, m in ((lora, 2), (ranked, 2), (opened, 2), (gated, 2), (bs, 1), (ex, 4), (st, st.n)):
            q.advance(m)
        ar.free("ld0", "ld1", "L0", "L1", "a0", "a1")
        return zr, bm, km, gate, pc

    def rwkv_scan(self, zr, bm, km, pc, vtok, causal, levels):
        nc, ar = self.nc, self.arena
        ytok = ar.take("ytok", 2, 4, RW_WIDTH)
        state = ar.take("state", 4, P)
        A = ar.take("A", 8, 4, P)
        X, XT, N, H = (ar.take(n, 8, P) for n in ("X", "XT", "N", "H"))
        btok = ar.take("btok", 4, RW_WIDTH)
        Dm, U = ar.take("Dm", 2, RW_WIDTH), ar.take("U", 2, RW_WIDTH)
        W = ar.take("W", 2, RW_WIDTH)
        decay = ar.take("decay", 4, P)
        ident, headones = self.tab("ident"), self.tab("headones")
        with nc.Block() as block:
            @block.vector
            def _(dve):
                nc.vector.memset(state, 0.0)

        order = ((0, 1, 2, 3), (1, 0, 3, 2))
        for s in range(4):
            tile = (order[0][s], order[1][s])
            tk = [slice(t * P, (t + 1) * P) for t in tile]
            self.rwkv_solve(zr, bm, km, vtok, tile, tk, A, W, btok, X, XT, N, H, causal, levels)

            half = ((0, 1), (1, 0))
            dsum, dmoved, usum, umoved = (self.counted(n) for n in ("d_summed", "d_moved", "u_summed", "u_moved"))
            ysum, ymoved, ssum, smoved = (self.counted(n) for n in ("y_summed", "y_moved", "state_summed", "state_step"))
            dready, csum = self.counted("decay_ready"), self.counted("own_summed")
            with nc.Block() as block:
                @block.gpsimd
                def _(pool):
                    for c in range(2):
                        if c == 1:
                            pool.wait_ge(smoved.sem, smoved.at(1))
                        for d in range(2):
                            ch = 2 * tile[d] + half[d][c]
                            for f in range(2):
                                last = nc.gpsimd.tensor_scalar(decay[:, 2 * d + f], headones, pc[d][:, f, ch:ch + 1], None, ALU.mult)
                        last.then_inc(dready.sem, 1)

                D_, Y_, C_ = (self.bank[i].rearrange("p (d n) -> p d n", d=2) for i in (0, 3, 4))
                U_ = (self.bank[1], self.bank[4])
                S_ = [self.bank[i] for i in (2, 5, 6, 7)]

                @block.tensor
                def _(pe):
                    for c in range(2):
                        hf = [slice(half[d][c] * HD, half[d][c] * HD + HD) for d in range(2)]
                        if c == 1:
                            pe.wait_ge(smoved.sem, smoved.at(1))
                        for d in range(2):
                            for f in range(2):
                                last = nc.tensor.matmul(D_[:, d, f * P:(f + 1) * P], zr[d][:, f, 0, tk[d]], state[:, 2 * d + f], start=True, stop=True)
                        last.then_inc(dsum.sem, 1)
                        for d in range(2):
                            for f in range(2):
                                fc = slice(f * P, (f + 1) * P)
                                nc.tensor.matmul(S_[2 * d + f][:, 0:P], btok[hf[d], 2 * d + 1, fc], vtok[hf[d], tile[d], fc], start=True, stop=False)
                                nc.tensor.matmul(S_[2 * d + f][:, 0:P], ident, state[:, 2 * d + f], start=False, stop=False)
                        pe.wait_ge(dmoved.sem, dmoved.at(c + 1))
                        for d in range(2):
                            for hd in range(4):
                                hc = slice(hd * HD, (hd + 1) * HD)
                                last = nc.tensor.matmul(U_[d][:, hc], XT[hf[d], 4 * d + hd], Dm[hf[d], d, hc], start=True, stop=True)
                        last.then_inc(usum.sem, 1)
                        if c == 1:
                            pe.wait_ge(ymoved.sem, ymoved.at(1))
                        for d in range(2):
                            for f in range(2):
                                last = nc.tensor.matmul(Y_[:, d, f * P:(f + 1) * P], zr[d][:, f, 1, tk[d]], state[:, 2 * d + f], start=True, stop=True)
                        last.then_inc(ysum.sem, 1)
                        pe.wait_ge(umoved.sem, umoved.at(c + 1))
                        for d in range(2):
                            for f in range(2):
                                fc = slice(f * P, (f + 1) * P)
                                last = nc.tensor.matmul(S_[2 * d + f][:, 0:P], btok[hf[d], 2 * d, fc], U[hf[d], d, fc], start=False, stop=True)
                        last.then_inc(ssum.sem, 1)
                    for d in range(2):
                        for hd in range(4):
                            hc = slice(hd * HD, (hd + 1) * HD)
                            nc.tensor.matmul(C_[:, d, hc], A[:, 4 * d + hd, 1], U[:, d, hc], start=True, stop=False)
                            last = nc.tensor.matmul(C_[:, d, hc], A[:, 4 * d + hd, 3], vtok[:, tile[d], hc], start=False, stop=True)
                    last.then_inc(csum.sem, 1)

                @block.vector
                def _(dve):
                    for c in range(2):
                        hf = [slice(half[d][c] * HD, half[d][c] * HD + HD) for d in range(2)]
                        dve.wait_ge(dsum.sem, dsum.at(c + 1))
                        for d in range(2):
                            last = nc.vector.tensor_tensor(Dm[hf[d], d], D_[hf[d], d], W[hf[d], d], ALU.add)
                        last.then_inc(dmoved.sem, 1)
                        dve.wait_ge(usum.sem, usum.at(c + 1))
                        for d in range(2):
                            last = nc.vector.tensor_copy(U[hf[d], d], U_[d][hf[d], 0:RW_WIDTH])
                        last.then_inc(umoved.sem, 1)
                        dve.wait_ge(ssum.sem, ssum.at(c + 1))
                        dve.wait_ge(dready.sem, dready.at(c + 1))
                        for i in range(4):
                            last = nc.vector.tensor_tensor(state[:, i], S_[i][:, 0:P], decay[:, i], ALU.mult)
                        last.then_inc(smoved.sem, 1)
                    dve.wait_ge(csum.sem, csum.at(1))
                    dve.wait_ge(ymoved.sem, ymoved.at(2))
                    for d in range(2):
                        nc.vector.tensor_tensor(ytok[:, d, tile[d]], C_[:, d], ytok[:, d, tile[d]], ALU.add)

                @block.scalar
                def _(act):
                    for c in range(2):
                        act.wait_ge(ysum.sem, ysum.at(c + 1))
                        for d in range(2):
                            hf = slice(half[d][c] * HD, half[d][c] * HD + HD)
                            last = nc.scalar.activation(ytok[hf, d, tile[d]], Y_[hf, d], ACT.Copy)
                        last.then_inc(ymoved.sem, 1)
            for q in (dsum, dmoved, usum, umoved, ysum, ymoved, ssum, smoved, dready):
                q.advance(2)
            csum.advance(1)
        ar.free("causal", "levels", "state", "A", "X", "XT", "N", "H", "btok", "Dm", "U", "decay", "W")
        return ytok

    def rwkv_solve(self, zr, bm, km, vtok, tile, tk, A, W, btok, X, XT, N, H, causal, levels):
        nc = self.nc
        made, masked = self.counted("pairs_made"), self.counted("pairs_masked")
        bkturned, bkmoved, wsum = self.counted("bk_turned"), self.counted("bk_moved"), self.counted("w_summed")
        ident = self.tab("ident")
        picked, turned, hs, hm, xs, xm = (self.counted(n) for n in ("level_picked", "x_turned", "h_summed", "h_moved", "x_summed", "x_added"))
        idb = ident.unsqueeze(1).to_broadcast([P, 4, P])
        bank4 = lambda b: self.bank[b].rearrange("p (h t) -> p h t", h=4)
        with nc.Block() as block:
            @block.gpsimd
            def _(pool):
                for lv in range(6):
                    for d in range(2):
                        if lv == 0:
                            pool.wait_ge(masked.sem, masked.at(4 * d + 4))
                        if lv == 1:
                            pool.wait_ge(turned.sem, turned.at(d + 1))
                            pool.wait_ge(xm.sem, xm.at(2 * d + 1))
                        if lv >= 2:
                            pool.wait_ge(hs.sem, hs.at(2 * (lv - 2) + d + 1))
                        g = slice(4 * d, 4 * d + 4)
                        m = levels[:, d, lv].unsqueeze(1).to_broadcast([P, 4, P])
                        nc.gpsimd.tensor_tensor(N[:, g], A[:, g, 0], m, ALU.mult).then_inc(picked.sem, 1)

            @block.vector
            def _(dve):
                for i in range(8):
                    dve.wait_ge(made.sem, made.at(i + 1))
                    m = causal[:, i // 4].unsqueeze(1).to_broadcast([P, 2, 2 * P])
                    nc.vector.tensor_tensor(A[:, i].rearrange("p (a b) t -> p a (b t)", a=2),
                                            self.bank[i % 4].rearrange("p (a b) -> p a b", a=2), m, ALU.mult).then_inc(masked.sem, 1)
                for d in range(2):
                    g = slice(4 * d, 4 * d + 4)
                    dve.wait_ge(picked.sem, picked.at(d + 1))
                    nc.vector.tensor_tensor(XT[:, g], N[:, g], idb, ALU.add).then_inc(xm.sem, 1)
                    dve.wait_ge(turned.sem, turned.at(d + 1))
                    nc.vector.tensor_tensor(X[:, g], bank4(d), idb, ALU.add).then_inc(xm.sem, 1)
                for lv in range(1, 6):
                    for d in range(2):
                        g = slice(4 * d, 4 * d + 4)
                        dve.wait_ge(xs.sem, xs.at(2 * (lv - 1) + d + 1))
                        nc.vector.tensor_tensor(XT[:, g], bank4(2 + d), XT[:, g], ALU.add).then_inc(xm.sem, 1)
                        if lv < 5:
                            nc.vector.tensor_tensor(X[:, g], bank4(4 + d), X[:, g], ALU.add).then_inc(xm.sem, 1)

            @block.scalar
            def _(act):
                for j in range(4):
                    act.wait_ge(bkturned.sem, bkturned.at(j + 1))
                    nc.scalar.activation(btok[:, j], self.bank[4 + j][:, 0:RW_WIDTH], ACT.Copy).then_inc(bkmoved.sem, 1)
                for i in range(10):
                    d = i % 2
                    if i == 2:
                        act.wait_ge(wsum.sem, wsum.at(1))
                        nc.scalar.activation(W.rearrange("p d n -> p (d n)"), self.bank[0], ACT.Copy)
                    act.wait_ge(hs.sem, hs.at(i + 1))
                    nc.scalar.activation(H[:, 4 * d:4 * d + 4], bank4(6 + d), ACT.Copy).then_inc(hm.sem, 1)

            @block.tensor
            def _(pe):
                for i in range(8):
                    d, hd = i // 4, i % 4
                    f, a = hd // 2, (hd % 2) * HD
                    if i >= 4:
                        pe.wait_ge(masked.sem, masked.at(i - 3))
                    zr_h = zr[d][a:a + HD, f, :, tk[d]]
                    nc.tensor.matmul(self.bank[i % 4][:, 0:2 * P], bm[d][a:a + HD, f, tk[d]], zr_h, start=True, stop=True)
                    nc.tensor.matmul(self.bank[i % 4][:, 2 * P:4 * P], km[d][a:a + HD, f, tk[d]], zr_h, start=True, stop=True).then_inc(made.sem, 1)
                for d in range(2):
                    for i, src in enumerate((bm[d], km[d])):
                        for f in range(2):
                            last = nc.tensor.transpose(self.bank[4 + 2 * d + i][:, f * P:(f + 1) * P], src[:, f, tk[d]], ident)
                        last.then_inc(bkturned.sem, 1)
                pe.wait_ge(masked.sem, masked.at(8))
                for d in range(2):
                    pe.wait_ge(picked.sem, picked.at(d + 1))
                    for hd in range(4):
                        last = nc.tensor.transpose(self.bank[d][:, hd * P:(hd + 1) * P], N[:, 4 * d + hd], ident)
                    last.then_inc(turned.sem, 1)
                for lv in range(1, 6):
                    for d in range(2):
                        i = 2 * (lv - 1) + d
                        if lv == 1:
                            pe.wait_ge(bkmoved.sem, bkmoved.at(3 + d))
                        pe.wait_ge(picked.sem, picked.at(2 * lv + d + 1))
                        pe.wait_ge(xm.sem, xm.at(2 * (i + 1)))
                        for hd in range(4):
                            last = nc.tensor.matmul(self.bank[6 + d][:, hd * P:(hd + 1) * P], N[:, 4 * d + hd], X[:, 4 * d + hd], start=True, stop=True)
                        last.then_inc(hs.sem, 1)
                    if lv == 1:
                        for i in range(8):
                            hc = slice((i % 4) * HD, (i % 4 + 1) * HD)
                            last = nc.tensor.matmul(self.bank[0][:, i * HD:(i + 1) * HD], A[:, i, 2], vtok[:, tile[i // 4], hc], start=True, stop=True)
                        last.then_inc(wsum.sem, 1)
                    for d in range(2):
                        pe.wait_ge(hm.sem, hm.at(2 * (lv - 1) + d + 1))
                        for hd in range(4):
                            c, q = slice(hd * P, (hd + 1) * P), 4 * d + hd
                            last = nc.tensor.matmul(self.bank[2 + d][:, c], H[:, q], XT[:, q], start=True, stop=True)
                            if lv < 5:
                                last = nc.tensor.matmul(self.bank[4 + d][:, c], XT[:, q], H[:, q], start=True, stop=True)
                        last.then_inc(xs.sem, 1)
        made.advance(8)
        masked.advance(8)
        bkturned.advance(4)
        bkmoved.advance(4)
        wsum.advance(1)
        picked.advance(12)
        turned.advance(2)
        hs.advance(10)
        hm.advance(10)
        xs.advance(10)
        xm.advance(22)

    def rwkv_out(self, layer, y, gate):
        nc, ar = self.nc, self.arena
        both = range(2)
        yT, sq, o = ar.take("yT", 4, T2), ar.take("sq", 4, T2), ar.take("o", 4, T2)
        turned, st, summed = self.counted("y_turned"), self.counted("headnorm_step"), self.counted("headnorm_summed")
        rooted = self.counted("rooted")
        with nc.Block() as block:
            @block.tensor
            def _(pe):
                for i in range(4):
                    d, f = i // 2, i % 2
                    for t in range(4):
                        last = nc.tensor.transpose(self.bank[i][:, t * P:(t + 1) * P], y[:, d, t, f * P:(f + 1) * P], self.tab("ident"))
                    last.then_inc(turned.sem, 1)
                for i in range(4):
                    pe.wait_ge(st.sem, st.at(i + 1))
                    nc.tensor.matmul(self.bank[4 + i], self.tab("headones"), yT[:, i], start=True, stop=True).then_inc(summed.sem, 1)
                for i in range(4):
                    pe.wait_ge(st.sem, st.at(i + 9))
                    nc.tensor.matmul(self.bank[i], self.tab("headones"), sq[:, i], start=True, stop=True).then_inc(summed.sem, 1)

            @block.vector
            def _(dve):
                for i in range(4):
                    dve.wait_ge(turned.sem, turned.at(i + 1))
                    nc.vector.tensor_copy(yT[:, i], self.bank[i]).then_inc(st.sem, 1)
                for i in range(4):
                    dve.wait_ge(summed.sem, summed.at(i + 1))
                    nc.vector.scalar_tensor_tensor(o[:, i], self.bank[4 + i], -1.0 / HD, yT[:, i], ALU.mult, ALU.add).then_inc(st.sem, 1)
                for i in range(4):
                    dve.wait_ge(st.sem, st.at(i + 5))
                    nc.vector.tensor_tensor(sq[:, i], o[:, i], o[:, i], ALU.mult).then_inc(st.sem, 1)
                for i in range(4):
                    dve.wait_ge(summed.sem, summed.at(i + 5))
                    nc.vector.tensor_scalar(yT[:, i], self.bank[i], 1.0 / HD, RW_GN_EPS, ALU.mult, ALU.add).then_inc(st.sem, 1)
                for i in range(4):
                    dve.wait_ge(st.sem, st.at(i + 13))
                    nc.vector.reciprocal(yT[:, i], yT[:, i]).then_inc(st.sem, 1)
                for i in range(4):
                    dve.wait_ge(rooted.sem, rooted.at(i + 1))
                    nc.vector.scalar_tensor_tensor(o[:, i], o[:, i], self.col(f"gn_g{layer}", i % 2), yT[:, i], ALU.mult, ALU.mult).then_inc(st.sem, 1)
                for i in range(4):
                    dve.wait_ge(st.sem, st.at(i + 21))
                    nc.vector.scalar_tensor_tensor(o[:, i], o[:, i], self.col(f"gn_b{layer}", i % 2), gate[i // 2][:, i % 2], ALU.add, ALU.mult).then_inc(st.sem, 1)
                dve.wait_ge(st.sem, st.at(28))
                for d in both:
                    nc.vector.tensor_tensor(self.hT[:, 4:6, :], self.hT[:, 4:6, :], o[:, 2 * d:2 * d + 2], ALU.add).then_inc(st.sem, 1)
                    if d == 0:
                        dve.wait_ge(st.sem, st.at(29))

            @block.scalar
            def _(act):
                for i in range(4):
                    act.wait_ge(st.sem, st.at(i + 17))
                    nc.scalar.activation(yT[:, i], yT[:, i], ACT.Sqrt).then_inc(rooted.sem, 1)
        rooted.advance(4)
        turned.advance(4)
        summed.advance(8)
        st.advance(30)
        ar.free("yT", "sq", "o")

    def conformer_open(self, cv, layer, seqs, bias, window):
        nc, ar = self.nc, self.arena
        pad = CV_LEN // 2
        ns, t0 = len(seqs), seqs[0].start
        tokens = slice(t0, T2)
        nt = T2 - t0
        h, o = ar.take("cvpad", 2, ns, SEQ + 2 * pad), ar.take("o", 2, nt)
        opened, st, taps = self.counted("cv_opened"), self.counted("cv_cleared"), self.counted("cv_tap")
        per_seq = lambda x: x.rearrange("p (s t) -> p s t", s=ns)
        with nc.Block() as block:
            @block.scalar
            def _(act):
                nc.scalar.activation(cv[:, 2:4, tokens], cv[:, 2:4, tokens], ACT.Sigmoid).then_inc(opened.sem, 1)

            @block.gpsimd
            def _(pool):
                nc.gpsimd.memset(h, 0.0).then_inc(st.sem, 1)

            @block.vector
            def _(dve):
                for hd in range(8):
                    nc.vector.tensor_tensor(bias[:, hd], bias[:, hd], window.unsqueeze(1).to_broadcast([P, 2, SEQ]), ALU.add)
                dve.wait_ge(st.sem, st.at(1))
                dve.wait_ge(opened.sem, opened.at(1))
                for f in range(2):
                    nc.vector.tensor_tensor(h[:, f, :, pad:pad + SEQ], per_seq(cv[:, f, tokens]), per_seq(cv[:, 2 + f, tokens]), ALU.mult)
        opened.advance(1)
        st.advance(1)

        def tap_step(tap):
            def fn(dve):
                if tap:
                    dve.wait_ge(taps.sem, taps.at(tap))
                for f in range(2):
                    w, src = self.col(f"dw_w{layer}_{tap}", f), h[:, f, :, tap:tap + SEQ]
                    if tap == 0:
                        last = nc.vector.tensor_scalar(per_seq(o[:, f]), src, w, self.col(f"dw_b{layer}", f), ALU.mult, ALU.add)
                    else:
                        last = nc.vector.scalar_tensor_tensor(per_seq(o[:, f]), src, w, per_seq(o[:, f]), ALU.mult, ALU.add)
                last.then_inc(taps.sem, 1)
            return fn

        def close():
            taps.advance(CV_LEN)
            self.conformer_close(o, layer, t0)
            ar.free("cvpad", "o")

        return [tap_step(tap) for tap in range(CV_LEN)], close

    def conformer_close(self, o, layer, t0):
        nc, ar = self.nc, self.arena
        nt = T2 - t0
        tmp = ar.take("tmp", 2, nt)
        st, summed, done = self.counted("cv_step"), self.counted("cv_summed"), self.counted("cv_out")
        rooted = self.counted("rooted")
        with nc.Block() as block:
            @block.scalar
            def _(act):
                act.wait_ge(st.sem, st.at(4))
                nc.scalar.activation(tmp[:, 0], tmp[:, 0], ACT.Sqrt).then_inc(rooted.sem, 1)
                act.wait_ge(done.sem, done.at(1))
                for f in range(2):
                    nc.scalar.activation(self.hT[:, 6 + f, t0:T2], o[:, f], ACT.Silu, bias=self.col(f"ln_b{layer}", f))

            @block.tensor
            def _(pe):
                for n in range(2):
                    if n == 1:
                        pe.wait_ge(st.sem, st.at(2))
                    src = o if n == 0 else tmp
                    for f in range(2):
                        last = nc.tensor.matmul(self.bank[n][:, 0:nt], self.tab("ones"), src[:, f], start=f == 0, stop=f == 1)
                    last.then_inc(summed.sem, 1)

            @block.vector
            def _(dve):
                n = 0

                def after(last):
                    nonlocal n
                    last.then_inc(st.sem, 1)
                    n += 1
                    dve.wait_ge(st.sem, st.at(n))

                dve.wait_ge(summed.sem, summed.at(1))
                for f in range(2):
                    last = nc.vector.scalar_tensor_tensor(o[:, f], self.bank[0][:, 0:nt], -1.0 / RW_WIDTH, o[:, f], ALU.mult, ALU.add)
                after(last)
                after(nc.vector.tensor_tensor(tmp, o, o, ALU.mult))
                dve.wait_ge(summed.sem, summed.at(2))
                after(nc.vector.tensor_scalar(tmp[:, 0], self.bank[1][:, 0:nt], 1.0 / RW_WIDTH, LN_EPS, ALU.mult, ALU.add))
                after(nc.vector.reciprocal(tmp[:, 0], tmp[:, 0]))
                dve.wait_ge(rooted.sem, rooted.at(1))
                for f in range(2):
                    last = nc.vector.scalar_tensor_tensor(o[:, f], o[:, f], self.col(f"ln_g{layer}", f), tmp[:, 0], ALU.mult, ALU.mult)
                last.then_inc(done.sem, 1)
        rooted.advance(1)
        summed.advance(2)
        done.advance(1)
        st.advance(4)
        ar.free("tmp")

    def block_two(self):
        nc, ins, ar = self.nc, self.ins, self.arena
        xT, hT = self.xT, self.hT
        at = lambda a: (lambda j: a[:, j])
        for layer in range(2):
            ctx = layer == 0
            seqs = [CTX, LAT] if ctx else [LAT]
            own = BOTH if ctx else LAT
            mod, gain = self.norm_gains(layer)
            self.modulated_norm(mod, gain, 0, True)

            qk = ar.take("qk", 8, T2)
            v = ar.take("v", 4, 512)
            cv = ar.take("cv", 4, T2)
            rwpad = ar.take("rwpad", 10, 2, SEQ + 2)
            with nc.Block() as block:
                @block.vector
                def _(dve):
                    for edge in (0, SEQ + 1):
                        nc.vector.memset(rwpad[:, :, :, edge:edge + 1], 0.0)

            bias = ar.take("bias", 8, 2, SEQ)
            window = ar.take("window", SEQ)
            flip = ar.take("flip", P)
            loads = [(window, self.table_src("window")), (flip, self.table_src("flip_rows"))]
            for hd in range(8):
                for row in range(4):
                    off = ((layer * 8 + hd) * 15 + 7 - row) * 127
                    loads.append((bias[(row % 2) * GRID_W:(row % 2 + 1) * GRID_W, hd, row // 2].rearrange("p (r c) -> p r c", r=4),
                                  bass.AP(self.rpb_dram, off, [[1, GRID_W], [127, 4], [1, GRID_W]])))

            rw_tables, rw_loads = self.rwkv_loads(layer)
            loads += rw_loads

            def copy_own(dst, j0, scale, n=4):
                def fn(dve, banks):
                    for j in range(n):
                        last = nc.vector.tensor_scalar(dst[:, j0 + j, own], banks[j][:, 0:own.stop - own.start], scale, None, ALU.mult)
                    return last
                return fn

            def v_evac(dve, banks):
                for t in range(4):
                    last = nc.vector.tensor_copy(v[:, t], banks[t])
                return last

            def rw_evac(j0, n):
                def fn(dve, banks):
                    for j in range(n):
                        last = nc.vector.tensor_copy(rwpad[:, j0 + j, :, 1:SEQ + 1], banks[j].rearrange("p (s t) -> p s t", s=2))
                    return last
                return fn

            F = lambda rows, act, evac, **kw: dict(kind="F", rows=rows, act=act, evac=evac, **kw)
            h_all = lambda k: hT[:, k, :]
            h_own = lambda k: hT[:, k, own]
            self.linear([F(D, h_own, {"vector": copy_own(qk, 0, HD ** -0.5)}), F(D, h_all, {"vector": self.copy_f(at(qk), 4)}),
                         dict(kind="T", rows=D, act=h_all, evac={"vector": v_evac}),
                         F(D, h_all, {"vector": rw_evac(0, 4)}), F(D, h_all, {"vector": rw_evac(4, 4)}),
                         F(D, h_all, {"vector": rw_evac(8, 2)}), F(D, h_own, {"vector": copy_own(cv, 0, 1.0)})], loads=loads)

            taps, conformer_close = self.conformer_open(cv, layer, seqs, bias, window)
            ar.free("cv")
            units = []
            for hd in range(8):
                a, ft = (hd % 2) * HD, hd // 2
                for i in range(2):
                    tq = slice(SEQ + i * P, SEQ + (i + 1) * P)
                    units.append(dict(q=[qk[a:a + HD, ft, tq]], k=[qk[a:a + HD, 4 + ft, :]],
                                      v=[v[:, t, hd * HD:(hd + 1) * HD] for t in range(4)],
                                      out=[hT[a:a + HD, ft, tq]], out_part=a, bias=bias[:, hd, i], count=None))
            if ctx:
                for hd in range(8):
                    a, ft = (hd % 2) * HD, hd // 2
                    for i in range(2):
                        tq = slice(i * P, (i + 1) * P)
                        units.append(dict(q=[qk[a:a + HD, ft, tq]], k=[qk[a:a + HD, 4 + ft, CTX]],
                                          v=[v[:, t, hd * HD:(hd + 1) * HD] for t in range(2)],
                                          out=[hT[a:a + HD, ft, tq]], out_part=a, bias=None, count=None))
            self.attention(units, flip, beside=taps)
            ar.free("qk", "v", "bias", "window", "flip")
            conformer_close()
            self.rwkv(rwpad, layer, rw_tables)

            def gates(n):
                out = [(LAT, lambda t: mod[:, (3 * n + 2) * DT + t, 0:1])]
                if ctx:
                    out.insert(0, (CTX, lambda t: mod[:, (3 * n + 2) * DT + t, 1:2]))
                return out

            self.linear([F(D, h_own, {"vector": self.residual(g, own, gates(0))}) for g in range(2)])
            self.modulated_norm(mod, gain, 1, ctx)
            if layer == 0:
                hidden = ar.take("hidden", D_FF // P, T2)
                groups = []
                for j0 in range(0, D_FF // P, 4):
                    n = min(4, D_FF // P - j0)

                    def silu_evac(act, banks, j0=j0, n=n):
                        for j in range(n):
                            last = nc.scalar.activation(hidden[:, j0 + j], banks[j], ACT.Silu)
                        return last

                    def up_evac(dve, banks, j0=j0, n=n):
                        for j in range(n):
                            last = nc.vector.tensor_tensor(hidden[:, j0 + j], banks[j], hidden[:, j0 + j], ALU.mult)
                        return last

                    groups.append(F(D, h_all, {"scalar": silu_evac}))
                    groups.append(F(D, h_all, {"vector": up_evac}, vector_after_scalar=True))
                self.linear(groups, side=SideProduct(self, 1, 6, 6))
                self.linear([F(D_FF, at(hidden), {"vector": self.residual(g, BOTH, gates(1))}) for g in range(2)])
                ar.free("hidden")
            else:
                self.experts(gates(1)[0][1])

        self.rmsnorm(lambda k: xT[:, k, LAT], DT, SEQ, [(slice(0, SEQ), lambda k: xT[:, k, LAT], lambda k: self.col("final_g", k), None)])

    def experts(self, gate_column):
        nc, ar, ins = self.nc, self.arena, self.ins
        hT, xT = self.hT, self.xT
        E, I = N_EXPERTS, MAX_ITEMS
        ident = self.tab("ident")
        router = ar.take("router", DT, E)
        gt = ar.take("gt", 2, 88)
        idx = ar.take("idx", 2, 8).bitcast(U32)
        sh = ar.take("shares", 4, E)
        oh = ar.take("oh", 3, I, E)
        it = ar.take("it", 8, I)
        number = ar.take("number", 16).bitcast(mybir.dt.int32)
        earlier, iota, items = ar.take("earlier", P), ar.take("iota", P), ar.take("items", I, E)
        xtok = ar.take("xtok", 2, D)
        pick = ar.take("pick", 2, I, P)
        spread = ar.take("spread", I, SEQ)
        gated = ar.take("gated", 4, P)
        self.load([(router, ins["moe_router_2"][0].rearrange("(k p) e -> p k e", p=P)),
                   (earlier, self.table_src("earlier")), (iota, self.table_src("iota128")),
                   (items.rearrange("p i e -> p (i e)"), self.table_src("items"))])
        logits, st, ed = self.counted("logits_ready"), self.counted("route_step"), self.counted("route_exp")
        placed, rows, rowsm = self.counted("places_summed"), self.counted("h_turned"), self.counted("h_rows_ready")
        gready, gturned, gmoved = self.counted("gated_ready"), self.counted("gated_turned"), self.counted("gated_moved")
        LG, TOP, IX, E1, G0, G1, DL, DN, M0, M1, MS, GS, PM = 0, 8, 16, 24, 25, 26, 27, 28, 32, 40, 48, 56, 64
        with nc.Block() as block:
            @block.tensor
            def _(pe):
                for t in range(2):
                    for k in range(DT):
                        last = nc.tensor.matmul(self.bank[t][:, 0:E], hT[:, k, SEQ + t * P:SEQ + (t + 1) * P], router[:, k, :], start=k == 0, stop=k == DT - 1)
                    last.then_inc(logits.sem, 1)
                for t in range(2):
                    for k in range(DT):
                        last = nc.tensor.transpose(self.bank[4 + 2 * t + k // 4][:, (k % 4) * P:(k % 4 + 1) * P], hT[:, k, SEQ + t * P:SEQ + (t + 1) * P], ident)
                last.then_inc(rows.sem, 1)
                pe.wait_ge(st.sem, st.at(8))
                nc.tensor.matmul(self.bank[2][:, 0:E], earlier, gt[:, 0, MS:MS + E], start=True, stop=True)
                nc.tensor.matmul(self.bank[2][:, 8:8 + E], earlier, gt[:, 1, MS:MS + E], start=True, stop=False)
                nc.tensor.matmul(self.bank[2][:, 8:8 + E], self.tab("ones"), gt[:, 0, MS:MS + E], start=False, stop=True)
                nc.tensor.matmul(self.bank[2][:, 16:16 + E], self.tab("ones"), gt[:, 0, MS:MS + E], start=True, stop=False)
                nc.tensor.matmul(self.bank[2][:, 16:16 + E], self.tab("ones"), gt[:, 1, MS:MS + E], start=False, stop=True).then_inc(placed.sem, 1)
                pe.wait_ge(rowsm.sem, rowsm.at(1))
                for i in range(2 * I):
                    pe.wait_ge(gready.sem, gready.at(i + 1))
                    if i >= 4:
                        pe.wait_ge(gmoved.sem, gmoved.at(i - 3))
                    nc.tensor.transpose(self.bank[4 + i % 4][:, 0:P], gated[:, i % 4], ident).then_inc(gturned.sem, 1)

            @block.scalar
            def _(act):
                act.wait_ge(rows.sem, rows.at(1))
                for t in range(2):
                    for b in range(2):
                        last = nc.scalar.activation(xtok[:, t, 512 * b:512 * b + 512], self.bank[4 + 2 * t + b], ACT.Copy)
                last.then_inc(rowsm.sem, 1)
                act.wait_ge(st.sem, st.at(4))
                for t in range(2):
                    last = nc.scalar.activation(gt[:, t, E1:E1 + 1], gt[:, t, DL:DL + 1], ACT.Exp)
                last.then_inc(ed.sem, 1)
                for i in range(2 * I):
                    act.wait_ge(gturned.sem, gturned.at(i + 1))
                    nc.scalar.activation(spread[:, i // 2, (i % 2) * P:(i % 2 + 1) * P], self.bank[4 + i % 4][:, 0:P], ACT.Copy).then_inc(gmoved.sem, 1)

            @block.vector
            def _(dve):
                n = 0

                def after(last):
                    nonlocal n
                    last.then_inc(st.sem, 1)
                    n += 1
                    dve.wait_ge(st.sem, st.at(n))

                both = (0, 1)
                wide = lambda x: x.unsqueeze(1).to_broadcast([P, I, E])
                dve.wait_ge(logits.sem, logits.at(2))
                for t in both:
                    last = nc.vector.tensor_copy(gt[:, t, LG:LG + E], self.bank[t][:, 0:E])
                after(last)
                for t in both:
                    last = nc.vector.max(gt[:, t, TOP:TOP + 8], gt[:, t, LG:LG + E])
                after(last)
                for t in both:
                    last = nc.vector.max_index(idx[:, t], gt[:, t, TOP:TOP + 8], gt[:, t, LG:LG + E])
                after(last)
                for t in both:
                    nc.vector.tensor_copy(gt[:, t, IX:IX + 8], idx[:, t])
                    last = nc.vector.tensor_tensor(gt[:, t, DL:DL + 1], gt[:, t, TOP + 1:TOP + 2], gt[:, t, TOP:TOP + 1], ALU.subtract)
                after(last)
                dve.wait_ge(ed.sem, ed.at(1))
                for t in both:
                    last = nc.vector.tensor_scalar(gt[:, t, DN:DN + 1], gt[:, t, E1:E1 + 1], 1.0, None, ALU.add)
                    for i, m in ((0, M0), (1, M1)):
                        last = nc.vector.tensor_scalar(gt[:, t, m:m + E], self.tab("iota8"), gt[:, t, IX + i:IX + i + 1], None, ALU.is_equal)
                after(last)
                for t in both:
                    last = nc.vector.reciprocal(gt[:, t, G0:G0 + 1], gt[:, t, DN:DN + 1])
                after(last)
                for t in both:
                    last = nc.vector.tensor_tensor(gt[:, t, G1:G1 + 1], gt[:, t, E1:E1 + 1], gt[:, t, G0:G0 + 1], ALU.mult)
                after(last)
                for t in both:
                    last = nc.vector.tensor_tensor(gt[:, t, MS:MS + E], gt[:, t, M0:M0 + E], gt[:, t, M1:M1 + E], ALU.add)
                after(last)
                for t in both:
                    last = nc.vector.tensor_scalar(gt[:, t, M0:M0 + E], gt[:, t, M0:M0 + E], gt[:, t, G0:G0 + 1], None, ALU.mult)
                after(last)
                for t in both:
                    last = nc.vector.scalar_tensor_tensor(gt[:, t, GS:GS + E], gt[:, t, M1:M1 + E], gt[:, t, G1:G1 + 1], gt[:, t, M0:M0 + E], ALU.mult, ALU.add)
                dve.wait_ge(placed.sem, placed.at(1))
                for t in both:
                    last = nc.vector.scalar_tensor_tensor(gt[:, t, PM:PM + E], self.bank[2][:, 8 * t:8 * t + E], 1000.0, gt[:, t, MS:MS + E], ALU.add, ALU.mult)
                    last = nc.vector.tensor_scalar(sh[:, t], self.bank[2][:, 16:16 + E], 1.0 if t == 0 else P + 1.0, None, ALU.is_ge)
                after(last)
                for t in both:
                    nc.vector.tensor_scalar(gt[:, t, PM:PM + E], gt[:, t, PM:PM + E], -1000.0, None, ALU.add)
                after(nc.vector.tensor_tensor(sh[:, 1], sh[:, 0], sh[:, 1], ALU.add))
                after(nc.vector.tensor_tensor_scan(sh[:, 2], self.tab("ones")[:, 0:E], sh[:, 1], 0.0, ALU.mult, ALU.add))
                after(nc.vector.tensor_tensor(sh[:, 3], sh[:, 2], sh[:, 1], ALU.subtract))
                nc.vector.tensor_tensor(oh[:, 0], items, wide(sh[:, 3]), ALU.is_ge)
                after(nc.vector.tensor_tensor(oh[:, 1], items, wide(sh[:, 2]), ALU.is_lt))
                nc.vector.tensor_tensor(oh[:, 2], items, wide(sh[:, 3]), ALU.subtract)
                after(nc.vector.tensor_tensor(oh[:, 0], oh[:, 0], oh[:, 1], ALU.mult))
                nc.vector.tensor_tensor(oh[:, 2], oh[:, 2], oh[:, 0], ALU.mult)
                after(nc.vector.tensor_tensor(oh[:, 1], wide(self.tab("iota8")), oh[:, 0], ALU.mult))
                nc.vector.tensor_reduce(it[:, 0], oh[:, 1], AX_X, ALU.add)
                after(nc.vector.tensor_reduce(it[:, 1], oh[:, 2], AX_X, ALU.add))
                nc.vector.tensor_copy(number[:, 0:I], it[:, 0])
                nc.vector.tensor_copy(number[:, I:I + 1], sh[:, 2, E - 1:E])
                after(nc.vector.tensor_scalar(it[:, 1], it[:, 1], float(P), None, ALU.mult))
                for src, col in ((PM, 2), (GS, 4)):
                    for t in both:
                        after(nc.vector.tensor_tensor(oh[:, 1], wide(gt[:, t, src:src + E]), oh[:, 0], ALU.mult))
                        after(nc.vector.tensor_reduce(it[:, col + t], oh[:, 1], AX_X, ALU.add))
                for t in both:
                    last = nc.vector.tensor_tensor(it[:, 2 + t], it[:, 2 + t], it[:, 1], ALU.subtract)
                after(last)
                for i in range(2 * I):
                    item, t = i // 2, i % 2
                    slot, gate = it[:, 2 + t, item:item + 1], it[:, 4 + t, item:item + 1]
                    if i >= 4:
                        dve.wait_ge(gturned.sem, gturned.at(i - 3))
                    nc.vector.tensor_scalar(gated[:, i % 4], iota, slot, gate, ALU.is_equal, ALU.mult).then_inc(gready.sem, 1)
                    nc.vector.tensor_scalar(pick[:, t, item], iota, slot, None, ALU.is_equal)
                st.n = n
        for q, k in ((logits, 2), (st, st.n), (ed, 1), (placed, 1), (rows, 1), (rowsm, 1), (gready, 2 * I), (gturned, 2 * I), (gmoved, 2 * I)):
            q.advance(k)
        ar.free("router", "gt", "idx", "shares", "oh", "it", "earlier", "iota", "items", "gated")

        acc = ar.take("acc", DT, SEQ)
        xg = ar.take("xg", DT, P)
        hk = ar.take("hk", 2, GROUP)
        hid = ar.take("hid", D_FFE // P, P)
        y = ar.take("y", D)
        n_col, n_in, n_down = D_FFE // GROUP, D // (TILE_K * P), D_FFE // (TILE_K * P)
        per = 2 * n_col * n_in + 2 * n_down
        assert per % WEIGHT_SLOTS == 0
        turns = per // WEIGHT_SLOTS
        t0 = self.taken
        used = self.tile_used
        wg, wu, wd = (ins[f"moe_w_{n}_2"][0] for n in ("gate", "up", "down"))

        def source(j, e):
            if j < 2 * n_col * n_in:
                g, half = divmod(j, n_in)
                w = wg if g % 2 == 0 else wu
                c, r = (g // 2) * GROUP, half * TILE_K * P
            else:
                g, half = divmod(j - 2 * n_col * n_in, n_down)
                w, c, r = wd, g * GROUP, half * TILE_K * P
            rows = w.rearrange("e r c -> (e r) c")
            return rows[bass.ds(e * w.shape[1] + r, TILE_K * P), c:c + GROUP].rearrange("(k p) n -> p k n", p=P)

        gathered, xready = self.counted("tokens_gathered"), self.counted("tokens_ready")
        silu, mult, turned, moved = (self.counted(n) for n in ("gate_silu", "gate_times_up", "hidden_turned", "hidden_ready"))
        ymoved, scattered, added = self.counted("outputs_moved"), self.counted("outputs_scattered"), self.counted("outputs_added")
        with nc.Block() as block:
            @block.sync
            def _(sync):
                def load_tile(j, x, e):
                    src = source(j, e)
                    sync.wait_ge(used.sem, x * per + (t0 + j - WEIGHT_SLOTS + 1))
                    sync.dma_start(self.ring[:, (t0 + j) % WEIGHT_SLOTS], src).then_inc(self.slot_full[(t0 + j) % WEIGHT_SLOTS].sem, 16)

                def expert_of(x):
                    return sync.value_load(number[0:1, bass.ds(x, 1)], min_val=0, max_val=E - 1)

                n_items = sync.value_load(number[0:1, I:I + 1], min_val=2, max_val=I)
                first = expert_of(0)
                for j in range(WEIGHT_SLOTS):
                    load_tile(j, 0, first)
                with sync.Fori(1, n_items) as x:
                    now, then = expert_of(x - 1), expert_of(x)
                    for j in range(WEIGHT_SLOTS, per):
                        load_tile(j, x - 1, now)
                    for j in range(WEIGHT_SLOTS):
                        load_tile(j, x, then)
                final = expert_of(n_items - 1)
                for j in range(WEIGHT_SLOTS, per):
                    load_tile(j, n_items - 1, final)

            @block.tensor
            def _(pe):
                n_items = pe.value_load(number[0:1, I:I + 1], min_val=2, max_val=I)
                pe.wait_ge(added.sem, added.at(2))
                with pe.Fori(0, n_items) as x:
                    j = 0

                    def next_tile():
                        nonlocal j
                        pe.wait_ge(self.slot_full[(t0 + j) % WEIGHT_SLOTS].sem, x * (16 * turns) + 16 * ((t0 + j) // WEIGHT_SLOTS + 1))
                        j += 1
                        return self.ring[:, (t0 + j - 1) % WEIGHT_SLOTS]

                    def turn_hidden(q):
                        pe.wait_ge(mult.sem, x * n_col + mult.at(q + 1))
                        if q >= 2:
                            pe.wait_ge(moved.sem, x * n_col + moved.at(q - 1))
                        else:
                            pe.wait_ge(added.sem, x * 2 + added.at(2))
                        for c in range(4):
                            last = nc.tensor.transpose(self.bank[4 + q % 2][:, c * P:(c + 1) * P], hk[:, q % 2, c * P:(c + 1) * P], ident)
                        last.then_inc(turned.sem, 1)

                    for f in range(DT):
                        for t in range(2):
                            last = nc.tensor.matmul(self.bank[f // 4][:, (f % 4) * P:(f % 4 + 1) * P], xtok[:, t, f * P:(f + 1) * P],
                                                    pick[:, t, bass.ds(x, 1), :].rearrange("p o s -> p (o s)"), start=t == 0, stop=t == 1)
                    last.then_inc(gathered.sem, 1)
                    for q in range(n_col):
                        if q == 0:
                            pe.wait_ge(xready.sem, x + xready.at(1))
                        elif q == 1:
                            pe.wait_ge(ymoved.sem, x * 2 + ymoved.at(2))
                        else:
                            pe.wait_ge(mult.sem, x * n_col + mult.at(q - 1))
                        for b in (2 * (q % 2), 2 * (q % 2) + 1):
                            for i in range(n_in):
                                w = next_tile()
                                for k in range(TILE_K):
                                    kk = i * TILE_K + k
                                    last = nc.tensor.matmul(self.bank[b], xg[:, kk], w[:, k], start=kk == 0, stop=kk == DT - 1)
                                last.then_inc(used.sem, 1)
                        if q >= 1:
                            turn_hidden(q - 1)
                    for b in range(2):
                        for i in range(n_down):
                            w = next_tile()
                            if b == 0:
                                pe.wait_ge(moved.sem, x * n_col + moved.at(i + 1))
                            for k in range(TILE_K):
                                kk = i * TILE_K + k
                                last = nc.tensor.matmul(self.bank[2 + b], hid[:, kk], w[:, k], start=kk == 0, stop=kk == n_down * TILE_K - 1)
                            last.then_inc(used.sem, 1)
                            if b == 0 and i == 0:
                                turn_hidden(n_col - 1)
                    for b in range(2):
                        pe.wait_ge(ymoved.sem, x * 2 + ymoved.at(2 + b + 1))
                        for f in range(4 * b, 4 * b + 4):
                            last = nc.tensor.matmul(self.bank[4 + f // 2][:, (f % 2) * SEQ:(f % 2 + 1) * SEQ], y[:, f * P:(f + 1) * P],
                                                    spread[:, bass.ds(x, 1), :].rearrange("p o t -> p (o t)"), start=True, stop=True)
                        last.then_inc(scattered.sem, 1)

            @block.scalar
            def _(act):
                n_items = act.value_load(number[0:1, I:I + 1], min_val=2, max_val=I)
                nc.scalar.activation(y[:, 0:1], self.tab("ones")[:, 0:1], ACT.Copy).then_inc(ymoved.sem, 2)
                with act.Fori(0, n_items) as x:
                    def move_hidden(q):
                        act.wait_ge(turned.sem, x * n_col + turned.at(q + 1))
                        nc.scalar.activation(hid[:, 4 * q:4 * q + 4].rearrange("p k s -> p (k s)"), self.bank[4 + q % 2], ACT.Copy).then_inc(moved.sem, 1)

                    act.wait_ge(gathered.sem, x + gathered.at(1))
                    for b in range(2):
                        last = nc.scalar.activation(xg[:, 4 * b:4 * b + 4].rearrange("p k s -> p (k s)"), self.bank[b], ACT.Copy)
                    last.then_inc(xready.sem, 1)
                    for q in range(n_col):
                        act.wait_ge(used.sem, x * per + used.at(2 * q * n_in + n_in))
                        nc.scalar.activation(hk[:, q % 2], self.bank[2 * (q % 2)], ACT.Silu).then_inc(silu.sem, 1)
                        if q >= 1:
                            move_hidden(q - 1)
                    move_hidden(n_col - 1)
                    for b in range(2):
                        act.wait_ge(used.sem, x * per + used.at(2 * n_col * n_in + (b + 1) * n_down))
                        nc.scalar.activation(y[:, 512 * b:512 * b + 512], self.bank[2 + b], ACT.Copy).then_inc(ymoved.sem, 1)

            @block.vector
            def _(dve):
                n_items = dve.value_load(number[0:1, I:I + 1], min_val=2, max_val=I)
                nc.vector.memset(acc, 0.0).then_inc(added.sem, 2)
                dve.wait_ge(added.sem, added.at(2))
                with dve.Fori(0, n_items) as x:
                    for q in range(n_col):
                        dve.wait_ge(used.sem, x * per + used.at(2 * (q + 1) * n_in))
                        dve.wait_ge(silu.sem, x * n_col + silu.at(q + 1))
                        nc.vector.tensor_tensor(hk[:, q % 2], self.bank[2 * (q % 2) + 1], hk[:, q % 2], ALU.mult).then_inc(mult.sem, 1)
                    for b in range(2):
                        dve.wait_ge(scattered.sem, x * 2 + scattered.at(b + 1))
                        for i in range(2 * b, 2 * b + 2):
                            a = acc[:, 2 * i:2 * i + 2].rearrange("p k t -> p (k t)")
                            last = nc.vector.tensor_tensor(a, self.bank[4 + i], a, ALU.add)
                        last.then_inc(added.sem, 1)
                dve.wait_ge(added.sem, n_items * 2 + added.at(2))
                for t in range(DT):
                    nc.vector.scalar_tensor_tensor(xT[:, t, LAT], acc[:, t], gate_column(t), xT[:, t, LAT], ALU.mult, ALU.add)
        ar.free("number", "xtok", "pick", "spread", "acc", "xg", "hk", "hid", "y")

    def store(self):
        nc = self.nc
        rows = self.arena.take("rows", 2, D)
        turned, moved, stored = self.counted("rows_turned"), self.counted("turned_moved"), self.counted("output_stored")
        with nc.Block() as block:
            @block.tensor
            def _(pe):
                for t in range(2):
                    for k in range(DT):
                        last = nc.tensor.transpose(self.bank[2 * t + k // 4][:, (k % 4) * P:(k % 4 + 1) * P], self.xT[:, k, SEQ + t * P:SEQ + (t + 1) * P], self.tab("ident"))
                    last.then_inc(turned.sem, 1)

            @block.vector
            def _(dve):
                for t in range(2):
                    dve.wait_ge(turned.sem, turned.at(t + 1))
                    for b in range(2):
                        last = nc.vector.tensor_copy(rows[:, t, 512 * b:512 * b + 512], self.bank[2 * t + b])
                    last.then_inc(moved.sem, 1)

            @block.sync
            def _(sync):
                for t in range(2):
                    sync.wait_ge(moved.sem, moved.at(t + 1))
                    sync.dma_start(self.out[0, t * P:(t + 1) * P, :], rows[:, t]).then_inc(stored.sem, 16)
                sync.wait_ge(stored.sem, stored.at(32))


def vector_rows(ins):
    rows = lambda ap: ap.rearrange("(r p) -> r p", p=P)
    out = [("g_mix", rows(ins["g_mix"][0])), ("g_out_dil", rows(ins["g_out_dil"][0])), ("g_out_moba", rows(ins["g_out_moba"][0])),
           ("g_cross", rows(ins["g_cross"][0])), ("g_mem", rows(ins["g_mem"][0])), ("g_ffn", rows(ins["g_ffn"][0])),
           ("g_final", rows(ins["g_final"])), ("conv_b", rows(ins["conv_b"][0]))]
    out += [(f"conv_w{t}", rows(ins["conv_w"][0, t])) for t in range(3)]
    out += [("c", rows(ins["c_2"][0])), ("c_ctx", rows(ins["c_ctx_2"]))]
    for l in range(2):
        out += [(f"norm1_g{l}", rows(ins["norm1_g_2"][l])), (f"norm2_g{l}", rows(ins["norm2_g_2"][l])), (f"mod_b{l}", rows(ins["mod_b_2"][l])),
                (f"mu_prev{l}", rows(ins["rw_mu_prev_2"][l])), (f"mu_next{l}", rows(ins["rw_mu_next_2"][l])),
                (f"w0{l}", ins["rw_w0_2"][l].rearrange("d (r p) -> (d r) p", p=P)), (f"a0{l}", ins["rw_a0_2"][l].rearrange("d (r p) -> (d r) p", p=P)),
                (f"k_k{l}", rows(ins["rw_k_k_2"][l])), (f"k_a{l}", rows(ins["rw_k_a_2"][l])),
                (f"r_k{l}", ins["rw_r_k_2"][l].rearrange("(a b) k -> a (b k)", b=2)),
                (f"gn_g{l}", rows(ins["rw_gn_g_2"][l])), (f"gn_b{l}", rows(ins["rw_gn_b_2"][l])),
                (f"dw_w{l}", ins["cv_dw_w_2"][l].rearrange("t (r p) -> (t r) p", p=P)),
                (f"dw_b{l}", rows(ins["cv_dw_b_2"][l])), (f"ln_g{l}", rows(ins["cv_ln_g_2"][l])), (f"ln_b{l}", rows(ins["cv_ln_b_2"][l]))]
    return out + [("final_g", rows(ins["final_g_2"]))]


def build(nc, ins, out):
    ctx = ExitStack()
    with ctx:
        pr = Program(nc, ins, out, ctx)
        pr.plan(ins["w_in"][0], 0, D, 0, 6 * 512)
        pr.plan(ins["w_out"][0], 0, D, 0, D)
        pr.plan(ins["w_kv_mem"][0], 0, D, D, D)
        pr.plan(ins["w_q_mem"][0], 0, D, 0, D)
        pr.plan(ins["w_kv_mem"][0], 0, D, 0, D)
        pr.plan(ins["w_o_mem"][0], 0, D, 0, D)
        for c in range(0, D_FF, GROUP):
            for w in ("w_gate", "w_up"):
                pr.plan(ins[w][0], 0, D, c, min(GROUP, D_FF - c))
        pr.plan(ins["w_down"][0], 0, D_FF, 0, D)
        for layer in range(2):
            w = ins["w_in_2"][layer]
            for c, n in ((0, 512), (512, 512), (1024, 512), (1536, 1280), (2816, 512)):
                pr.plan(w, 0, D, c, n)
            pr.plan(ins["w_out_2"][layer], 0, D, 0, D)
            if layer == 0:
                for c in range(0, D_FF, GROUP):
                    for n in ("ffn_w_gate_2", "ffn_w_up_2"):
                        pr.plan(ins[n][0], 0, D, c, min(GROUP, D_FF - c))
                pr.plan(ins["ffn_w_down_2"][0], 0, D_FF, 0, D)
        pr.load_vectors(vector_rows(ins))
        for l in range(2):
            for tap in range(CV_LEN):
                pr.vec[f"dw_w{l}_{tap}"] = pr.vec[f"dw_w{l}"] + 2 * tap
        pr.bias_lines()
        pr.conditioning()
        pr.block_one()
        pr.block_two()
        pr.store()


_NAMES = ["x", "mem", "w_in", "g_mix", "g_out_dil", "g_out_moba", "w_out", "rel_bias", "g_cross", "g_mem", "w_q_mem",
          "w_kv_mem", "w_o_mem", "g_ffn", "w_gate", "w_up", "conv_w", "conv_b", "w_down", "g_final", "c_2", "ctx_2",
          "c_ctx_2", "norm1_g_2", "norm2_g_2", "mod_w_2", "mod_b_2", "w_in_2", "w_out_2", "na_rpb_2", "rw_mu_prev_2",
          "rw_mu_next_2", "rw_w0_2", "rw_w2_2", "rw_a0_2", "rw_a2_2", "rw_g2_2", "rw_k_k_2", "rw_k_a_2", "rw_r_k_2",
          "rw_gn_g_2", "rw_gn_b_2", "cv_dw_w_2", "cv_dw_b_2", "cv_ln_g_2", "cv_ln_b_2", "ffn_w_gate_2", "ffn_w_up_2",
          "ffn_w_down_2", "moe_router_2", "moe_w_gate_2", "moe_w_up_2", "moe_w_down_2", "final_g_2"]


def kernel(**inputs):
    import concourse.bacc as bacc
    from concourse.bass_utils import run_bass_kernel_spmd

    nc = bacc.Bacc("TRN2", target_bir_lowering=False, num_devices=1)
    arrays, ins = {}, {}
    for name in _NAMES:
        a = np.ascontiguousarray(inputs[name])
        arrays[f"in_{name}"] = a
        ins[name] = nc.dram_tensor(f"in_{name}", a.shape, mybir.dt.from_np(a.dtype), kind="ExternalInput").ap()
    tables = np.concatenate(list(_TABLES.values()), axis=1)
    arrays["shape_tables"] = tables
    ins["tables"] = nc.dram_tensor("shape_tables", tables.shape, F32, kind="ExternalInput").ap()
    out = nc.dram_tensor("out", (1, SEQ, D), F32, kind="ExternalOutput").ap()
    build(nc, ins, out)
    return run_bass_kernel_spmd(nc, [arrays], core_ids=[0]).results[0]["out"]
```
